# Optimizing a Trainium2 kernel written in Bass

```python
import jax, jax.numpy as jnp
from jax import lax
import numpy as np
import math

D_MODEL = 1024
BATCH = 1
SEQ = 256
DEPTH = 1

CHUNK = 64
Q_BLOCK = 2 * CHUNK
HEAD_DIM = 64
CONV_CH = 256
CONV_W = 3
SB_HEADS = 6
FOX_HEADS = 6
SB_DIM = SB_HEADS * HEAD_DIM
FOX_DIM = FOX_HEADS * HEAD_DIM
D_MIX = CONV_CH + SB_DIM + FOX_DIM
D_IN = 3 * CONV_CH + 3 * SB_DIM + 3 * FOX_DIM + FOX_HEADS
N_MOD = 6
N_EXPERTS = 32
TOP_K = 4
D_EXPERT = D_MODEL
SWIGLU_ALPHA = 1.702
SWIGLU_LIMIT = 7.0
EPS = 1e-6


def _rms(x):
    xf = x.astype(jnp.float32)
    return (xf * lax.rsqrt(jnp.mean(xf * xf, axis=-1, keepdims=True) + EPS)).astype(x.dtype)

def rms_norm(x, g):
    return _rms(x) * g

def short_conv_mixer(gb, gc, u, conv_w):
    v = gc * u
    y = lax.conv_general_dilated(v, conv_w[:, None, :], window_strides=(1,), padding=[(CONV_W - 1, 0)],
                                 dimension_numbers=('NWC', 'WIO', 'NWC'), feature_group_count=CONV_CH)
    return gb * y

def _query_blocks(t):
    b, h, s = t.shape[:3]
    t = t.reshape((b, h, s // Q_BLOCK, Q_BLOCK) + t.shape[3:])
    return jnp.moveaxis(t, 2, 0)

def _merge_blocks(o):
    nb, b, h, qb, d = o.shape
    return o.transpose(1, 0, 3, 2, 4).reshape(b, nb * qb, h * d)

def stick_breaking_attention(q, k, v):
    s = q.shape[2]
    scale = q.shape[-1] ** -0.5
    kpos = jnp.arange(s)

    def block(args):
        qb, start = args
        z = jnp.einsum('bhqd,bhkd->bhqk', qb, k, preferred_element_type=jnp.float32) * scale
        qpos = start + jnp.arange(Q_BLOCK)
        strict = kpos[None, :] < qpos[:, None]
        log_beta = jax.nn.log_sigmoid(z)
        log_1mb = jnp.where(strict, jax.nn.log_sigmoid(-z), 0.0)
        rest = lax.cumsum(log_1mb, axis=3, reverse=True) - log_1mb
        w = jnp.where(strict, jnp.exp(log_beta + rest), 0.0)
        return jnp.einsum('bhqk,bhkd->bhqd', w.astype(v.dtype), v)

    starts = jnp.arange(s // Q_BLOCK, dtype=jnp.int32) * Q_BLOCK
    return _merge_blocks(lax.map(block, (_query_blocks(q), starts)))

def forgetting_attention(q, k, v, log_f):
    s = q.shape[2]
    scale = q.shape[-1] ** -0.5
    kpos = jnp.arange(s)
    cum = lax.cumsum(log_f, axis=2)

    def block(args):
        qb, fq, start = args
        logits = jnp.einsum('bhqd,bhkd->bhqk', qb, k, preferred_element_type=jnp.float32) * scale
        logits = logits + (fq[..., None] - cum[:, :, None, :])
        qpos = start + jnp.arange(Q_BLOCK)
        causal = kpos[None, :] <= qpos[:, None]
        p = jax.nn.softmax(jnp.where(causal, logits, -jnp.inf), axis=-1)
        return jnp.einsum('bhqk,bhkd->bhqd', p.astype(v.dtype), v)

    starts = jnp.arange(s // Q_BLOCK, dtype=jnp.int32) * Q_BLOCK
    return _merge_blocks(lax.map(block, (_query_blocks(q), _query_blocks(cum), starts)))

def moe_ffn(h, router_w, router_b, w_mlp1, b_mlp1, w_mlp2, b_mlp2):
    b, s, d = h.shape
    xt = h.reshape(b * s, d)
    logits = (xt @ router_w + router_b).astype(jnp.float32)
    top_vals, top_idx = lax.top_k(logits, TOP_K)
    top_w = jax.nn.softmax(top_vals, axis=-1)
    combine = jnp.einsum('tk,tke->et', top_w, jax.nn.one_hot(top_idx, N_EXPERTS, dtype=jnp.float32))

    def expert_step(acc, params):
        w1, b1, w2, b2, gate_e = params
        u = xt @ w1 + b1
        glu = jnp.minimum(u[:, ::2], SWIGLU_LIMIT)
        lin = jnp.clip(u[:, 1::2], -SWIGLU_LIMIT, SWIGLU_LIMIT)
        a = glu * jax.nn.sigmoid(SWIGLU_ALPHA * glu) * (lin + 1)
        out = a @ w2 + b2
        return acc + gate_e[:, None] * out.astype(jnp.float32), None

    acc0 = jnp.zeros((b * s, d), jnp.float32)
    acc, _ = lax.scan(expert_step, acc0, (w_mlp1, b_mlp1, w_mlp2, b_mlp2, combine))
    return acc.astype(h.dtype).reshape(b, s, d)

def hybrid_layer(x, c, norm1_g, w_ada, b_ada, w_in, conv_w, sb_q_g, sb_k_g, fox_q_g, fox_k_g, fox_f_b,
                 out_norm_g, w_out, norm2_g, router_w, router_b, w_mlp1, b_mlp1, w_mlp2, b_mlp2):
    b, s, d = x.shape
    mod = (jax.nn.silu(c) @ w_ada + b_ada).reshape(b, N_MOD, 1, d)
    shift1, scale1, gate1, shift2, scale2, gate2 = (mod[:, i] for i in range(N_MOD))

    h = rms_norm(x, norm1_g) * (1 + scale1) + shift1
    proj = h @ w_in
    cuts = [int(v) for v in np.cumsum([CONV_CH] * 3 + [SB_DIM] * 3 + [FOX_DIM] * 3)]
    cb, cc, cu, sq, sk, sv, fq, fk, fv, flog = jnp.split(proj, cuts, axis=-1)

    def heads(t, n):
        return t.reshape(b, s, n, HEAD_DIM).transpose(0, 2, 1, 3)

    y_conv = short_conv_mixer(cb, cc, cu, conv_w)
    y_sb = stick_breaking_attention(rms_norm(heads(sq, SB_HEADS), sb_q_g),
                                    rms_norm(heads(sk, SB_HEADS), sb_k_g), heads(sv, SB_HEADS))
    log_f = jax.nn.log_sigmoid((flog + fox_f_b).astype(jnp.float32)).transpose(0, 2, 1)
    y_fox = forgetting_attention(rms_norm(heads(fq, FOX_HEADS), fox_q_g),
                                 rms_norm(heads(fk, FOX_HEADS), fox_k_g), heads(fv, FOX_HEADS), log_f)
    y = jnp.concatenate([y_conv, y_sb, y_fox], axis=-1)
    y = _rms(y.reshape(b, s, D_MIX // HEAD_DIM, HEAD_DIM)).reshape(b, s, D_MIX) * out_norm_g
    x = x + gate1 * (y @ w_out)

    h2 = rms_norm(x, norm2_g) * (1 + scale2) + shift2
    return x + gate2 * moe_ffn(h2, router_w, router_b, w_mlp1, b_mlp1, w_mlp2, b_mlp2)

def first_inputs(seed: int = 0) -> dict:
    key = jax.random.key(seed)
    ks = jax.random.split(key, 24)
    nrm = jax.random.normal
    f32 = jnp.float32
    L, D, E = DEPTH, D_MODEL, N_EXPERTS
    return {
        'x': nrm(ks[0], (BATCH, SEQ, D), f32),
        'c': nrm(ks[1], (BATCH, D), f32),
        'norm1_g': 1.0 + 0.05 * nrm(ks[2], (L, D), f32),
        'w_ada': 0.5 * D ** -0.5 * nrm(ks[3], (L, D, N_MOD * D), f32),
        'b_ada': 0.02 * nrm(ks[4], (L, N_MOD * D), f32),
        'w_in': D ** -0.5 * nrm(ks[5], (L, D, D_IN), f32),
        'conv_w': CONV_W ** -0.5 * nrm(ks[6], (L, CONV_W, CONV_CH), f32),
        'sb_q_g': 1.0 + 0.05 * nrm(ks[7], (L, HEAD_DIM), f32),
        'sb_k_g': 1.0 + 0.05 * nrm(ks[8], (L, HEAD_DIM), f32),
        'fox_q_g': 1.0 + 0.05 * nrm(ks[9], (L, HEAD_DIM), f32),
        'fox_k_g': 1.0 + 0.05 * nrm(ks[10], (L, HEAD_DIM), f32),
        'fox_f_b': 2.0 + 0.5 * nrm(ks[11], (L, FOX_HEADS), f32),
        'out_norm_g': 1.0 + 0.05 * nrm(ks[12], (L, D_MIX), f32),
        'w_out': D_MIX ** -0.5 * nrm(ks[13], (L, D_MIX, D), f32),
        'norm2_g': 1.0 + 0.05 * nrm(ks[14], (L, D), f32),
        'router_w': D ** -0.5 * nrm(ks[15], (L, D, E), f32),
        'router_b': 0.01 * nrm(ks[16], (L, E), f32),
        'w_mlp1': D ** -0.5 * nrm(ks[17], (L, E, D, 2 * D_EXPERT), f32),
        'b_mlp1': 0.01 * nrm(ks[18], (L, E, 2 * D_EXPERT), f32),
        'w_mlp2': D_EXPERT ** -0.5 * nrm(ks[19], (L, E, D_EXPERT, D), f32),
        'b_mlp2': 0.01 * nrm(ks[20], (L, E, D), f32),
    }

def first_block(x, c, norm1_g, w_ada, b_ada, w_in, conv_w, sb_q_g, sb_k_g, fox_q_g, fox_k_g, fox_f_b,
              out_norm_g, w_out, norm2_g, router_w, router_b, w_mlp1, b_mlp1, w_mlp2, b_mlp2):
    for l in range(DEPTH):
        x = hybrid_layer(x, c, norm1_g[l], w_ada[l], b_ada[l], w_in[l], conv_w[l], sb_q_g[l], sb_k_g[l],
                         fox_q_g[l], fox_k_g[l], fox_f_b[l], out_norm_g[l], w_out[l], norm2_g[l],
                         router_w[l], router_b[l], w_mlp1[l], b_mlp1[l], w_mlp2[l], b_mlp2[l])
    return x


DEPTH_2 = 2

MIX_WIDTH = D_MODEL
A_HEADS = 4
A_HEAD_DIM = MIX_WIDTH // 2 // A_HEADS
A_WIDTH = A_HEADS * A_HEAD_DIM
B_HEADS = 4
B_HEAD_DIM = MIX_WIDTH // 2 // B_HEADS
B_WIDTH = B_HEADS * B_HEAD_DIM
IN_AB = A_WIDTH + 2 * B_WIDTH
CONV_WIDTH = 31
POOL_WINDOWS = (2, 4, 8, 16)
C_GROUPS = len(POOL_WINDOWS)
C_GROUP_DIM = D_MODEL // C_GROUPS
D_FF = int(math.ceil((8 * D_MODEL / 3) / 256) * 256)
N_EVEN = (DEPTH_2 + 1) // 2
N_ODD = DEPTH_2 // 2
RMS_EPS = 1e-6
LN_EPS = 1e-5


def rmsnorm(x, g):
    xf = x.astype(jnp.float32)
    inv = lax.rsqrt(jnp.mean(xf * xf, axis=-1, keepdims=True) + RMS_EPS)
    return (xf * inv).astype(x.dtype) * g

def layernorm(x, g, b):
    xf = x.astype(jnp.float32)
    mu = jnp.mean(xf, axis=-1, keepdims=True)
    var = jnp.mean(jnp.square(xf - mu), axis=-1, keepdims=True)
    return ((xf - mu) * lax.rsqrt(var + LN_EPS)).astype(x.dtype) * g + b

def swiglu_ffn(h, w_gate, w_up, w_down):
    return (jax.nn.silu(h @ w_gate) * (h @ w_up)) @ w_down

def fnet_heads(a, fnet_map):
    bsz, seq, _ = a.shape
    a4 = a.reshape(bsz, seq, A_HEADS, A_HEAD_DIM).astype(jnp.float32)
    f = jnp.fft.fft2(a4, axes=(1, 3), norm="ortho").real.astype(a.dtype)
    y = jnp.einsum("bshd,hde->bshe", f, fnet_map)
    return y.reshape(bsz, seq, A_WIDTH)

def conformer_conv_heads(v, gate, conv_w, conv_b, ln_g, ln_b):
    u = v * jax.nn.sigmoid(gate)
    pad = CONV_WIDTH // 2
    u = lax.conv_general_dilated(
        u, conv_w[:, None, :].astype(u.dtype),
        window_strides=(1,), padding=[(pad, pad)],
        dimension_numbers=("NWC", "WIO", "NWC"),
        feature_group_count=B_WIDTH) + conv_b
    bsz, seq, _ = u.shape
    u = u.reshape(bsz, seq, B_HEADS, B_HEAD_DIM)
    u = layernorm(u, ln_g.reshape(B_HEADS, B_HEAD_DIM), ln_b.reshape(B_HEADS, B_HEAD_DIM))
    return jax.nn.silu(u).reshape(bsz, seq, B_WIDTH)

def centred_pool_minus_self(u, window):
    seq = u.shape[1]
    uf = u.astype(jnp.float32)
    cs = jnp.concatenate([jnp.zeros_like(uf[:, :1]), lax.cumsum(uf, axis=1)], axis=1)
    pos = jnp.arange(seq, dtype=jnp.int32)
    lo = jnp.clip(pos - window // 2, 0, seq)
    hi = jnp.clip(pos - window // 2 + window, 0, seq)
    win_sum = jnp.take(cs, hi, axis=1) - jnp.take(cs, lo, axis=1)
    cnt = (hi - lo).astype(jnp.float32)[None, :, None]
    return (win_sum / cnt - uf).astype(u.dtype)

def pool_mixer(h, pool_map, pool_scale):
    outs = []
    for gi, w in enumerate(POOL_WINDOWS):
        hg = h[..., gi * C_GROUP_DIM:(gi + 1) * C_GROUP_DIM]
        pg = centred_pool_minus_self(hg, w)
        outs.append(pg @ pool_map[gi])
    return jnp.concatenate(outs, axis=-1) * pool_scale

def second_inputs(seed: int = 0) -> dict:
    key = jax.random.key(seed)
    ks = jax.random.split(key, 20)
    f32 = jnp.float32
    nrm = lambda k, shape, fan_in: jax.random.normal(k, shape, f32) * (fan_in ** -0.5)
    gain = lambda k, shape: 1.0 + 0.05 * jax.random.normal(k, shape, f32)
    return {
        "x": jax.random.normal(ks[0], (BATCH, SEQ, D_MODEL), f32),
        "norm_mix_g": gain(ks[1], (DEPTH_2, D_MODEL)),
        "norm_ffn_g": gain(ks[2], (DEPTH_2, D_MODEL)),
        "w_in_ab": nrm(ks[3], (N_EVEN, D_MODEL, IN_AB), D_MODEL),
        "fnet_map": nrm(ks[4], (N_EVEN, A_HEADS, A_HEAD_DIM, A_HEAD_DIM), A_HEAD_DIM),
        "conv_w": nrm(ks[5], (N_EVEN, CONV_WIDTH, B_WIDTH), CONV_WIDTH),
        "conv_b": 0.02 * jax.random.normal(ks[6], (N_EVEN, B_WIDTH), f32),
        "conv_ln_g": gain(ks[7], (N_EVEN, B_WIDTH)),
        "conv_ln_b": 0.02 * jax.random.normal(ks[8], (N_EVEN, B_WIDTH), f32),
        "w_out_ab": nrm(ks[9], (N_EVEN, MIX_WIDTH, D_MODEL), MIX_WIDTH),
        "pool_map": nrm(ks[10], (N_ODD, C_GROUPS, C_GROUP_DIM, C_GROUP_DIM), C_GROUP_DIM),
        "pool_scale": 1.0 + 0.1 * jax.random.normal(ks[11], (N_ODD, D_MODEL), f32),
        "ffn_w_gate": nrm(ks[12], (DEPTH_2, D_MODEL, D_FF), D_MODEL),
        "ffn_w_up": nrm(ks[13], (DEPTH_2, D_MODEL, D_FF), D_MODEL),
        "ffn_w_down": nrm(ks[14], (DEPTH_2, D_FF, D_MODEL), D_FF),
        "final_g": gain(ks[15], (D_MODEL,)),
    }

def second_block(x, norm_mix_g, norm_ffn_g, w_in_ab, fnet_map, conv_w, conv_b, conv_ln_g,
              conv_ln_b, w_out_ab, pool_map, pool_scale, ffn_w_gate, ffn_w_up, ffn_w_down,
              final_g):
    for layer in range(DEPTH_2):
        h = rmsnorm(x, norm_mix_g[layer])
        if layer % 2 == 0:
            e = layer // 2
            p = h @ w_in_ab[e]
            ya = fnet_heads(p[..., :A_WIDTH], fnet_map[e])
            yb = conformer_conv_heads(p[..., A_WIDTH:A_WIDTH + B_WIDTH],
                                      p[..., A_WIDTH + B_WIDTH:],
                                      conv_w[e], conv_b[e], conv_ln_g[e], conv_ln_b[e])
            y = jnp.concatenate([ya, yb], axis=-1) @ w_out_ab[e]
        else:
            o = layer // 2
            y = pool_mixer(h, pool_map[o], pool_scale[o])
        x = x + y
        h = rmsnorm(x, norm_ffn_g[layer])
        x = x + swiglu_ffn(h, ffn_w_gate[layer], ffn_w_up[layer], ffn_w_down[layer])
    return rmsnorm(x, final_g)


def setup_inputs(seed=0):
    out = dict(first_inputs(seed))
    for name, value in second_inputs(seed + 1).items():
        if name != "x":
            out[name + "_2"] = value
    return out


def reference(
    x, c, norm1_g, w_ada, b_ada, w_in, conv_w, sb_q_g, sb_k_g, fox_q_g, fox_k_g, fox_f_b,
    out_norm_g, w_out, norm2_g, router_w, router_b, w_mlp1, b_mlp1, w_mlp2, b_mlp2,
    norm_mix_g_2, norm_ffn_g_2, w_in_ab_2, fnet_map_2, conv_w_2, conv_b_2, conv_ln_g_2,
    conv_ln_b_2, w_out_ab_2, pool_map_2, pool_scale_2, ffn_w_gate_2, ffn_w_up_2, ffn_w_down_2,
    final_g_2,
):
    x = first_block(
        x, c, norm1_g, w_ada, b_ada, w_in, conv_w, sb_q_g, sb_k_g, fox_q_g, fox_k_g, fox_f_b,
        out_norm_g, w_out, norm2_g, router_w, router_b, w_mlp1, b_mlp1, w_mlp2, b_mlp2,
    )
    return second_block(
        x, norm_mix_g_2, norm_ffn_g_2, w_in_ab_2, fnet_map_2, conv_w_2, conv_b_2, conv_ln_g_2,
        conv_ln_b_2, w_out_ab_2, pool_map_2, pool_scale_2, ffn_w_gate_2, ffn_w_up_2,
        ffn_w_down_2, final_g_2,
    )


_drawn_inputs = setup_inputs


def setup_inputs(seed=0):
    import zlib

    import numpy as np

    out = dict(_drawn_inputs(seed))
    spreads = {}
    factors = {'sb_q_g': 5.083,
     'sb_k_g': 5.719,
     'fox_q_g': 5.285,
     'fox_k_g': 4.293,
     'router_b': 2.956,
     'b_mlp1': 23.988,
     'b_mlp2': 30.008,
     'conv_b_2': 4.16,
     'conv_ln_b_2': 7.661}
    for name, (base, spread) in spreads.items():
        noise = np.random.default_rng([zlib.crc32(name.encode()), seed]).standard_normal(out[name].shape)
        drawn = base * np.exp(spread * noise) if base else spread * noise
        out[name] = __import__('jax').numpy.asarray(drawn.astype(out[name].dtype))
    for name, factor in factors.items():
        out[name] = (out[name] * factor).astype(out[name].dtype)
    return out
```

```python
from contextlib import ExitStack

import numpy as np

import concourse.bass as bass
from concourse import mybir

F32 = mybir.dt.float32
I32 = mybir.dt.int32
ALU = mybir.AluOpType
ACT = mybir.ActivationFunctionType
AX = mybir.AxisListType.X

NRING = 14
UNIT = 2048
NEXP = 32
CAP = 64
NFF = 22
BIG = 1.0e30

C_IE, C_T1, C_T2, C_MS, C_CM, C_ONE, C_IOTA, C_END = 0, 384, 512, 640, 768, 1152, 1280, 1408

ROWS = ["norm1_g", "norm2_g", "out_norm_g", "mix0", "mix1", "ffn0", "ffn1", "pool_scale", "final"]
RID = {n: i for i, n in enumerate(ROWS)}

CB, CC, CU, SQ, SK, SV, FQ, FK, FV, FL = 0, 256, 512, 768, 1152, 1536, 1920, 2304, 2688, 3072


def constants():
    p = np.arange(128)[:, None]
    c = np.arange(128)[None, :]
    t = np.zeros((128, C_END), np.float32)
    t[:, C_IE:C_IE + 384] = (np.arange(384)[None, :] == p + 128)
    t[:, C_T1:C_T1 + 128] = (p <= c)
    t[:, C_T2:C_T2 + 128] = (p > c)
    t[:, C_MS:C_MS + 128] = (p < c)
    causal = np.where(c <= p, 0.0, -BIG)
    t[:, C_CM:C_CM + 128] = causal
    t[:, C_CM + 256:C_CM + 384] = causal
    t[:, C_ONE:C_ONE + 128] = 1.0
    t[:, C_IOTA:C_IOTA + 128] = c % CAP + 1
    return t


def dft_tables():
    def cs(n, scale):
        k = (np.arange(n)[:, None] * np.arange(n)[None, :]) % n
        a = 2.0 * np.pi * k / n
        return np.cos(a) * scale, np.sin(a) * scale
    c2, s2 = cs(256, 1.0 / 16.0)
    c1, s1 = cs(128, 128.0 ** -0.5)
    out = np.zeros((128, 1280), np.float32)
    for b in range(2):
        out[:, b * 512:b * 512 + 256] = c2[b * 128:(b + 1) * 128]
        out[:, b * 512 + 256:b * 512 + 512] = s2[b * 128:(b + 1) * 128]
    out[:, 1024:1152] = c1
    out[:, 1152:1280] = -s1
    return out


def pool_tables():
    out = np.zeros((128, 2048), np.float32)
    pos = np.arange(256)
    for g, w in enumerate((2, 4, 8, 16)):
        lo = np.clip(pos - w // 2, 0, 256)
        hi = np.clip(pos - w // 2 + w, 0, 256)
        m = np.zeros((256, 256))
        for t in range(256):
            m[lo[t]:hi[t], t] = 1.0 / (hi[t] - lo[t])
        m -= np.eye(256)
        for b in range(2):
            out[:, (g * 2 + b) * 256:(g * 2 + b + 1) * 256] = m[b * 128:(b + 1) * 128]
    return out


class Queue:

    def __init__(self, sem):
        self.sem, self.n, self.items, self.seen, self.open = sem, 0, [], {}, []

    def op(self, fn, *after, sig=True):
        waits = []
        for sem, val in after:
            if self.seen.get(id(sem), 0) < val:
                waits.append((sem, val))
                self.seen[id(sem)] = val
        self.items.append(("op", waits, fn, sig))
        if sig:
            self.n += 1
        return (self.sem, self.n)

    def mark(self):
        if self.items[-1][0] == "op" and not self.items[-1][3]:
            self.items[-1] = self.items[-1][:3] + (True,)
            self.n += 1
        return (self.sem, self.n)

    def last(self):
        return (self.sem, self.n)

    def begin(self, count_ap, limit, ready):
        self.op(None, ready, sig=False)
        self.open.append((self.items, self.n, dict(self.seen), count_ap, limit))
        self.items = []

    def end(self):
        body = self.items
        self.items, n0, self.seen, ap, limit = self.open.pop()
        self.items.append(("if", ap, limit, body, n0, self.n - n0))

    def play(self, eng, items=None):
        for it in self.items if items is None else items:
            if it[0] == "op":
                for sem, val in it[1]:
                    eng.wait_ge(sem, val)
                if it[2] is not None:
                    ins = it[2](eng)
                    if it[3]:
                        ins.then_inc(self.sem, 1)
            else:
                _, ap, limit, body, n0, n = it
                v = eng.value_load(ap, min_val=0, max_val=256)
                with eng.If(v > limit):
                    self.play(eng, body)
                with eng.Else():
                    if n:
                        eng.wait_ge(self.sem, n0)
                        eng.sem_inc(self.sem, n)


def build(nc, I, out):
    with ExitStack() as ctx:
        def sem(name):
            return ctx.enter_context(nc.semaphore(name))

        ring = ctx.enter_context(nc.sbuf_tensor("ring", [128, NRING * UNIT], F32))
        AW = 24300
        A = ctx.enter_context(nc.sbuf_tensor("arena", [128, AW], F32))
        PS = ctx.enter_context(nc.psum_tensor("ps", [128, 8, 512], F32))

        P = Queue(sem("s_pe"))
        V = Queue(sem("s_dve"))
        S = Queue(sem("s_act"))

        top = [0]

        def al(n):
            o = top[0]
            top[0] += n
            assert top[0] <= AW, top[0]
            return o

        def v1(o, n, p0=0, p1=128):
            return A[p0:p1, o:o + n]

        def mm(o, l, r, start, stop, *after, sig=False, skip=False):
            return P.op(lambda e: e.matmul(o, l, r, start=start, stop=stop, skip_group_check=skip), *after, sig=sig)

        def tr(o, i, n, *after, sig=False):
            return P.op(lambda e: e.transpose(o, i, n), *after, sig=sig)

        def ts(o, i, s1, s2, op0, op1, *after):
            if op1 is None:
                return V.op(lambda e: e.tensor_scalar(o, i, s1, None, op0), *after)
            return V.op(lambda e: e.tensor_scalar(o, i, s1, s2, op0, op1), *after)

        def tt_(o, a, b, op, *after):
            return V.op(lambda e: e.tensor_tensor(o, a, b, op), *after)

        def stt(o, a, s, b, op0, op1, *after):
            return V.op(lambda e: e.scalar_tensor_tensor(out=o, in0=a, scalar=s, in1=b, op0=op0, op1=op1), *after)

        def vcopy(o, i, *after):
            return V.op(lambda e: e.tensor_copy(o, i), *after)

        def red(o, i, op, *after):
            return V.op(lambda e: e.tensor_reduce(o, i, AX, op), *after)

        def recip(o, i, *after):
            return V.op(lambda e: e.reciprocal(o, i), *after)

        def act(o, i, f, *after, **kw):
            return S.op(lambda e: e.activation(o, i, f, **kw), *after)

        s_slot = [sem(f"s_slot{i}") for i in range(NRING)]
        stream = []
        freed = []

        def item(src, view):
            n = len(stream)
            s = n % NRING
            stream.append((view(ring[:, s * UNIT:(s + 1) * UNIT]), src, s))
            return view(ring[:, s * UNIT:(s + 1) * UNIT]), (s_slot[s], 16 * (n // NRING + 1)), n

        def release(n):
            t = P.mark()
            while len(freed) < n:
                freed.append(t)

        def rows_item(w, r0, nk, c0, ncol):
            src = w[r0:r0 + 128 * nk, c0:c0 + ncol].rearrange("(c p) n -> p c n", p=128)
            return item(src, lambda u: u[:, 0:nk * ncol].rearrange("p (c n) -> p c n", c=nk))

        small = []

        def load(dst, src, *after):
            s = sem(f"s_l{len(small)}")
            small.append((dst, src, s, after))
            return (s, 16)

        o_c = al(C_END)
        CT = lambda a, n=128, p0=0, p1=128: v1(o_c + a, n, p0, p1)
        ident = CT(C_IE + 128)
        ones = CT(C_ONE)

        def sel(p0, k, r, m):
            return A[p0:p0 + k, o_c + C_IE + 128 + p0 + r:o_c + C_IE + 129 + p0 + r].to_broadcast([k, m])

        def shifted(s, prev):
            a = C_IE + (256 if prev else 128) - s
            return CT(a)

        o_x = al(2048)
        X = v1(o_x, 2048).rearrange("p (t d) -> p t d", t=2)
        o_rows = al(1024)
        NROW = len(ROWS)
        rows = v1(o_rows, 1024, 0, NROW)
        o_gc = al(8 * NROW)
        gcol = v1(o_gc, 8 * NROW).rearrange("p (k r) -> p k r", k=8)
        o_sm = al(400)
        sm_top = [o_sm]

        def sm(n, p0=0, p1=128):
            o = sm_top[0]
            sm_top[0] += n
            assert sm_top[0] <= o_sm + 400
            return v1(o, n, p0, p1)

        base = top[0]

        t_const = load(v1(o_c, C_END), I["const"])
        o_c8 = al(128)
        c8 = v1(o_c8, 128, 0, 8)
        t_c = load(c8, I["c"].rearrange("a (k p) -> (a k) p", p=128))
        t_rows = [load(v1(o_rows, 1024, i, i + 1), a) for i, a in enumerate([
            I["norm1_g"][0:1, :], I["norm2_g"][0:1, :], I["out_norm_g"][0:1, :],
            I["norm_mix_g_2"][0:1, :], I["norm_mix_g_2"][1:2, :],
            I["norm_ffn_g_2"][0:1, :], I["norm_ffn_g_2"][1:2, :],
            I["pool_scale_2"][0:1, :], I["final_g_2"].rearrange("(a n) -> a n", a=1)])]
        t_x = load(X, I["x"].rearrange("a (t p) d -> p (a t) d", p=128))

        o_P = al(6144)
        PJ = v1(o_P, 6144).rearrange("p (t n) -> p t n", t=2)
        o_hT = al(2048)
        hT = v1(o_hT, 2048).rearrange("p (k t) -> p k t", k=8)
        o_qk = al(3072)
        QKT = v1(o_qk, 3072).rearrange("p (c t) -> p c t", c=12)
        o_mr = al(1536)
        modr = v1(o_mr, 1536).rearrange("p (b n) -> p b n", b=3)
        o_ws = al(4608)
        WS = [v1(o_ws + 1152 * i, 1152).rearrange("p (h n) -> p h n", h=3) for i in range(4)]
        Y = v1(o_ws, 2048).rearrange("p (t n) -> p t n", t=2)
        T2k = v1(o_ws + 2048, 2048).rearrange("p (t n) -> p t n", t=2)
        o_cT = al(256)
        cTp = v1(o_cT, 256).rearrange("p (k m) -> p k m", k=8)
        o_wf = al(48)
        wf = v1(o_wf, 48).rearrange("p (k n) -> p k n", k=8)
        o_small1 = al(256)
        fbrow = v1(o_small1, 6, 0, 1)
        rbrow = sm(32, 0, 1)
        o_cw = al(256)
        cwr = v1(o_cw, 256, 0, 3)
        gq = [v1(o_small1 + 8 + i, 1) for i in range(4)]

        t_ab = []
        for q in range(4):
            t_ab.append(load(modr[32 * q:32 * q + 1, :, :],
                             I["b_ada"].rearrange("a (b q n) -> a q b n", b=3, q=4)[:, q, :, :],
                             None))
        t_wf = load(wf, I["w_in"][0, :, FL:FL + 6].rearrange("(k p) n -> p k n", p=128))
        t_fb = load(fbrow, I["fox_f_b"])
        t_rb = load(rbrow, I["router_b"])
        t_cw = load(cwr, I["conv_w"][0, :, :])
        t_gq = []
        for i, n in enumerate(["sb_q_g", "sb_k_g", "fox_q_g", "fox_k_g"]):
            for hf in range(2):
                t_gq.append(load(A[64 * hf:64 * hf + 64, o_small1 + 8 + i:o_small1 + 9 + i],
                                 I[n].rearrange("a d -> d a")))

        t_z0 = V.op(lambda e: e.memset(v1(o_mr, 1536), 0.0))
        t_z1 = V.op(lambda e: e.memset(v1(o_cT, 256), 0.0))
        for i, (d, s, q, a) in enumerate(small):
            if a == (None,):
                small[i] = (d, s, q, (t_z0,))

        sc = sm(128, 0, 8)
        t = act(sc, c8, ACT.Sigmoid, t_c)
        t = tt_(sc, sc, c8, ALU.mult, t)
        t = tr(PS[:, 0, 0:8], sc, CT(C_IE + 128, 8, 0, 8), t, t_const, sig=True)
        t_cT = vcopy(cTp[:, :, 0], PS[:, 0, 0:8], t, t_z1)
        for k in range(8):
            t = tr(PS[:, 1, k * NROW:(k + 1) * NROW], A[0:NROW, o_rows + k * 128:o_rows + (k + 1) * 128],
                   CT(C_IE + 128, NROW, 0, NROW), *t_rows, sig=(k == 7))
        t_gcol = vcopy(gcol.rearrange("p k r -> p (k r)"), PS[:, 1, 0:8 * NROW], t)

        rs = sm(8)

        def rms_rows(dst, sq, *after):
            ss, rr = rs[:, 0:2], rs[:, 2:4]
            for i in range(2):
                t = act(sq[:, i, :], X[:, i, :], ACT.Square, *after, accum_out=ss[:, i:i + 1])
            t = ts(rr, ss, 1.0 / 1024, 1e-6, ALU.mult, ALU.add, t)
            t = act(rr, rr, ACT.Sqrt, t)
            t = recip(rr, rr, t)
            for i in range(2):
                t2 = ts(dst[:, i, :], X[:, i, :], rr[:, i:i + 1], None, ALU.mult, None, t)
            return t2

        def to_T(src, dst, banks, t_src, t_bank, scale=None, bias=None, t_sb=()):
            toks = []
            for m in range(4):
                b = banks[m % len(banks)]
                for k in (2 * m, 2 * m + 1):
                    for i in range(2):
                        w = [t_src] + t_bank
                        if m >= len(banks):
                            w.append(toks[m - len(banks)])
                        o = (k % 2) * 256 + i * 128
                        t = tr(PS[:, b, o:o + 128], src(i, k), ident, *w, sig=(k % 2 == 1 and i == 1))
                for k in ((2 * m,) if scale is None else (2 * m, 2 * m + 1)):
                    o = (k % 2) * 256
                    if scale is None:
                        po = dst[:, k:k + 2, :]
                        pin = PS[:, b, :].rearrange("p (c n) -> p c n", c=2)
                        tk = act(po, pin, ACT.Copy, t) if m % 2 else vcopy(po, pin, t)
                        continue
                    pin, po = PS[:, b, o:o + 256], dst[:, k, :]
                    if bias is None:
                        s = scale(k)
                        if m % 2:
                            tk = act(po, pin, ACT.Copy, t, *t_sb, scale=s)
                        else:
                            tk = ts(po, pin, s, None, ALU.mult, None, t, *t_sb)
                    else:
                        s, b_ = scale(k), bias(k)
                        if m % 2:
                            tk = act(po, pin, ACT.Identity, t, *t_sb, scale=s, bias=b_)
                        else:
                            tk = ts(po, pin, s, b_, ALU.mult, ALU.add, t, *t_sb)
                toks.append(tk)
            return toks[-2:]

        xn = Y
        t_xn = rms_rows(xn, T2k, t_x)

        def ada_block(b, bank, t_bank):
            us = [rows_item(I["w_ada"][0], k * 128, 1, b * 2048, 2048) for k in range(8)]

            def step(k):
                u, tk, n = us[k]
                for q in range(4):
                    t = mm(PS[32 * q:32 * q + 32, bank, :], cTp[:, k, :], u[:, 0, q * 512:(q + 1) * 512],
                           k == 0, k == 7, tk, t_cT, *t_bank, sig=(q == 3))
                release(n + 1)
                return t

            def fin(t):
                return tt_(modr[:, b, :], PS[:, bank, :], modr[:, b, :], ALU.add, t, *t_ab)
            return step, fin

        step, fin = ada_block(0, 2, [])
        for k in range(8):
            t = step(k)
        t_m0 = fin(t)
        for cc in range(4):
            t = tr(PS[:, 3, cc * 128:(cc + 1) * 128], modr[:, 0, cc * 128:(cc + 1) * 128], ident, t_m0, sig=(cc == 3))
        mview = PS[:, 3, :].rearrange("p (c q z) -> p q c z", c=4, q=4)
        a1 = sm(8)
        s1 = sm(8)
        t_a1 = stt(a1.rearrange("p (q c) -> p q c", q=2), mview[:, 2:4, :, 0], 1.0,
                   gcol[:, :, RID["norm1_g"]].rearrange("p (q c) -> p q c", q=2), ALU.add, ALU.mult, t, t_gcol)
        t_s1 = vcopy(s1.rearrange("p (q c) -> p q c", q=2), mview[:, 0:2, :, 0], t)
        t_hT = to_T(lambda i, k: xn[:, i, k * 128:(k + 1) * 128], hT, [4, 5, 6, 7], t_xn, [],
                    scale=lambda k: a1[:, k:k + 1], bias=lambda k: s1[:, k:k + 1], t_sb=[t_a1, t_s1])

        ev = {}
        for j in range(3):
            bk = [0, 1, 2, 3] if j % 2 == 0 else [4, 5, 6, 7]
            for kk in range(4):
                u, tk, n = rows_item(I["w_in"][0], kk * 256, 2, j * 1024, 1024)
                for c in range(2):
                    k = 2 * kk + c
                    for i in range(2):
                        for ns in range(2):
                            w = [tk, *t_hT]
                            if k == 0:
                                w += [t_a1, t_s1, t_cT, t_gcol] if j == 0 else ev.get(j - 2, [])
                            t = mm(PS[:, bk[2 * i + ns], :], hT[:, k, i * 128:(i + 1) * 128],
                                   u[:, c, ns * 512:(ns + 1) * 512], k == 0, k == 7, *w,
                                   sig=(k == 7))
                release(n + 1)
            ev[j] = []
            for i in range(2):
                for ns in range(2):
                    d = PJ[:, i, j * 1024 + ns * 512:j * 1024 + (ns + 1) * 512]
                    sr = PS[:, bk[2 * i + ns], :]
                    ev[j].append(act(d, sr, ACT.Copy, t) if ns else vcopy(d, sr, t))
        for i in range(2):
            for k in range(8):
                mm(PS[:, 4, i * 8:i * 8 + 6], hT[:, k, i * 128:(i + 1) * 128], wf[:, k, :], k == 0, False, t_wf, *ev[1])
            t_fl = mm(PS[:, 4, i * 8:i * 8 + 6], CT(C_ONE, 128, 0, 1), fbrow, False, True, t_fb, sig=True)

        fz = PS[:, 4, 0:16].rearrange("p (t h) -> p t h", t=2)[:, :, 0:6]
        lf = sm(12).rearrange("p (t h) -> p t h", t=2)
        lg = sm(12).rearrange("p (t h) -> p t h", t=2)
        t = act(lg, fz, ACT.Abs, t_fl)
        t = act(lg, lg, ACT.Exp, t, scale=-1.0)
        t = ts(lg, lg, 1.0, None, ALU.add, None, t)
        t = act(lg, lg, ACT.Ln, t)
        t_lf = stt(lf, fz, 0.0, lg, ALU.min, ALU.subtract, t)
        cum = sm(12).rearrange("p (t h) -> p t h", t=2)
        mm(PS[:, 5, 0:6], CT(C_T1), lf[:, 0, :], True, True, t_lf, *ev[1])
        mm(PS[:, 5, 8:14], ones, lf[:, 0, :], True, False)
        t = mm(PS[:, 5, 8:14], CT(C_T1), lf[:, 1, :], False, True, sig=True)
        t_cum = vcopy(cum, PS[:, 5, 0:16].rearrange("p (t h) -> p t h", t=2)[:, :, 0:6], t)
        for i in range(2):
            t = tr(PS[0:6, 6, i * 128:(i + 1) * 128], cum[:, i, :], ident, t_cum, *ev[1], sig=(i == 1))
        o_cumT = al(256)
        cumT = v1(o_cumT, 256, 0, 6)
        t_cumT = ts(cumT, PS[0:6, 6, 0:256], -1.0, None, ALU.mult, None, t)

        rq = v1(o_small1 + 16, 48)
        t_qk = []
        sqs = v1(o_ws, 1536).rearrange("p (t n) -> p t n", t=2)
        t_g8 = [ts(gq[i], gq[i], 0.125, None, ALU.mult, None, *t_gq) for i in (0, 2)]
        prev = list(t_hT)
        for kind, c0 in ((0, SQ), (1, FQ)):
            evs = ev[0] + ev[1] + ev[2]
            seg = PJ[:, :, c0:c0 + 768]
            t = act(sqs, seg, ACT.Square, *evs, *prev)
            r = rq[:, kind * 24:kind * 24 + 24]
            t = red(r, v1(o_ws, 1536).rearrange("p (h d) -> p h d", d=64), ALU.add, t)
            prev = [t]
            t = ts(r, r, 1.0 / 64, 1e-6, ALU.mult, ALU.add, t)
            t = act(r, r, ACT.Sqrt, t)
            t = recip(r, r, t)
            for i in range(2):
                sg = seg[:, i, :].rearrange("p (h d) -> p h d", d=64)
                t2 = tt_(sg, sg, r[:, i * 12:i * 12 + 12].to_broadcast([128, 12, 64]) if False else
                         A[:, o_small1 + 16 + kind * 24 + i * 12:o_small1 + 16 + kind * 24 + i * 12 + 12]
                         .rearrange("p (h o) -> p h o", o=1).to_broadcast([128, 12, 64]), ALU.mult, t)
            for m in range(3):
                b = (kind * 3 + m) % 4
                w = [t2] + ev[2]
                if kind * 3 + m >= 4:
                    w.append(t_qk[kind * 3 + m - 4])
                for c in (2 * m, 2 * m + 1):
                    for i in range(2):
                        o = (c % 2) * 256 + i * 128
                        t = tr(PS[:, b, o:o + 128], PJ[:, i, c0 + c * 128:c0 + (c + 1) * 128], ident, *w,
                               sig=(c % 2 == 1 and i == 1))
                for c in (2 * m, 2 * m + 1):
                    g = gq[2 * kind + (c >= 3)]
                    d, o = QKT[:, kind * 6 + c, :], (c % 2) * 256
                    if m % 2:
                        tk = act(d, PS[:, b, o:o + 256], ACT.Copy, t, *t_g8, *t_gq, scale=g)
                    else:
                        tk = ts(d, PS[:, b, o:o + 256], g, None, ALU.mult, None, t, *t_g8, *t_gq)
                t_qk.append(tk)

        wo_units = None
        ada1 = ada_block(1, 7, [t_m0] + list(t_hT) + ev[1])
        ada_state = {"k": 0, "blk": 0, "t": None}
        ada2 = ada_block(2, 7, [])

        def ada_more(n):
            st = ada_state
            for _ in range(n):
                if st["blk"] == 2:
                    return
                step, fin = (ada1, ada2)[st["blk"]]
                if st["blk"] == 1 and st["k"] == 0:
                    P.op(None, st["t1"], sig=False)
                st["t"] = step(st["k"])
                st["k"] += 1
                if st["k"] == 8:
                    st[f"t{st['blk'] + 1}"] = fin(st["t"])
                    st["blk"] += 1
                    st["k"] = 0

        free = {b: list(t_qk) for b in range(7)}
        t_ws = list(prev) + [t2]
        MS = CT(C_MS).rearrange("p (o n) -> p o n", o=1).to_broadcast([128, 3, 128])
        for g in range(2):
            LG, LB, L1 = WS[0], WS[1], WS[2]
            for hh in range(3):
                h = 3 * g + hh
                c, o = h // 2, (h % 2) * 64
                kT, qT = QKT[o:o + 64, 3 + c, :], QKT[o:o + 64, c, :]
                mm(PS[:, hh, 0:256], kT[:, 0:128], qT, True, True, *free[hh])
                t = mm(PS[:, hh, 256:384], kT[:, 128:256], qT[:, 128:256], True, True, sig=True)
            Z = PS[:, 0:3, 0:384]
            t = act(LG, Z, ACT.Abs, t, *t_ws)
            t = act(LG, LG, ACT.Exp, t, scale=-1.0)
            t = ts(LG, LG, 1.0, None, ALU.add, None, t)
            t = act(LG, LG, ACT.Ln, t)
            t = stt(LB, Z, 0.0, LG, ALU.min, ALU.subtract, t)
            t = tt_(L1, LB, Z, ALU.subtract, t)
            tt_(L1[:, :, 0:128], L1[:, :, 0:128], MS, ALU.mult, t)
            t = tt_(L1[:, :, 256:384], L1[:, :, 256:384], MS, ALU.mult, t)
            ada_more(4)
            for hh in range(3):
                b = 3 + hh
                mm(PS[:, b, 0:256], CT(C_T2), L1[:, hh, 0:256], True, False, t, *free[b])
                mm(PS[:, b, 128:256], ones, L1[:, hh, 256:384], False, False)
                t2 = mm(PS[:, b, 256:384], CT(C_T2), L1[:, hh, 256:384], False, True, sig=True)
            t = tt_(LB, LB, PS[:, 3:6, 0:384], ALU.add, t2)
            t = act(LG, LB, ACT.Exp, t)
            tt_(LG[:, :, 0:128], LG[:, :, 0:128], MS, ALU.mult, t)
            t = tt_(LG[:, :, 256:384], LG[:, :, 256:384], MS, ALU.mult, t)
            ada_more(4)
            for hh in range(3):
                h = 3 * g + hh
                vv = [PJ[:, i, SV + h * 64:SV + (h + 1) * 64] for i in range(2)]
                oo = [PS[:, 6, i * 256 + hh * 64:i * 256 + (hh + 1) * 64] for i in range(2)]
                mm(oo[0], LG[:, hh, 0:128], vv[0], True, True, t, *free[6])
                mm(oo[1], LG[:, hh, 128:256], vv[0], True, False)
                t2 = mm(oo[1], LG[:, hh, 256:384], vv[1], False, True, sig=True)
            t = vcopy(PJ[:, :, SQ + 192 * g:SQ + 192 * g + 192],
                      PS[:, 6, :].rearrange("p (t n) -> p t n", t=2)[:, :, 0:192], t2)
            t_ws = [t2, t]
            for b in range(7):
                free[b] = [t]

        mx = v1(o_small1 + 64, 6)
        sums = v1(o_small1 + 72, 6)
        for g in range(2):
            E, ET = WS[0], WS[1]
            for hh in range(3):
                h = 3 * g + hh
                c, o = h // 2, (h % 2) * 64
                kT, qT = QKT[o:o + 64, 9 + c, :], QKT[o:o + 64, 6 + c, :]
                mm(PS[:, hh, 0:128], qT[:, 0:128], kT[:, 0:128], True, False, *free[hh])
                mm(PS[:, hh, 0:128], sel(0, 6, h, 128), cumT[:, 0:128], False, True, t_cumT)
                mm(PS[:, hh, 128:384], qT[:, 128:256], kT, True, False)
                t = mm(PS[:, hh, 128:384], sel(0, 6, h, 128), cumT[:, 0:256], False, True, sig=True)
            for hh in range(3):
                h = 3 * g + hh
                stt(E[:, hh, 0:128], PS[:, hh, 0:128], cum[:, 0, h:h + 1], CT(C_CM), ALU.add, ALU.add, t, *t_ws)
                tl = stt(E[:, hh, 128:384], PS[:, hh, 128:384], cum[:, 1, h:h + 1], CT(C_CM + 128, 256),
                         ALU.add, ALU.add, t)
            red(mx[:, 0:3], E[:, :, 0:128], ALU.max, tl)
            t = red(mx[:, 3:6], E[:, :, 128:384], ALU.max, tl)
            t = ts(mx, mx, -1.0, None, ALU.mult, None, t)
            for hh in range(3):
                act(E[:, hh, 0:128], E[:, hh, 0:128], ACT.Exp, t, bias=mx[:, hh:hh + 1],
                    accum_out=sums[:, hh:hh + 1])
                t2 = act(E[:, hh, 128:384], E[:, hh, 128:384], ACT.Exp, bias=mx[:, 3 + hh:4 + hh],
                         accum_out=sums[:, 3 + hh:4 + hh])
            t_r = recip(sums, sums, t2)
            for hh in range(3):
                for q in range(3):
                    t = tr(PS[:, 3 + hh, q * 128:(q + 1) * 128], E[:, hh, q * 128:(q + 1) * 128], ident,
                           t2, *free[3 + hh], sig=(q == 2))
            t3 = act(ET, PS[:, 3:6, 0:384], ACT.Copy, t)
            for hh in range(3):
                h = 3 * g + hh
                vv = [PJ[:, i, FV + h * 64:FV + (h + 1) * 64] for i in range(2)]
                oo = [PS[:, 6, i * 256 + hh * 64:i * 256 + (hh + 1) * 64] for i in range(2)]
                mm(oo[0], ET[:, hh, 0:128], vv[0], True, True, t3, *free[6])
                mm(oo[1], ET[:, hh, 128:256], vv[0], True, False)
                t2 = mm(oo[1], ET[:, hh, 256:384], vv[1], False, True, sig=True)
            for i in range(2):
                rb = sums[:, 3 * i:3 * i + 3].rearrange("p (h o) -> p h o", o=1).to_broadcast([128, 3, 64])
                t = tt_(PJ[:, i, FQ + 192 * g:FQ + 192 * g + 192].rearrange("p (h d) -> p h d", d=64),
                        PS[:, 6, i * 256:i * 256 + 192].rearrange("p (h d) -> p h d", d=64), rb, ALU.mult, t2, t_r)
            t_ws = [t2, t]
            for b in range(7):
                free[b] = [t]
        ada_more(16)

        vcv = v1(o_qk, 512).rearrange("p (t n) -> p t n", t=2)
        vw = [v1(o_qk + 512 + 512 * i, 512).rearrange("p (t n) -> p t n", t=2) for i in range(3)]
        t_v = tt_(vcv, PJ[:, :, CC:CC + 256], PJ[:, :, CU:CU + 256], ALU.mult, t, t2)
        for w in range(3):
            t = mm(PS[:, w, 0:256], sel(0, 3, w, 128), cwr, True, True, t_cw, *free[w], sig=True)
            for i in range(2):
                tw = tt_(vw[w][:, i, :], PS[:, w, 0:256], vcv[:, i, :], ALU.mult, t, t_v)
        for i in range(2):
            o = PS[:, 3, i * 256:(i + 1) * 256]
            for w in range(3):
                last = w == 2
                mm(o, shifted(2 - w, False), vw[w][:, i, :], w == 0, last and i == 0, tw, *free[3], sig=last)
            if i == 1:
                mm(o, shifted(2, True), vw[0][:, 0, :], False, False)
                t = mm(o, shifted(1, True), vw[1][:, 0, :], False, True, sig=True)
        t_y = tt_(PJ[:, :, CB:CB + 256], PS[:, 3, :].rearrange("p (t n) -> p t n", t=2), PJ[:, :, CB:CB + 256],
                  ALU.mult, t)

        gr = v1(o_small1 + 80, 32).rearrange("p (t g) -> p t g", t=2)
        segs = [(CB, 4, 0), (SQ, 6, 4), (FQ, 6, 10)]
        for c0, n, g0 in segs:
            t = act(Y[:, :, g0 * 64:(g0 + n) * 64], PJ[:, :, c0:c0 + n * 64], ACT.Square, t_y, *t_ws)
        t = red(gr.rearrange("p t g -> p (t g)"), v1(o_ws, 2048).rearrange("p (g d) -> p g d", d=64), ALU.add, t)
        t = ts(gr, gr, 1.0 / 64, 1e-6, ALU.mult, ALU.add, t)
        t = act(gr, gr, ACT.Sqrt, t)
        t = recip(gr, gr, t)
        for i in range(2):
            for c0, n, g0 in segs:
                rb = gr[:, i, g0:g0 + n].rearrange("p (g o) -> p g o", o=1).to_broadcast([128, n, 64])
                t2 = tt_(Y[:, i, g0 * 64:(g0 + n) * 64].rearrange("p (g d) -> p g d", d=64),
                         PJ[:, i, c0:c0 + n * 64].rearrange("p (g d) -> p g d", d=64), rb, ALU.mult, t)
        t_yT = to_T(lambda i, k: Y[:, i, k * 128:(k + 1) * 128], hT, [0, 1, 2, 3], t2, [t_y, t2],
                    scale=lambda k: gcol[:, k, RID["out_norm_g"]:RID["out_norm_g"] + 1])

        def spread(bank, k, p0, r, rhs, *after):
            return mm(PS[:, bank, :], sel(p0, k, r, 128), rhs, True, True, *after, sig=True)

        def mod_row(bank, v, half, *after):
            f = v * 1024 + half * 512
            b, q = f // 2048, (f % 2048) // 512
            return mm(PS[:, bank, :], sel_w(q), modr[:, b, :], True, True, *after, sig=True)

        def sel_w(q):
            return A[:, o_c + C_IE + 128 + 32 * q:o_c + C_IE + 129 + 32 * q].to_broadcast([128, 128])

        t_mod = [ada_state["t1"], ada_state["t2"]]
        G1B = v1(o_P, 1024)
        A2B = v1(o_P + 1024, 1024)
        S2B = v1(o_P + 2048, 1024)
        TMP = v1(o_P + 3072, 1024)
        tg = []
        for hf in range(2):
            t = mod_row(4 + hf, 2, hf, *t_mod, t_y, t2, *free[4])
            tg.append(act(G1B[:, hf * 512:(hf + 1) * 512], PS[:, 4 + hf, :], ACT.Copy, t, t2))
        for hf in range(2):
            t = mod_row(6 + hf, 3, hf, *t_mod, *free[6])
            tg.append(act(S2B[:, hf * 512:(hf + 1) * 512], PS[:, 6 + hf, :], ACT.Copy, t))
        for hf in range(2):
            t = mod_row(4 + hf, 4, hf, *tg)
            tg.append(act(TMP[:, hf * 512:(hf + 1) * 512], PS[:, 4 + hf, :], ACT.Copy, t))
        t_a2 = []
        for hf in range(2):
            t = spread(6 + hf, NROW, 0, RID["norm2_g"], A[0:NROW, o_rows + hf * 512:o_rows + hf * 512 + 512], *tg)
            t_a2.append(stt(A2B[:, hf * 512:(hf + 1) * 512], TMP[:, hf * 512:(hf + 1) * 512], 1.0, PS[:, 6 + hf, :],
                            ALU.add, ALU.mult, t, *tg))

        def out_proj(w, lT, t_l, gate, t_bank, banks=(0, 1, 2, 3), tmp=None):
            for kk in range(4):
                u, tk, n = rows_item(w, kk * 256, 2, 0, 1024)
                for c in range(2):
                    k = 2 * kk + c
                    for i in range(2):
                        for ns in range(2):
                            t = mm(PS[:, banks[2 * i + ns], :], lT[:, k, i * 128:(i + 1) * 128],
                                   u[:, c, ns * 512:(ns + 1) * 512], k == 0, k == 7, tk, *t_l, *t_bank, sig=(k == 7))
                release(n + 1)
            for i in range(2):
                for ns in range(2):
                    xs = X[:, i, ns * 512:(ns + 1) * 512]
                    pb = PS[:, banks[2 * i + ns], :]
                    if gate is not None:
                        t = tt_(tmp[:, i, ns * 512:(ns + 1) * 512], pb, gate[:, ns * 512:(ns + 1) * 512], ALU.mult, t, *tg)
                        t = tt_(xs, xs, tmp[:, i, ns * 512:(ns + 1) * 512], ALU.add, t)
                    else:
                        t = tt_(xs, xs, pb, ALU.add, t)
            return t

        t_x1 = out_proj(I["w_out"][0], hT, t_yT, G1B, list(t_yT), tmp=T2k)

        o_h2 = o_hT
        H2 = v1(o_h2, 2048).rearrange("p (t n) -> p t n", t=2)
        t = rms_rows(Y, T2k, t_x1)
        ab = A2B.rearrange("p (o n) -> p o n", o=1).to_broadcast([128, 2, 1024])
        sb_ = S2B.rearrange("p (o n) -> p o n", o=1).to_broadcast([128, 2, 1024])
        t = tt_(H2, Y, ab, ALU.mult, t, *t_a2)
        t_h2 = tt_(H2, H2, sb_, ALU.add, t)
        H2T = T2k.rearrange("p t n -> p (t n)").rearrange("p (k t) -> p k t", k=8)
        t_h2T = to_T(lambda i, k: H2[:, i, k * 128:(k + 1) * 128], H2T, [4, 5, 6, 7], t_h2, [t_h2, *t_a2])
        o_rw = o_qk + 2048
        rw = v1(o_rw, 256).rearrange("p (k n) -> p k n", k=8)
        t_rw = load(rw, I["router_w"][0].rearrange("(k p) n -> p k n", p=128), t_v, tw, t_x1)
        rt = o_rw + 256
        lgt = v1(rt, 64).rearrange("p (t n) -> p t n", t=2)
        top8 = v1(rt + 64, 16).rearrange("p (t n) -> p t n", t=2)
        gt = v1(rt + 80, 64).rearrange("p (t n) -> p t n", t=2)
        eq = v1(rt + 144, 64).rearrange("p (t n) -> p t n", t=2)
        ce = v1(rt + 208, 64).rearrange("p (t n) -> p t n", t=2)
        ngt = v1(rt + 272, 4)
        nmx = v1(rt + 276, 4)
        for i in range(2):
            o = PS[:, 0, i * 32:(i + 1) * 32]
            for k in range(8):
                mm(o, H2T[:, k, i * 128:(i + 1) * 128], rw[:, k, :], k == 0, False, t_rw, *t_h2T, t_x1)
            t = mm(o, CT(C_ONE, 128, 0, 1), rbrow, False, True, t_rb, sig=True)
        t = vcopy(lgt, PS[:, 0, 0:64].rearrange("p (t n) -> p t n", t=2), t)
        o_gate = al(64)
        gate = v1(o_gate, 64).rearrange("p (t n) -> p t n", t=2)
        o_pos = al(64)
        posm = v1(o_pos, 64).rearrange("p (t n) -> p t n", t=2)
        o_cnt = al(32)
        for i in range(2):
            tm = V.op(lambda e, i=i: e.max(top8[:, i, :], lgt[:, i, :]), t)
        for i in range(2):
            v4 = top8[:, i, 3:4]
            tg_ = ts(gt[:, i, :], lgt[:, i, :], v4, None, ALU.is_gt, None, tm)
            te = ts(eq[:, i, :], lgt[:, i, :], v4, None, ALU.is_equal, None, tm)
            tn = red(ngt[:, i:i + 1], gt[:, i, :], ALU.add, tg_)
            tn = ts(ngt[:, i:i + 1], ngt[:, i:i + 1], -1.0, 4.0, ALU.mult, ALU.add, tn)
            tc = V.op(lambda e, i=i: e.tensor_tensor_scan(ce[:, i, :], CT(C_ONE, 32), eq[:, i, :], 0.0,
                                                          ALU.mult, ALU.add), te)
            tc = stt(eq[:, i, :], ce[:, i, :], ngt[:, i:i + 1], eq[:, i, :], ALU.is_le, ALU.mult, tc, tn)
            tc = tt_(gt[:, i, :], gt[:, i, :], eq[:, i, :], ALU.add, tc)
            tx = ts(nmx[:, i:i + 1], top8[:, i, 0:1], -1.0, None, ALU.mult, None, tm)
            tx = act(ce[:, i, :], lgt[:, i, :], ACT.Exp, tx, tc, bias=nmx[:, i:i + 1])
            tx = tt_(ce[:, i, :], ce[:, i, :], gt[:, i, :], ALU.mult, tx)
            tx = red(nmx[:, 2 + i:3 + i], ce[:, i, :], ALU.add, tx)
            tx = recip(nmx[:, 2 + i:3 + i], nmx[:, 2 + i:3 + i], tx)
            t_gate = ts(gate[:, i, :], ce[:, i, :], nmx[:, 2 + i:3 + i], None, ALU.mult, None, tx)
        t_selm = tc
        mm(PS[:, 1, 0:32], CT(C_T1), gt[:, 0, :], True, True, t_selm, t_x1)
        mm(PS[:, 1, 32:64], ones, gt[:, 0, :], True, False)
        t = mm(PS[:, 1, 32:64], CT(C_T1), gt[:, 1, :], False, True, sig=True)
        t_pos = tt_(posm, PS[:, 1, 0:64].rearrange("p (t n) -> p t n", t=2), gt, ALU.mult, t)
        mm(PS[0:1, 2, 0:32], CT(C_ONE, 1), gt[:, 0, :], True, False, t_x1)
        t = mm(PS[0:1, 2, 0:32], CT(C_ONE, 1), gt[:, 1, :], False, True, sig=True)
        cnt = A[0:1, o_cnt:o_cnt + 32].bitcast(I32)
        t_cnt = vcopy(cnt, PS[0:1, 2, 0:32], t)
        for i in range(2):
            t = tr(PS[0:32, 3, i * 128:(i + 1) * 128], gate[:, i, :], ident, t_gate, t_x1, sig=(i == 1))
        gT = v1(rt, 256, 0, 32)
        t_gT = vcopy(gT, PS[0:32, 3, 0:256], t, t_pos, t_gate)

        G2B = v1(o_P + 4096, 1024)
        o_acc = o_P
        ACCv = v1(o_acc, 2048).rearrange("p (t n) -> p t n", t=2)
        B1 = v1(o_P + 2048, 2048, 0, 32)
        B2 = v1(o_P + 5120, 1024, 0, 32)
        t_b1 = load(B1, I["b_mlp1"][0], t_h2)
        t_b2 = load(B2, I["b_mlp2"][0], t_h2)
        tg2 = []
        for hf in range(2):
            t = mod_row(4 + hf, 5, hf, *t_h2T)
            tg2.append(act(G2B[:, hf * 512:(hf + 1) * 512], PS[:, 4 + hf, :], ACT.Copy, t, t_h2))
        for i in range(2):
            for ns in range(2):
                b = 4 + 2 * i + ns
                t = mm(PS[:, b, :], gT[:, i * 128:(i + 1) * 128], B2[:, ns * 512:(ns + 1) * 512], True, True,
                       t_gT, t_b2, *tg2, *t_h2T, sig=True)
                t_acc = vcopy(ACCv[:, i, ns * 512:(ns + 1) * 512], PS[:, b, :], t, t_h2)
        t_moe0 = [t_acc, t_gT, t_pos, t_gate, t_cnt]

        w_ = [o_ws, o_ws + 4608]

        def take(n):
            o = w_[0]
            w_[0] += n
            assert w_[0] <= w_[1]
            return v1(o, n)

        XG = take(512)
        GLU = take(512)
        LIN = take(512)
        SIG = take(512)
        OB = take(512)
        OBO = take(512)
        AT = take(512)
        SG = take(256)
        ST = take(128)
        w_ = [o_qk, o_qk + 2560]
        XGT = [take(512) for _ in range(3)]
        SGT = [take(256) for _ in range(3)]
        w_ = [o_mr, o_mr + 1536]
        pc = take(128)

        fb = {b: list(t_moe0) for b in range(8)}
        B = {"xg": list(t_moe0), "glu": list(t_moe0), "at": [], "ob": [], "obo": [], "sg": list(t_moe0), "st": []}
        xr = [list(t_moe0), list(t_moe0), list(t_moe0)]
        sr = [list(t_moe0), list(t_moe0), list(t_moe0)]

        def gather(e, c, k):
            if c:
                t0 = ts(pc[:, 0:2], posm[:, :, e], -float(CAP * c), None, ALU.add, None, *B["st"], *t_mod, tg2[1])
                at = lambda i: pc[:, i:i + 1]
            else:
                t0 = t_pos
                at = lambda i: posm[:, i, e:e + 1]
            for i in range(2):
                t1 = ts(ST[:, i * 64:(i + 1) * 64], CT(C_IOTA, 64), at(i), None, ALU.is_equal, None, t0, *B["st"])
            for i in range(2):
                t2 = ts(SG[:, i * 128:(i + 1) * 128], CT(C_IOTA), at(i), gate[:, i, e:e + 1], ALU.is_equal, ALU.mult,
                        t0, *B["sg"])
            for i in range(2):
                for g in range(2):
                    t = mm(PS[64 * g:64 * g + 64, 3, :], ST[:, i * 64:(i + 1) * 64], H2[:, i, g * 512:(g + 1) * 512],
                           i == 0, i == 1, t1, *fb[3], sig=(i == 1 and g == 1))
            B["st"] = [t]
            t = act(XG, PS[:, 3, :], ACT.Copy, t, *B["xg"])
            fb[3] = [t]
            for q in range(4):
                tq = tr(PS[:, 2, q * 128:(q + 1) * 128], XG[:, q * 128:(q + 1) * 128], ident, t, *fb[2], sig=(q == 3))
            B["xg"] = [tq]
            t_x = vcopy(XGT[k], PS[:, 2, :], tq, *xr[k])
            for i in range(2):
                tq = tr(PS[:, 2, i * 128:(i + 1) * 128], SG[:, i * 128:(i + 1) * 128], ident, t2, t_x, sig=(i == 1))
            B["sg"] = [tq]
            t_s = vcopy(SGT[k], PS[:, 2, 0:256], tq, *sr[k])
            fb[2] = [t_s]
            return t_x, t_s

        def mlp1(e, u1, k, t_x):
            x4 = XGT[k].rearrange("p (c z) -> p c z", c=4)
            for g in range(2):
                for ns in range(2):
                    f = (2 * g + ns) * 512
                    mm(PS[64 * g:64 * g + 64, ns, :], sel(0, 32, e, 64), B1[:, f:f + 512], True, False,
                       t_b1, *fb[0])
            for k8 in range(8):
                u, tk, n = u1[k8]
                kg, kc = k8 // 4, k8 % 4
                for ns in range(2):
                    for g in range(2):
                        f = (2 * g + ns) * 512
                        t = mm(PS[64 * g:64 * g + 64, ns, :], x4[:, kc, 64 * kg:64 * kg + 64], u[:, 0, f:f + 512],
                               False, k8 == 7, tk, t_x, sig=(k8 == 7))
            xr[k] = [t]
            return t

        def glu(t):
            U = PS[:, 0:2, :].rearrange("p b (n two) -> p b n two", two=2)
            g3 = GLU.rearrange("p (b n) -> p b n", b=2)
            l3 = LIN.rearrange("p (b n) -> p b n", b=2)
            tg = ts(g3, U[:, :, :, 0], 7.0, None, ALU.min, None, t, *B["glu"])
            tl = ts(l3, U[:, :, :, 1], 7.0, -7.0, ALU.min, ALU.max, t)
            fb[0] = [tl]
            t_s = act(SIG, GLU, ACT.Sigmoid, tg, *B["glu"], scale=1.702)
            tl = stt(LIN, LIN, 1.0, GLU, ALU.add, ALU.mult, tl)
            return tt_(LIN, LIN, SIG, ALU.mult, t_s, tl)

        def mlp2(u2, t_a, ob, key):
            for q in range(4):
                t = tr(PS[:, 2, q * 128:(q + 1) * 128], LIN[:, q * 128:(q + 1) * 128], ident, t_a, *fb[2], sig=(q == 3))
            B["glu"] = [t]
            t_at = act(AT, PS[:, 2, :], ACT.Copy, t, *B["at"])
            fb[2] = [t_at]
            a4 = AT.rearrange("p (c z) -> p c z", c=4)
            for k8 in range(8):
                u, tk, n = u2[k8 // 2]
                kg, kc = k8 // 4, k8 % 4
                for g in range(2):
                    t = mm(PS[64 * g:64 * g + 64, 3, :], a4[:, kc, 64 * kg:64 * kg + 64],
                           u[:, k8 % 2, g * 512:(g + 1) * 512], k8 == 0, k8 == 7, tk, t_at, *fb[3],
                           sig=(k8 == 7 and g == 1))
            B["at"] = [t]
            t = act(ob, PS[:, 3, :], ACT.Copy, t, *B[key])
            fb[3] = [t]
            return t

        def back(k, ob, key, t_o, t_s):
            for i in range(2):
                for g in range(2):
                    t = mm(PS[:, 4 + 2 * i + g, :], SGT[k][64 * g:64 * g + 64, i * 128:(i + 1) * 128],
                           ob[64 * g:64 * g + 64, :], True, True, t_o, t_s, *fb[4 + 2 * i], sig=(g == 1))
                ta = tt_(ACCv[:, i, :].rearrange("p (g n) -> p g n", g=2), PS[:, 4 + 2 * i:6 + 2 * i, :],
                         ACCv[:, i, :].rearrange("p (g n) -> p g n", g=2), ALU.add, t, t_acc, *acc_last[i])
                acc_last[i] = [ta]
                fb[4 + 2 * i] = [ta]
            B[key] = [t]
            sr[k] = [t]

        acc_last = [[], []]

        def lot(e, c, u1, u2):
            t_x, t_s = gather(e, c, 2)
            t = mlp1(e, u1, 2, t_x)
            t = glu(t)
            t = mlp2(u2, t, OBO, "obo")
            back(2, OBO, "obo", t, t_s)

        nxt = gather(0, 0, 0)
        for e in range(NEXP):
            u1 = [rows_item(I["w_mlp1"][0, e], k * 128, 1, 0, 2048) for k in range(8)]
            u2 = [rows_item(I["w_mlp2"][0, e], k * 256, 2, 0, 1024) for k in range(4)]
            t_x, t_s = nxt
            t = mlp1(e, u1, e % 2, t_x)
            t_a = glu(t)
            if e + 1 < NEXP:
                nxt = gather(e + 1, 0, (e + 1) % 2)
            t_o = mlp2(u2, t_a, OB, "ob")
            ce_ = cnt[0:1, e:e + 1]
            for q in (P, V, S):
                q.begin(ce_, CAP, t_cnt)
            lot(e, 1, u1, u2)
            for q in (P, V, S):
                q.begin(ce_, 2 * CAP, t_cnt)
            lot(e, 2, u1, u2)
            lot(e, 3, u1, u2)
            for q in (P, V, S):
                q.end()
            for q in (P, V, S):
                q.end()
            release(u2[3][2] + 1)
            back(e % 2, OB, "ob", t_o, t_s)
        t_back = acc_last[0] + acc_last[1]

        for i in range(2):
            t = tt_(ACCv[:, i, :], ACCv[:, i, :], G2B, ALU.mult, *t_back, *tg2)
            t_x2 = tt_(X[:, i, :], X[:, i, :], ACCv[:, i, :], ALU.add, t)
        free = {b: [*t_back, t_x2, P.last(), V.last(), S.last()] for b in range(8)}

        top[0] = base
        o_n = al(2048)
        XN = v1(o_n, 2048).rearrange("p (t n) -> p t n", t=2)
        o_n2 = al(2048)
        XS = v1(o_n2, 2048).rearrange("p (t n) -> p t n", t=2)
        o_h = al(2048)
        HT = v1(o_h, 2048).rearrange("p (k t) -> p k t", k=8)
        o_f = al(NFF * 256)
        FT = v1(o_f, NFF * 256).rearrange("p (k t) -> p k t", k=NFF)
        av = v1(o_f, 1024).rearrange("p (t n) -> p t n", t=2)
        UP = 15 + 256 + 15
        uT = v1(o_f + 1024, 4 * UP).rearrange("p (c n) -> p c n", c=4)
        CS = v1(o_f + 2200, 512)
        FH = v1(o_f + 2712, 256)
        SGm = v1(o_f + 2968, 1024).rearrange("p (c n) -> p c n", c=4)
        CV = v1(o_f + 3992, 1024).rearrange("p (c n) -> p c n", c=4)
        o_y = al(2048)
        YT = v1(o_y, 2048).rearrange("p (k t) -> p k t", k=8)
        o_cw2 = al(124 + 16)
        cw2 = v1(o_cw2, 124).rearrange("p (c w) -> p c w", c=4)
        cb2 = v1(o_cw2 + 124, 4)
        lg2 = v1(o_cw2 + 128, 4)
        lb2 = v1(o_cw2 + 132, 4)
        o_cwr = al(512 + 128)
        cwrow = v1(o_cwr, 512, 0, 31)
        vrow = v1(o_cwr + 512, 128, 0, 12)
        t_cwr = load(cwrow, I["conv_w_2"][0], *free[0])
        t_vr = [load(v1(o_cwr + 512, 128, 4 * j, 4 * j + 4), I[n][0].rearrange("(c p) -> c p", p=128), *free[0])
                for j, n in enumerate(["conv_b_2", "conv_ln_g_2", "conv_ln_b_2"])]
        assert top[0] <= AW

        for c in range(4):
            t = tr(PS[:, 7, c * 31:(c + 1) * 31], cwrow[:, c * 128:(c + 1) * 128], CT(C_IE + 128, 31, 0, 31),
                   t_cwr, *free[7])
        t = tr(PS[:, 7, 124:136], vrow, CT(C_IE + 128, 12, 0, 12), *t_vr, sig=True)
        t_cw2 = vcopy(v1(o_cw2, 136), PS[:, 7, 0:136], t, *free[7])
        free[7] = [t_cw2]
        t_up = V.op(lambda e: e.memset(v1(o_f + 1024, 4 * UP), 0.0), *free[0])

        def gk(name):
            return lambda k: gcol[:, k, RID[name]:RID[name] + 1]

        def norm_T(name, t_x, banks=(0, 1, 2, 3)):
            t = rms_rows(XN, XS, t_x, *free[0])
            tt = to_T(lambda i, k: XN[:, i, k * 128:(k + 1) * 128], HT, list(banks), t,
                      [x for b in banks for x in free[b]], scale=gk(name))
            for b in banks:
                free[b] = list(tt)
            return tt

        t_h = norm_T("mix0", t_x2)
        ups = [rows_item(I["w_in_ab_2"][0], kk * 256, 2, 0, 1024) for kk in range(4)]
        for k in range(8):
            u, tk, n = ups[k // 2]
            for i in range(2):
                t = mm(PS[:, 4 + i, :], HT[:, k, i * 128:(i + 1) * 128], u[:, k % 2, 0:512], k == 0, k == 7,
                       tk, *t_h, *free[4 + i], sig=(k == 7))
        ta = [vcopy(av[:, 0, :], PS[:, 4, :], t, *free[4]), act(av[:, 1, :], PS[:, 5, :], ACT.Copy, t, *free[5])]
        for c in range(4):
            for k in range(8):
                u, tk, n = ups[k // 2]
                t = mm(PS[:, c // 2, (c % 2) * 256:(c % 2) * 256 + 256], u[:, k % 2, 512 + c * 128:640 + c * 128],
                       HT[:, k, :], k == 0, k == 7, tk, *free[c // 2], sig=(k == 7))
        t_vT = t
        release(ups[3][2] + 1)
        gps = [rows_item(I["w_in_ab_2"][0], kk * 512, 4, 1024, 512) for kk in range(2)]
        for c in range(4):
            for k in range(8):
                u, tk, n = gps[k // 4]
                t = mm(PS[:, 2 + c // 2, (c % 2) * 256:(c % 2) * 256 + 256], u[:, k % 4, c * 128:(c + 1) * 128],
                       HT[:, k, :], k == 0, k == 7, tk, *free[2 + c // 2], sig=(k == 7))
        release(gps[1][2] + 1)
        t = act(SGm, PS[:, 2:4, :].rearrange("p b (c n) -> p (b c) n", c=2), ACT.Sigmoid, t, *free[0])
        t_u = tt_(uT[:, :, 15:271], PS[:, 0:2, :].rearrange("p b (c n) -> p (b c) n", c=2), SGm, ALU.mult,
                  t, t_vT, t_up)
        for b in range(4):
            free[b] = [t_u]

        dft, t_dft, n_dft = item(I["dft"], lambda u: u[:, 0:1280])
        fm, t_fm, n_fm = item(I["fnet_map_2"][0].rearrange("h d e -> d h e"),
                              lambda u: u[:, 0:512].rearrange("p (h e) -> p h e", h=4))
        t_yf = []
        prevs = list(free[0])
        for h in range(4):
            for i in range(2):
                t = mm(PS[:, 6, :], av[:, i, h * 128:(h + 1) * 128], dft[:, i * 512:(i + 1) * 512], i == 0, i == 1,
                       t_dft, *ta, *free[6], sig=(i == 1))
            t = act(CS, PS[:, 6, :], ACT.Copy, t, *prevs)
            free[6] = [t]
            mm(PS[:, 7, 0:256], dft[:, 1024:1152], CS[:, 0:256], True, False, t, *free[7])
            t = mm(PS[:, 7, 0:256], dft[:, 1152:1280], CS[:, 256:512], False, True, sig=True)
            prevs = [t]
            t = act(FH, PS[:, 7, 0:256], ACT.Copy, t)
            free[7] = [t]
            t = mm(PS[:, 5, 0:256], fm[:, h, :], FH, True, True, t, t_fm, *ta, *free[5], sig=True)
            prevs.append(t)
            t = act(YT[:, h, :], PS[:, 5, 0:256], ACT.Copy, t)
            free[5] = [t]
            t_yf.append(t)
        release(n_fm + 1)

        for c in range(4):
            t = ts(CV[:, c, :], uT[:, c, 0:256], cw2[:, c, 0:1], cb2[:, c:c + 1], ALU.mult, ALU.add, t_u, t_cw2)
        tk4 = [t] * 4
        for w in range(1, 31):
            for c in range(4):
                tk4[c] = stt(CV[:, c, :], uT[:, c, w:w + 256], cw2[:, c, w:w + 1], CV[:, c, :], ALU.mult, ALU.add,
                             tk4[c])
        c2 = CV.rearrange("p (b c) n -> p b (c n)", b=2)
        s2 = SGm.rearrange("p (b c) n -> p b (c n)", b=2)
        t = tk4[3]
        for b in range(2):
            t1 = mm(PS[:, b, :], ones, c2[:, b, :], True, True, t, *free[b], sig=True)
        t = stt(c2, PS[:, 0:2, :], -1.0 / 128, c2, ALU.mult, ALU.add, t1)
        t = act(s2, c2, ACT.Square, t)
        for b in range(2):
            t1 = mm(PS[:, 2 + b, :], ones, s2[:, b, :], True, True, t, *free[2 + b], sig=True)
        t = ts(s2, PS[:, 2:4, :], 1.0 / 128, 1e-5, ALU.mult, ALU.add, t1)
        t = act(s2, s2, ACT.Sqrt, t)
        t = recip(s2, s2, t)
        t = tt_(c2, c2, s2, ALU.mult, t)
        for c in range(4):
            t = ts(CV[:, c, :], CV[:, c, :], lg2[:, c:c + 1], lb2[:, c:c + 1], ALU.mult, ALU.add, t)
        t = act(SGm, CV, ACT.Sigmoid, t)
        t_yc = tt_(YT[:, 4:8, :], CV, SGm, ALU.mult, t, *free[0])
        for b in range(4):
            free[b] = [t_yc]
        t_x3 = out_proj(I["w_out_ab_2"][0], YT, [t_yc, *t_yf], None, [t_yc])
        for b in range(4):
            free[b] = [t_x3]
        t_ffree = [t_x3, t_yc, *t_yf]

        def ffn(l, t_x, name, t_free):
            t_h = norm_T(name, t_x, (4, 5, 6, 7))
            SGF = XS.rearrange("p t n -> p (t n)")
            hb = [XN.rearrange("p t n -> p (t n)")]
            wg, wu, wd = I["ffn_w_gate_2"][l], I["ffn_w_up_2"][l], I["ffn_w_down_2"][l]
            tf = []
            for j in range(NFF // 2):
                ug = rows_item(wg, 0, 8, j * 256, 256)
                uu = rows_item(wu, 0, 8, j * 256, 256)
                bs = [(0, 1), (2, 3)][j % 2]
                for m in range(2):
                    for (u, tk, n), b in ((ug, bs[0]), (uu, bs[1])):
                        for k in range(8):
                            t = mm(PS[:, b, m * 256:(m + 1) * 256], u[:, k, m * 128:(m + 1) * 128], HT[:, k, :],
                                   k == 0, k == 7, tk, *t_h, *free[b], sig=(k == 7))
                release(uu[2] + 1)
                sg = SGF[:, (j % 2) * 512:(j % 2) * 512 + 512]
                t1 = act(sg, PS[:, bs[0], :], ACT.Sigmoid, t, *(tf[-2:-1]))
                t1 = tt_(sg, sg, PS[:, bs[0], :], ALU.mult, t1)
                t1 = tt_(FT[:, 2 * j:2 * j + 2, :].rearrange("p c n -> p (c n)"), sg, PS[:, bs[1], :], ALU.mult, t1,
                         *t_free)
                tf.append(t1)
                free[bs[0]] = free[bs[1]] = [t1]
            for kk in range(NFF // 2):
                u, tk, n = rows_item(wd, kk * 256, 2, 0, 1024)
                for c in range(2):
                    k = 2 * kk + c
                    for i in range(2):
                        for ns in range(2):
                            b = 4 + 2 * i + ns
                            t = mm(PS[:, b, :], FT[:, k, i * 128:(i + 1) * 128], u[:, c, ns * 512:(ns + 1) * 512],
                                   k == 0, k == NFF - 1, tk, tf[k // 2], *free[b], sig=(k == NFF - 1))
                release(n + 1)
            for i in range(2):
                for ns in range(2):
                    xs = X[:, i, ns * 512:(ns + 1) * 512]
                    t2 = tt_(xs, xs, PS[:, 4 + 2 * i + ns, :], ALU.add, t)
            for b in range(8):
                free[b] = [t2]
            return t2

        t_x4 = ffn(0, t_x3, "ffn0", t_ffree)

        t = rms_rows(XN, XS, t_x4)
        pt, t_pt, n_pt = item(I["pool"], lambda u: u)
        pm, t_pm, n_pm = item(I["pool_map_2"][0].rearrange("g (c p) e -> p (g c) e", p=128),
                              lambda u: u.rearrange("p (g e) -> p g e", g=8))
        tp = []
        for k in range(8):
            g = k // 2
            b = k % 4
            for i in range(2):
                t1 = mm(PS[:, b, 0:256], XN[:, i, k * 128:(k + 1) * 128], pt[:, (g * 2 + i) * 256:(g * 2 + i + 1) * 256],
                        i == 0, i == 1, t, t_pt, *free[b], sig=(i == 1))
            sc_ = gk("mix1")(k)
            if k % 2:
                tk = act(HT[:, k, :], PS[:, b, 0:256], ACT.Copy, t1, scale=sc_)
            else:
                tk = ts(HT[:, k, :], PS[:, b, 0:256], sc_, None, ALU.mult, None, t1)
            free[b] = [tk]
            tp.append(tk)
        SC = XS.rearrange("p t n -> p (t n)")
        tsb = []
        for hf in range(2):
            t = spread(4 + hf, NROW, 0, RID["pool_scale"], A[0:NROW, o_rows + hf * 512:o_rows + hf * 512 + 512], *free[4])
            tsb.append(act(SC[:, hf * 512:(hf + 1) * 512], PS[:, 4 + hf, :], ACT.Copy, t))
        for b in (4, 5):
            free[b] = list(tsb)
        for i in range(2):
            for g in range(4):
                b = 4 + 2 * i + g // 2
                for c in range(2):
                    t = mm(PS[:, b, (g % 2) * 256:(g % 2) * 256 + 256], HT[:, 2 * g + c, i * 128:(i + 1) * 128],
                           pm[:, 2 * g + c, :], c == 0, c == 1, t_pm, *tp, *free[b], *tsb, sig=(c == 1))
        release(n_pm + 1)
        for i in range(2):
            for ns in range(2):
                tmp = SC[:, 1024:1536]
                t1 = tt_(tmp, PS[:, 4 + 2 * i + ns, :], SC[:, ns * 512:(ns + 1) * 512], ALU.mult, t, *tsb, V.last())
                xs = X[:, i, ns * 512:(ns + 1) * 512]
                t_x5 = tt_(xs, xs, tmp, ALU.add, t1)
        for b in range(8):
            free[b] = [t_x5, *tp]
        t_x6 = ffn(1, t_x5, "ffn1", [t_x5])

        t = rms_rows(XN, XS, t_x6)
        for hf in range(2):
            t1 = spread(hf, NROW, 0, RID["final"], A[0:NROW, o_rows + hf * 512:o_rows + hf * 512 + 512], *free[0])
            for i in range(2):
                xs = XN[:, i, hf * 512:(hf + 1) * 512]
                t_out = tt_(xs, xs, PS[:, hf, :], ALU.mult, t1, t)

        s_out = sem("s_out")
        block = ctx.enter_context(nc.Block())

        @block.sync
        def _(e):
            for n, (dst, src, s) in enumerate(stream):
                if n >= NRING:
                    e.wait_ge(*freed[n - NRING])
                    e.wait_ge(s_slot[s], 16 * (n // NRING))
                e.dma_start(dst, src).then_inc(s_slot[s], 16)
            e.wait_ge(*t_out)
            e.dma_start(out.rearrange("a (t p) d -> p (a t) d", p=128), XN).then_inc(s_out, 16)
            e.wait_ge(s_out, 16)

        @block.gpsimd
        def _(e):
            for dst, src, s, after in small:
                if after:
                    for q, v in after:
                        e.wait_ge(q, v)
                    e.dma_start(dst, src).then_inc(s, 16)

        @block.scalar
        def _(e):
            for dst, src, s, after in small:
                if not after:
                    e.dma_start(dst, src).then_inc(s, 16)
            S.play(e)

        @block.vector
        def _(e):
            V.play(e)

        @block.tensor
        def _(e):
            P.play(e)


_INS = ["x", "c", "norm1_g", "w_ada", "b_ada", "w_in", "conv_w", "sb_q_g", "sb_k_g", "fox_q_g", "fox_k_g", "fox_f_b",
        "out_norm_g", "w_out", "norm2_g", "router_w", "router_b", "w_mlp1", "b_mlp1", "w_mlp2", "b_mlp2",
        "norm_mix_g_2", "norm_ffn_g_2", "w_in_ab_2", "fnet_map_2", "conv_w_2", "conv_b_2", "conv_ln_g_2",
        "conv_ln_b_2", "w_out_ab_2", "pool_map_2", "pool_scale_2", "ffn_w_gate_2", "ffn_w_up_2", "ffn_w_down_2",
        "final_g_2"]


def kernel(**inputs):
    import concourse.bacc as _bacc
    from concourse.bass_utils import run_bass_kernel_spmd as _run

    nc = _bacc.Bacc("TRN2", target_bir_lowering=False, num_devices=1)
    arrays, aps = {}, {}
    for name in _INS:
        a = np.ascontiguousarray(inputs[name])
        arrays[f"in_{name}"] = a
        aps[name] = nc.dram_tensor(f"in_{name}", a.shape, mybir.dt.from_np(a.dtype), kind="ExternalInput").ap()
    for name, a in (("const", constants()), ("dft", dft_tables()), ("pool", pool_tables())):
        arrays[f"in_{name}"] = a
        aps[name] = nc.dram_tensor(f"in_{name}", a.shape, mybir.dt.from_np(a.dtype), kind="ExternalInput").ap()
    out = nc.dram_tensor("out_0", (1, 256, 1024), F32, kind="ExternalOutput").ap()
    build(nc, aps, out)
    r = _run(nc, [arrays], core_ids=[0])
    return r.results[0]["out_0"]
```

```python
from contextlib import ExitStack

import numpy as np

import concourse.bass as bass
from concourse import mybir

F32 = mybir.dt.float32
F32R = mybir.dt.float32r
I32 = mybir.dt.int32
ALU = mybir.AluOpType
ACT = mybir.ActivationFunctionType
AX = mybir.AxisListType.X

NRING = 14
UNIT = 2048
NEXP = 32
CAP = 64
NFF = 22
BIG = 1.0e30

C_IE, C_T1, C_T2, C_MS, C_CM, C_ONE, C_IOTA, C_END = 0, 384, 512, 640, 768, 1152, 1280, 1408

ROWS = ["norm1_g", "norm2_g", "out_norm_g", "mix0", "mix1", "ffn0", "ffn1", "pool_scale", "final"]
RID = {n: i for i, n in enumerate(ROWS)}

CB, CC, CU, SQ, SK, SV, FQ, FK, FV, FL = 0, 256, 512, 768, 1152, 1536, 1920, 2304, 2688, 3072


def constants():
    p = np.arange(128)[:, None]
    c = np.arange(128)[None, :]
    t = np.zeros((128, C_END), np.float32)
    t[:, C_IE:C_IE + 384] = (np.arange(384)[None, :] == p + 128)
    t[:, C_T1:C_T1 + 128] = (p <= c)
    t[:, C_T2:C_T2 + 128] = (p > c)
    t[:, C_MS:C_MS + 128] = (p < c)
    causal = np.where(c <= p, 0.0, -BIG)
    t[:, C_CM:C_CM + 128] = causal
    t[:, C_CM + 256:C_CM + 384] = causal
    t[:, C_ONE:C_ONE + 128] = 1.0
    t[:, C_IOTA:C_IOTA + 128] = c % CAP + 1
    return t


def dft_tables():
    def cs(n, scale):
        k = (np.arange(n)[:, None] * np.arange(n)[None, :]) % n
        a = 2.0 * np.pi * k / n
        return np.cos(a) * scale, np.sin(a) * scale
    c2, s2 = cs(256, 1.0 / 16.0)
    c1, s1 = cs(128, 128.0 ** -0.5)
    out = np.zeros((128, 1280), np.float32)
    for b in range(2):
        out[:, b * 512:b * 512 + 256] = c2[b * 128:(b + 1) * 128]
        out[:, b * 512 + 256:b * 512 + 512] = s2[b * 128:(b + 1) * 128]
    out[:, 1024:1152] = c1
    out[:, 1152:1280] = -s1
    return out


def pool_tables():
    out = np.zeros((128, 2048), np.float32)
    pos = np.arange(256)
    for g, w in enumerate((2, 4, 8, 16)):
        lo = np.clip(pos - w // 2, 0, 256)
        hi = np.clip(pos - w // 2 + w, 0, 256)
        m = np.zeros((256, 256))
        for t in range(256):
            m[lo[t]:hi[t], t] = 1.0 / (hi[t] - lo[t])
        m -= np.eye(256)
        for b in range(2):
            out[:, (g * 2 + b) * 256:(g * 2 + b + 1) * 256] = m[b * 128:(b + 1) * 128]
    return out


class Queue:

    def __init__(self, sem):
        self.sem, self.n, self.items, self.seen, self.open = sem, 0, [], {}, []
        self.loaded = None

    def op(self, fn, *after, sig=True):
        waits = []
        for sem, val in after:
            if self.seen.get(id(sem), 0) < val:
                waits.append((sem, val))
                self.seen[id(sem)] = val
        self.items.append(("op", waits, fn, sig))
        if sig:
            self.n += 1
        return (self.sem, self.n)

    def mark(self):
        if self.items[-1][0] == "op" and self.items[-1][2] is not None and not self.items[-1][3]:
            self.items[-1] = self.items[-1][:3] + (True,)
            self.n += 1
        return (self.sem, self.n)

    def last(self):
        return (self.sem, self.n)

    def begin(self, count_ap, limit, ready):
        self.op(None, ready, sig=False)
        self.open.append((self.items, self.n, dict(self.seen), count_ap, limit))
        self.items = []

    def end(self):
        body = self.items
        self.items, n0, self.seen, ap, limit = self.open.pop()
        self.items.append(("if", ap, limit, body, n0, self.n - n0))

    def play(self, eng, items=None):
        for it in self.items if items is None else items:
            if it[0] == "op":
                for sem, val in it[1]:
                    eng.wait_ge(sem, val)
                if it[2] is not None:
                    ins = it[2](eng)
                    if it[3]:
                        ins.then_inc(self.sem, 1)
            else:
                _, ap, limit, body, n0, n = it
                if self.loaded is None or self.loaded[0] is not ap:
                    self.loaded = (ap, eng.value_load(ap, min_val=0, max_val=256))
                v = self.loaded[1]
                with eng.If(v > limit):
                    self.play(eng, body)
                with eng.Else():
                    if n:
                        eng.wait_ge(self.sem, n0)
                        eng.sem_inc(self.sem, n)


def build(nc, I, out):
    with ExitStack() as ctx:
        def sem(name):
            return ctx.enter_context(nc.semaphore(name))

        AW = 24536
        at_ring = -(-nc.sbuf_base // 32) * 32
        ring = ctx.enter_context(nc.sbuf_tensor("ring", [128, NRING * UNIT], F32))
        A = ctx.enter_context(nc.sbuf_tensor("arena", [128, AW], F32))
        at_arena = at_ring + NRING * UNIT * 4

        def rounded(name, at, n):
            return nc.alloc_sbuf_tensor_at(name, [128, n], F32R, offset=at)[:, :]
        PS = ctx.enter_context(nc.psum_tensor("ps", [128, 8, 512], F32))

        P = Queue(sem("s_pe"))
        V = Queue(sem("s_dve"))
        S = Queue(sem("s_act"))

        top = [0]

        def al(n):
            o = top[0]
            top[0] += n
            assert top[0] <= AW, top[0]
            return o

        def v1(o, n, p0=0, p1=128):
            return A[p0:p1, o:o + n]

        def mm(o, l, r, start, stop, *after, sig=False, skip=False):
            return P.op(lambda e: e.matmul(o, l, r, start=start, stop=stop, skip_group_check=skip), *after, sig=sig)

        def tr(o, i, n, *after, sig=False):
            return P.op(lambda e: e.transpose(o, i, n), *after, sig=sig)

        def ts(o, i, s1, s2, op0, op1, *after):
            if op1 is None:
                return V.op(lambda e: e.tensor_scalar(o, i, s1, None, op0), *after)
            return V.op(lambda e: e.tensor_scalar(o, i, s1, s2, op0, op1), *after)

        def tt_(o, a, b, op, *after):
            return V.op(lambda e: e.tensor_tensor(o, a, b, op), *after)

        def stt(o, a, s, b, op0, op1, *after):
            return V.op(lambda e: e.scalar_tensor_tensor(out=o, in0=a, scalar=s, in1=b, op0=op0, op1=op1), *after)

        def vcopy(o, i, *after):
            return V.op(lambda e: e.tensor_copy(o, i), *after)

        def red(o, i, op, *after):
            return V.op(lambda e: e.tensor_reduce(o, i, AX, op), *after)

        def recip(o, i, *after):
            return V.op(lambda e: e.reciprocal(o, i), *after)

        def act(o, i, f, *after, **kw):
            return S.op(lambda e: e.activation(o, i, f, **kw), *after)

        s_slot = [sem(f"s_slot{i}") for i in range(NRING)]
        stream = []
        freed = []
        held = {}
        turn = {"slots": list(range(NRING)), "at": 0}

        def item(src, view):
            n = len(stream)
            s = turn["slots"][turn["at"] % len(turn["slots"])]
            turn["at"] += 1
            before = held.setdefault(s, [])
            stream.append((view(ring[:, s * UNIT:(s + 1) * UNIT]), src, s, before[-1] if before else None))
            before.append(n)
            return view(ring[:, s * UNIT:(s + 1) * UNIT]), (s_slot[s], 16 * len(before)), n

        def release(n, t=None):
            t = t or P.mark()
            while len(freed) < n:
                freed.append(t)

        def rows_item(w, r0, nk, c0, ncol):
            src = w[r0:r0 + 128 * nk, c0:c0 + ncol].rearrange("(c p) n -> p c n", p=128)
            return item(src, lambda u: u[:, 0:nk * ncol].rearrange("p (c n) -> p c n", c=nk))

        small = []

        def load(dst, src, *after):
            s = sem(f"s_l{len(small)}")
            small.append((dst, src, s, after))
            return (s, 16)

        o_c = al(C_END)
        CT = lambda a, n=128, p0=0, p1=128: v1(o_c + a, n, p0, p1)
        ident = CT(C_IE + 128)
        ones = CT(C_ONE)

        def sel(p0, k, r, m):
            return A[p0:p0 + k, o_c + C_IE + 128 + p0 + r:o_c + C_IE + 129 + p0 + r].to_broadcast([k, m])

        def shifted(s, prev):
            a = C_IE + (256 if prev else 128) - s
            return CT(a)

        o_x = al(2048)
        X = v1(o_x, 2048).rearrange("p (t d) -> p t d", t=2)
        o_rows = al(1024)
        NROW = len(ROWS)
        rows = v1(o_rows, 1024, 0, NROW)
        o_gc = al(8 * NROW)
        gcol = v1(o_gc, 8 * NROW).rearrange("p (k r) -> p k r", k=8)
        o_sm = al(400)
        sm_top = [o_sm]

        def sm(n, p0=0, p1=128):
            o = sm_top[0]
            sm_top[0] += n
            assert sm_top[0] <= o_sm + 400
            return v1(o, n, p0, p1)

        o_c8 = al(128)
        base = top[0]

        c8 = v1(o_c8, 128, 0, 8)
        t_c = load(c8, I["c"].rearrange("a (k p) -> (a k) p", p=128))
        t_const = load(v1(o_c, C_END), I["const"])
        t_x = load(X, I["x"].rearrange("a (t p) d -> p (a t) d", p=128))
        t_rows = [load(v1(o_rows, 1024, i, i + 1), a) for i, a in enumerate([
            I["norm1_g"][0:1, :], I["norm2_g"][0:1, :], I["out_norm_g"][0:1, :],
            I["norm_mix_g_2"][0:1, :], I["norm_mix_g_2"][1:2, :],
            I["norm_ffn_g_2"][0:1, :], I["norm_ffn_g_2"][1:2, :],
            I["pool_scale_2"][0:1, :], I["final_g_2"].rearrange("(a n) -> a n", a=1)])]

        o_P = al(6144)
        PJ = v1(o_P, 6144).rearrange("p (t n) -> p t n", t=2)
        o_hT = al(2304)
        hT = v1(o_hT, 2048).rearrange("p (k t) -> p k t", k=8)
        o_qk = al(3072)
        QKT = v1(o_qk, 3072).rearrange("p (c t) -> p c t", c=12)
        o_mr = al(1536)
        modr = v1(o_mr, 1536).rearrange("p (b n) -> p b n", b=3)
        o_ws = al(4608)
        WS = [v1(o_ws + 1152 * i, 1152).rearrange("p (h n) -> p h n", h=3) for i in range(4)]
        Y = v1(o_ws, 2048).rearrange("p (t n) -> p t n", t=2)
        T2k = v1(o_ws + 2048, 2048).rearrange("p (t n) -> p t n", t=2)
        o_cT = al(256)
        cTp = v1(o_cT, 256).rearrange("p (k m) -> p k m", k=8)
        o_wf = al(48)
        wf = v1(o_wf, 48).rearrange("p (k n) -> p k n", k=8)
        o_small1 = al(256)
        fbrow = v1(o_small1, 6, 0, 1)
        rbrow = sm(32, 0, 1)
        o_cw = al(256)
        cwr = v1(o_cw, 256, 0, 3)
        gq = [v1(o_small1 + 8 + i, 1) for i in range(4)]

        t_ab = []
        for q in range(4):
            t_ab.append(load(modr[32 * q:32 * q + 1, :, :],
                             I["b_ada"].rearrange("a (b q n) -> a q b n", b=3, q=4)[:, q, :, :],
                             None))
        t_wf = load(wf, I["w_in"][0, :, FL:FL + 6].rearrange("(k p) n -> p k n", p=128))
        t_fb = load(fbrow, I["fox_f_b"])
        t_rb = load(rbrow, I["router_b"])
        t_cw = load(cwr, I["conv_w"][0, :, :])
        t_gq = []
        o_cwr = al(512)
        cwrow = v1(o_cwr, 512, 0, 31)
        vrow = v1(o_c8, 128, 32, 44)
        t_cwr = load(cwrow, I["conv_w_2"][0])
        t_vr = [load(v1(o_c8, 128, 32 + 4 * j, 36 + 4 * j), I[n][0].rearrange("(c p) -> c p", p=128))
                for j, n in enumerate(["conv_b_2", "conv_ln_g_2", "conv_ln_b_2"])]
        for i, n in enumerate(["sb_q_g", "sb_k_g", "fox_q_g", "fox_k_g"]):
            for hf in range(2):
                t_gq.append(load(A[64 * hf:64 * hf + 64, o_small1 + 8 + i:o_small1 + 9 + i],
                                 I[n].rearrange("a d -> d a")))

        t_z0 = V.op(lambda e: e.memset(v1(o_mr, 1536), 0.0))
        t_z1 = V.op(lambda e: e.memset(v1(o_cT, 256), 0.0))
        for i, (d, s, q, a) in enumerate(small):
            if a == (None,):
                small[i] = (d, s, q, (t_z0,))

        sc = sm(128, 0, 8)
        t = act(sc, c8, ACT.Sigmoid, t_c)
        t = tt_(sc, sc, c8, ALU.mult, t)
        t = tr(PS[:, 0, 0:8], sc, CT(C_IE + 128, 8, 0, 8), t, t_const, sig=True)
        t_cT = vcopy(cTp[:, :, 0], PS[:, 0, 0:8], t, t_z1)
        rs = sm(8)

        def rms_rows(dst, sq, *after):
            ss, rr = rs[:, 0:2], rs[:, 2:4]
            for i in range(2):
                t = act(sq[:, i, :], X[:, i, :], ACT.Square, *after, accum_out=ss[:, i:i + 1])
            t = ts(rr, ss, 1.0 / 1024, 1e-6, ALU.mult, ALU.add, t)
            t = act(rr, rr, ACT.Sqrt, t)
            t = recip(rr, rr, t)
            for i in range(2):
                t2 = ts(dst[:, i, :], X[:, i, :], rr[:, i:i + 1], None, ALU.mult, None, t)
            return t2

        def to_T(src, dst, banks, t_src, t_bank, scale=None, bias=None, t_sb=()):
            toks = []
            for m in range(4):
                b = banks[m % len(banks)]
                for k in (2 * m, 2 * m + 1):
                    for i in range(2):
                        w = [t_src] + t_bank
                        if m >= len(banks):
                            w.append(toks[m - len(banks)])
                        o = (k % 2) * 256 + i * 128
                        t = tr(PS[:, b, o:o + 128], src(i, k), ident, *w, sig=(k % 2 == 1 and i == 1))
                for k in ((2 * m,) if scale is None else (2 * m, 2 * m + 1)):
                    o = (k % 2) * 256
                    if scale is None:
                        po = dst[:, k:k + 2, :]
                        pin = PS[:, b, :].rearrange("p (c n) -> p c n", c=2)
                        tk = act(po, pin, ACT.Copy, t) if m % 2 else vcopy(po, pin, t)
                        continue
                    pin, po = PS[:, b, o:o + 256], dst[:, k, :]
                    if bias is None:
                        s = scale(k)
                        if m % 2:
                            tk = act(po, pin, ACT.Copy, t, *t_sb, scale=s)
                        else:
                            tk = ts(po, pin, s, None, ALU.mult, None, t, *t_sb)
                    else:
                        s, b_ = scale(k), bias(k)
                        if m % 2:
                            tk = act(po, pin, ACT.Identity, t, *t_sb, scale=s, bias=b_)
                        else:
                            tk = ts(po, pin, s, b_, ALU.mult, ALU.add, t, *t_sb)
                toks.append(tk)
            return toks[-2:]

        xn = Y
        t_xn = rms_rows(xn, T2k, t_x)

        def ada_block(b, bank, t_bank):
            us = [rows_item(I["w_ada"][0], k * 128, 1, b * 2048, 2048) for k in range(8)]

            def step(k):
                u, tk, n = us[k]
                for q in range(4):
                    t = mm(PS[32 * q:32 * q + 32, bank, :], cTp[:, k, :], u[:, 0, q * 512:(q + 1) * 512],
                           k == 0, k == 7, tk, t_cT, *t_bank, sig=(q == 3))
                release(n + 1)
                return t

            def fin(t):
                return tt_(modr[:, b, :], PS[:, bank, :], modr[:, b, :], ALU.add, t, *t_ab)
            return step, fin

        step, fin = ada_block(0, 2, [])
        for k in range(8):
            t_ada = step(k)
        for k in range(8):
            t = tr(PS[:, 1, k * NROW:(k + 1) * NROW], A[0:NROW, o_rows + k * 128:o_rows + (k + 1) * 128],
                   CT(C_IE + 128, NROW, 0, NROW), *t_rows, sig=(k == 7))
        t_gcol = vcopy(gcol.rearrange("p k r -> p (k r)"), PS[:, 1, 0:8 * NROW], t)

        t_m0 = fin(t_ada)
        for cc in range(4):
            t = tr(PS[:, 3, cc * 128:(cc + 1) * 128], modr[:, 0, cc * 128:(cc + 1) * 128], ident, t_m0, sig=(cc == 3))
        mview = PS[:, 3, :].rearrange("p (c q z) -> p q c z", c=4, q=4)
        a1 = sm(8)
        s1 = sm(8)
        t_a1 = stt(a1.rearrange("p (q c) -> p q c", q=2), mview[:, 2:4, :, 0], 1.0,
                   gcol[:, :, RID["norm1_g"]].rearrange("p (q c) -> p q c", q=2), ALU.add, ALU.mult, t, t_gcol)
        t_s1 = vcopy(s1.rearrange("p (q c) -> p q c", q=2), mview[:, 0:2, :, 0], t)
        t_hT = to_T(lambda i, k: xn[:, i, k * 128:(k + 1) * 128], hT, [4, 5, 6, 7], t_xn, [],
                    scale=lambda k: a1[:, k:k + 1], bias=lambda k: s1[:, k:k + 1], t_sb=[t_a1, t_s1])

        free = {b: [t_a1, t_s1, t_cT, t_gcol, *t_hT] for b in range(8)}
        cwb = v1(o_qk, 768)
        for w in range(3):
            t = mm(PS[:, 4 + w // 2, (w % 2) * 256:(w % 2) * 256 + 256], sel(0, 3, w, 128), cwr, True, True, t_cw,
                   *free[4], sig=True)
            if w:
                t_cwb = vcopy(cwb[:, 512 * (w - 1):512 * (w - 1) + 512 // w], PS[:, 3 + w, 0:512 // w], t)
                free[3 + w] = [t_cwb]

        ev = {}

        def project(j, bk):
            for kk in range(4):
                u, tk, n = rows_item(I["w_in"][0], kk * 256, 2, j * 1024, 1024)
                for c in range(2):
                    k = 2 * kk + c
                    for i in range(2):
                        for ns in range(2):
                            b = bk + 2 * i + ns
                            t = mm(PS[:, b, :], hT[:, k, i * 128:(i + 1) * 128],
                                   u[:, c, ns * 512:(ns + 1) * 512], k == 0, k == 7, tk, *free[b], sig=(k == 7))
                release(n + 1)
            return t

        def land(j, bk, t):
            ev[j] = []
            for i in range(2):
                for ns in range(2):
                    b = bk + 2 * i + ns
                    d = PJ[:, i, j * 1024 + ns * 512:j * 1024 + (ns + 1) * 512]
                    ev[j].append(act(d, PS[:, b, :], ACT.Copy, t) if ns else vcopy(d, PS[:, b, :], t))
                    free[b] = ev[j][-1:]

        rq = v1(o_small1 + 16, 48)
        t_g8 = [ts(gq[i], gq[i], 0.125, None, ALU.mult, None, *t_gq) for i in (0, 2)]

        def head_norm(kind, c0, o_sq, *after):
            sqs = v1(o_sq, 1536).rearrange("p (t n) -> p t n", t=2)
            seg = PJ[:, :, c0:c0 + 768]
            t = act(sqs, seg, ACT.Square, *after)
            o_r = o_small1 + 16 + kind * 24
            r = v1(o_r, 24)
            t = red(r, v1(o_sq, 1536).rearrange("p (h d) -> p h d", d=64), ALU.add, t)
            t = ts(r, r, 1.0 / 64, 1e-6, ALU.mult, ALU.add, t)
            t = act(r, r, ACT.Sqrt, t)
            t = recip(r, r, t)
            for i in range(2):
                sg = seg[:, i, :].rearrange("p (h d) -> p h d", d=64)
                ri = v1(o_r + 12 * i, 12).rearrange("p (h o) -> p h o", o=1).to_broadcast([128, 12, 64])
                t2 = tt_(sg, sg, ri, ALU.mult, t)
            return t2

        t_qk = {}

        def head_turn(kind, c0, b0, t_n):
            for m in range(3):
                b = b0 + m
                for c in (2 * m, 2 * m + 1):
                    for i in range(2):
                        o = (c % 2) * 256 + i * 128
                        t = tr(PS[:, b, o:o + 128], PJ[:, i, c0 + c * 128:c0 + (c + 1) * 128], ident, t_n, *free[b],
                               sig=(c % 2 == 1 and i == 1))
                for c in (2 * m, 2 * m + 1):
                    g = gq[2 * kind + (c >= 3)]
                    d, o = QKT[:, kind * 6 + c, :], (c % 2) * 256
                    if m % 2:
                        tk = act(d, PS[:, b, o:o + 256], ACT.Copy, t, *t_g8, *t_gq, t_v, t_vw, scale=g)
                    else:
                        tk = ts(d, PS[:, b, o:o + 256], g, None, ALU.mult, None, t, *t_g8, *t_gq, t_v, t_vw)
                t_qk.setdefault(kind, []).append(tk)
                free[b] = [tk]

        t = project(0, 0)
        land(0, 0, t)
        vcv = v1(o_ws, 512).rearrange("p (t n) -> p t n", t=2)
        vw = [v1(o_ws + 512 + 512 * i, 512).rearrange("p (t n) -> p t n", t=2) for i in range(3)]
        t_v = tt_(vcv, PJ[:, :, CC:CC + 256], PJ[:, :, CU:CU + 256], ALU.mult, *ev[0], *t_hT)
        for w in range(3):
            cb_ = cwb[:, w * 256:(w + 1) * 256].rearrange("p (o n) -> p o n", o=1).to_broadcast([128, 2, 256])
            t_vw = tt_(vw[w], vcv, cb_, ALU.mult, t_v, t_cwb)
        t = project(1, 4)
        land(1, 4, t)
        t_n0 = head_norm(0, SQ, o_ws + 2304, *ev[0], *ev[1], *t_hT)
        t = project(2, 0)
        for i in range(2):
            for k in range(8):
                mm(PS[:, 4, i * 8:i * 8 + 6], hT[:, k, i * 128:(i + 1) * 128], wf[:, k, :], k == 0, False, t_wf, *free[4])
            t_fl = mm(PS[:, 4, i * 8:i * 8 + 6], CT(C_ONE, 128, 0, 1), fbrow, False, True, t_fb, sig=True)
        land(2, 0, t)
        head_turn(0, SQ, 5, t_n0)
        t_n1 = head_norm(1, FQ, o_ws + 2304, *ev[1], *ev[2], t_n0)

        for i in range(2):
            o = PS[:, 0, i * 256:(i + 1) * 256]
            for w in range(3):
                last = w == 2
                t = mm(o, shifted(2 - w, False), vw[w][:, i, :], w == 0, last and i == 0, t_vw, *free[0])
            if i == 1:
                mm(o, shifted(2, True), vw[0][:, 0, :], False, False)
                t_cv = mm(o, shifted(1, True), vw[1][:, 0, :], False, True, sig=True)

        fz = PS[:, 4, 0:16].rearrange("p (t h) -> p t h", t=2)[:, :, 0:6]
        lf = sm(12).rearrange("p (t h) -> p t h", t=2)
        lg = sm(12).rearrange("p (t h) -> p t h", t=2)
        t = act(lg, fz, ACT.Abs, t_fl)
        t = act(lg, lg, ACT.Exp, t, scale=-1.0)
        t = act(lg, lg, ACT.Ln, t, bias=CT(C_ONE, 1))
        t_lf = stt(lf, fz, 0.0, lg, ALU.min, ALU.subtract, t)
        free[4] = [t_lf]

        ada = [ada_block(1, 4, [t_lf]), ada_block(2, 4, [t_lf])]
        ada_at = {"n": 0}
        t_mod = []

        def ada_more(n):
            for _ in range(n):
                k = ada_at["n"]
                if k == 16:
                    return
                ada_at["n"] += 1
                if k == 8:
                    P.op(None, t_mod[0], sig=False)
                t = ada[k // 8][0](k % 8)
                if k % 8 == 7:
                    t_mod.append(ada[k // 8][1](t))

        cum = sm(12).rearrange("p (t h) -> p t h", t=2)
        o_cumT = al(256)
        cumT = v1(o_cumT, 256, 0, 6)

        def running():
            mm(PS[:, 4, 16:22], CT(C_T1), lf[:, 0, :], True, True, t_lf)
            mm(PS[:, 4, 24:30], ones, lf[:, 0, :], True, False)
            t = mm(PS[:, 4, 24:30], CT(C_T1), lf[:, 1, :], False, True, sig=True)
            t_cum = vcopy(cum, PS[:, 4, 16:32].rearrange("p (t h) -> p t h", t=2)[:, :, 0:6], t)
            for i in range(2):
                t = tr(PS[0:6, 4, i * 128:(i + 1) * 128], cum[:, i, :], ident, t_cum, sig=(i == 1))
            t = ts(cumT, PS[0:6, 4, 0:256], -1.0, None, ALU.mult, None, t)
            P.op(None, t, sig=False)
            return t

        WC = [v1(o_hT + 1152 * i, 1152).rearrange("p (h n) -> p h n", h=3) for i in range(2)]
        MS2 = CT(C_MS).rearrange("p (a b n) -> p a b n", a=1, b=1).to_broadcast([128, 3, 2, 128])
        st = {}

        def diag(x):
            return x.rearrange("p h (b n) -> p h b n", b=3)[:, :, 0:3:2, :]

        def sb_z(g):
            for hh in range(3):
                h = 3 * g + hh
                c, o = h // 2, (h % 2) * 64
                kT, qT = QKT[o:o + 64, 3 + c, :], QKT[o:o + 64, c, :]
                mm(PS[:, 5 + hh, 0:256], kT[:, 0:128], qT, True, True, *free[5 + hh], *t_qk[0])
                t = mm(PS[:, 5 + hh, 256:384], kT[:, 128:256], qT[:, 128:256], True, True, sig=True)
            st["sz", g] = t

        def sb_a(g, L, LB, *after):
            Z = PS[:, 5:8, 0:384]
            t = act(L, Z, ACT.Abs, st["sz", g], *after)
            t = act(L, L, ACT.Exp, t, scale=-1.0)
            t = act(L, L, ACT.Ln, t, bias=CT(C_ONE, 1))
            t = stt(LB, Z, 0.0, L, ALU.min, ALU.subtract, t, *after)
            t = tt_(L, LB, Z, ALU.subtract, t)
            for b in (5, 6, 7):
                free[b] = [t]
            st["sa", g] = tt_(diag(L), diag(L), MS2, ALU.mult, t)

        def sb_r(g, L):
            for hh in range(3):
                b = 5 + hh
                mm(PS[:, b, 0:256], CT(C_T2), L[:, hh, 0:256], True, False, st["sa", g], *free[b])
                mm(PS[:, b, 128:256], ones, L[:, hh, 256:384], False, False)
                t = mm(PS[:, b, 256:384], CT(C_T2), L[:, hh, 256:384], False, True, sig=True)
            st["sr", g] = t

        def sb_b(g, L, LB):
            t = tt_(LB, LB, PS[:, 5:8, 0:384], ALU.add, st["sr", g])
            for b in (5, 6, 7):
                free[b] = [t]
            t = act(L, LB, ACT.Exp, t, st["sr", g])
            st["sb", g] = tt_(diag(L), diag(L), MS2, ALU.mult, t)

        def weigh(g, W, t_w, c_v):
            for hh in range(3):
                h = 3 * g + hh
                vv = [PJ[:, i, c_v + h * 64:c_v + (h + 1) * 64] for i in range(2)]
                oo = [PS[:, 0, i * 256 + hh * 64:i * 256 + (hh + 1) * 64] for i in range(2)]
                mm(oo[0], W[:, hh, 0:128], vv[0], True, True, t_w, *free[0])
                mm(oo[1], W[:, hh, 128:256], vv[0], True, False)
                t = mm(oo[1], W[:, hh, 256:384], vv[1], False, True, sig=True)
            return t

        def sb_o(g, L):
            t = weigh(g, L, st["sb", g], SV)
            t2 = vcopy(PJ[:, :, SQ + 192 * g:SQ + 192 * g + 192],
                       PS[:, 0, :].rearrange("p (t n) -> p t n", t=2)[:, :, 0:192], t)
            free[0] = [t2]
            st["so", g] = t2

        mxs = [v1(o_small1 + 64 + 16 * g, 6) for g in range(2)]
        sms = [v1(o_small1 + 72 + 16 * g, 6) for g in range(2)]

        def fx_z(g):
            for hh in range(3):
                h = 3 * g + hh
                b = 1 + hh
                c, o = h // 2, (h % 2) * 64
                kT, qT = QKT[o:o + 64, 9 + c, :], QKT[o:o + 64, 6 + c, :]
                mm(PS[:, b, 0:128], qT[:, 0:128], kT[:, 0:128], True, False, *free[b], *t_qk[1])
                mm(PS[:, b, 0:128], sel(0, 6, h, 128), cumT[:, 0:128], False, True, t_cumT)
                mm(PS[:, b, 128:384], qT[:, 128:256], kT, True, False)
                t = mm(PS[:, b, 128:384], sel(0, 6, h, 128), cumT[:, 0:256], False, True, sig=True)
            st["fz", g] = t

        def fx_a(g, E, *after):
            mx, sums, t = mxs[g], sms[g], st["fz", g]
            for hh in range(3):
                h = 3 * g + hh
                stt(E[:, hh, 0:128], PS[:, 1 + hh, 0:128], cum[:, 0, h:h + 1], CT(C_CM), ALU.add, ALU.add, t, *after)
                tl = stt(E[:, hh, 128:384], PS[:, 1 + hh, 128:384], cum[:, 1, h:h + 1], CT(C_CM + 128, 256),
                         ALU.add, ALU.add, t)
                free[1 + hh] = [tl]
            red(mx[:, 0:3], E[:, :, 0:128], ALU.max, tl)
            t = red(mx[:, 3:6], E[:, :, 128:384], ALU.max, tl)
            t = ts(mx, mx, -1.0, None, ALU.mult, None, t)
            for hh in range(3):
                act(E[:, hh, 0:128], E[:, hh, 0:128], ACT.Exp, t, bias=mx[:, hh:hh + 1],
                    accum_out=sums[:, hh:hh + 1])
                t2 = act(E[:, hh, 128:384], E[:, hh, 128:384], ACT.Exp, bias=mx[:, 3 + hh:4 + hh],
                         accum_out=sums[:, 3 + hh:4 + hh])
            st["fe", g] = t2
            st["fr", g] = recip(sums, sums, t2)

        def fx_t(g, E):
            for hh in range(3):
                for q in range(3):
                    t = tr(PS[:, 1 + hh, q * 128:(q + 1) * 128], E[:, hh, q * 128:(q + 1) * 128], ident,
                           st["fe", g], *free[1 + hh], sig=(q == 2))
            st["ft", g] = t

        def fx_b(g, ET, *after):
            t = act(ET, PS[:, 1:4, 0:384], ACT.Copy, st["ft", g], *after)
            for b in (1, 2, 3):
                free[b] = [t]
            st["fb", g] = t

        def fx_o(g, ET):
            t = weigh(g, ET, st["fb", g], FV)
            for i in range(2):
                rb = sms[g][:, 3 * i:3 * i + 3].rearrange("p (h o) -> p h o", o=1).to_broadcast([128, 3, 64])
                t2 = tt_(PJ[:, i, FQ + 192 * g:FQ + 192 * g + 192].rearrange("p (h d) -> p h d", d=64),
                         PS[:, 0, i * 256:i * 256 + 192].rearrange("p (h d) -> p h d", d=64), rb, ALU.mult, t,
                         st["fr", g])
            free[0] = [t2]
            st["fo", g] = t2

        sb_z(0)
        sb_a(0, WS[0], WS[1], t_cv, t_qk[0][-1])
        t_cumT = running()
        t_yc0 = tt_(PJ[:, :, CB:CB + 256], PS[:, 0, :].rearrange("p (t n) -> p t n", t=2), PJ[:, :, CB:CB + 256],
                    ALU.mult, t_cv)
        free[0] = [t_yc0]
        head_turn(1, FQ, 1, t_n1)
        fx_z(0)
        fx_a(0, WS[2], t_n1)
        sb_r(0, WS[0])
        sb_b(0, WS[0], WS[1])
        ada_more(3)
        fx_t(0, WS[2])
        fx_b(0, WS[3])
        sb_z(1)
        sb_a(1, WC[0], WC[1], t_fl)
        sb_o(0, WS[0])
        ada_more(2)
        fx_z(1)
        fx_a(1, WS[0], st["so", 0])
        fx_o(0, WS[3])
        sb_r(1, WC[0])
        sb_b(1, WC[0], WC[1])
        ada_more(3)
        fx_t(1, WS[0])
        fx_b(1, WS[1], st["sb", 0])
        ada_more(3)
        sb_o(1, WC[0])
        fx_o(1, WS[1])
        t_y = V.last()
        t_ws = [t_y, st["fb", 1], P.last()]
        t2 = t_y
        for b in range(8):
            free[b] = [*free[b], t_y]
        ada_more(16)

        gr = v1(o_small1 + 80, 32).rearrange("p (t g) -> p t g", t=2)
        segs = [(CB, 4, 0), (SQ, 6, 4), (FQ, 6, 10)]
        for c0, n, g0 in segs:
            t = act(Y[:, :, g0 * 64:(g0 + n) * 64], PJ[:, :, c0:c0 + n * 64], ACT.Square, t_y, *t_ws)
        t = red(gr.rearrange("p t g -> p (t g)"), v1(o_ws, 2048).rearrange("p (g d) -> p g d", d=64), ALU.add, t)
        t = ts(gr, gr, 1.0 / 64, 1e-6, ALU.mult, ALU.add, t)
        t = act(gr, gr, ACT.Sqrt, t)
        t = recip(gr, gr, t)
        for i in range(2):
            for c0, n, g0 in segs:
                rb = gr[:, i, g0:g0 + n].rearrange("p (g o) -> p g o", o=1).to_broadcast([128, n, 64])
                t2 = tt_(Y[:, i, g0 * 64:(g0 + n) * 64].rearrange("p (g d) -> p g d", d=64),
                         PJ[:, i, c0:c0 + n * 64].rearrange("p (g d) -> p g d", d=64), rb, ALU.mult, t)
        t_yT = to_T(lambda i, k: Y[:, i, k * 128:(k + 1) * 128], hT, [0, 1, 2, 3], t2, [t_y, t2],
                    scale=lambda k: gcol[:, k, RID["out_norm_g"]:RID["out_norm_g"] + 1])

        def spread(bank, k, p0, r, rhs, *after):
            return mm(PS[:, bank, :], sel(p0, k, r, 128), rhs, True, True, *after, sig=True)

        def mod_row(bank, v, half, *after):
            f = v * 1024 + half * 512
            b, q = f // 2048, (f % 2048) // 512
            return mm(PS[:, bank, :], sel_w(q), modr[:, b, :], True, True, *after, sig=True)

        def sel_w(q):
            return A[:, o_c + C_IE + 128 + 32 * q:o_c + C_IE + 129 + 32 * q].to_broadcast([128, 128])

        G1B = v1(o_P, 1024)
        A2B = v1(o_P + 1024, 1024)
        S2B = v1(o_P + 2048, 1024)
        TMP = v1(o_P + 3072, 1024)
        tg = []
        for hf in range(2):
            t = mod_row(4 + hf, 2, hf, *t_mod, t_y, t2, *free[4])
            tg.append(act(G1B[:, hf * 512:(hf + 1) * 512], PS[:, 4 + hf, :], ACT.Copy, t, t2))
        for hf in range(2):
            t = mod_row(6 + hf, 3, hf, *t_mod, *free[6])
            tg.append(act(S2B[:, hf * 512:(hf + 1) * 512], PS[:, 6 + hf, :], ACT.Copy, t))
        for hf in range(2):
            t = mod_row(4 + hf, 4, hf, *tg)
            tg.append(act(TMP[:, hf * 512:(hf + 1) * 512], PS[:, 4 + hf, :], ACT.Copy, t))
        t_a2 = []
        for hf in range(2):
            t = spread(6 + hf, NROW, 0, RID["norm2_g"], A[0:NROW, o_rows + hf * 512:o_rows + hf * 512 + 512], *tg)
            t_a2.append(stt(A2B[:, hf * 512:(hf + 1) * 512], TMP[:, hf * 512:(hf + 1) * 512], 1.0, PS[:, 6 + hf, :],
                            ALU.add, ALU.mult, t, *tg))

        def out_proj(w, lT, t_l, gate, t_bank, banks=(0, 1, 2, 3), tmp=None):
            for kk in range(4):
                u, tk, n = rows_item(w, kk * 256, 2, 0, 1024)
                for c in range(2):
                    k = 2 * kk + c
                    for i in range(2):
                        for ns in range(2):
                            t = mm(PS[:, banks[2 * i + ns], :], lT[:, k, i * 128:(i + 1) * 128],
                                   u[:, c, ns * 512:(ns + 1) * 512], k == 0, k == 7, tk, *t_l, *t_bank, sig=(k == 7))
                release(n + 1)
            for i in range(2):
                for ns in range(2):
                    xs = X[:, i, ns * 512:(ns + 1) * 512]
                    pb = PS[:, banks[2 * i + ns], :]
                    if gate is not None:
                        t = tt_(tmp[:, i, ns * 512:(ns + 1) * 512], pb, gate[:, ns * 512:(ns + 1) * 512], ALU.mult, t, *tg)
                        t = tt_(xs, xs, tmp[:, i, ns * 512:(ns + 1) * 512], ALU.add, t)
                    else:
                        t = tt_(xs, xs, pb, ALU.add, t)
            return t

        tw = t_vw
        t_x1 = out_proj(I["w_out"][0], hT, t_yT, G1B, list(t_yT), tmp=T2k)

        o_h2 = o_hT
        H2 = v1(o_h2, 2048).rearrange("p (t n) -> p t n", t=2)
        t = rms_rows(Y, T2k, t_x1)
        ab = A2B.rearrange("p (o n) -> p o n", o=1).to_broadcast([128, 2, 1024])
        sb_ = S2B.rearrange("p (o n) -> p o n", o=1).to_broadcast([128, 2, 1024])
        t = tt_(H2, Y, ab, ALU.mult, t, *t_a2)
        t_h2 = tt_(H2, H2, sb_, ALU.add, t)
        H2T = T2k.rearrange("p t n -> p (t n)").rearrange("p (k t) -> p k t", k=8)
        t_h2T = to_T(lambda i, k: H2[:, i, k * 128:(k + 1) * 128], H2T, [4, 5, 6, 7], t_h2, [t_h2, *t_a2])
        o_rw = o_qk + 2048
        rw = v1(o_rw, 256).rearrange("p (k n) -> p k n", k=8)
        t_rw = load(rw, I["router_w"][0].rearrange("(k p) n -> p k n", p=128), t_v, tw, t_x1)
        rt = o_rw + 256
        lgt = v1(rt, 64).rearrange("p (t n) -> p t n", t=2)
        top8 = v1(rt + 64, 16).rearrange("p (t n) -> p t n", t=2)
        gt = v1(rt + 80, 64).rearrange("p (t n) -> p t n", t=2)
        eq = v1(rt + 144, 64).rearrange("p (t n) -> p t n", t=2)
        ce = v1(rt + 208, 64).rearrange("p (t n) -> p t n", t=2)
        ngt = v1(rt + 272, 4)
        nmx = v1(rt + 276, 4)
        for i in range(2):
            o = PS[:, 0, i * 32:(i + 1) * 32]
            for k in range(8):
                mm(o, H2T[:, k, i * 128:(i + 1) * 128], rw[:, k, :], k == 0, False, t_rw, *t_h2T, t_x1)
            t = mm(o, CT(C_ONE, 128, 0, 1), rbrow, False, True, t_rb, sig=True)
        t = vcopy(lgt, PS[:, 0, 0:64].rearrange("p (t n) -> p t n", t=2), t)
        o_gate = al(64)
        gate = v1(o_gate, 64).rearrange("p (t n) -> p t n", t=2)
        o_pos = al(64)
        posm = v1(o_pos, 64).rearrange("p (t n) -> p t n", t=2)
        o_cnt = al(32)
        for i in range(2):
            tm = V.op(lambda e, i=i: e.max(top8[:, i, :], lgt[:, i, :]), t)
        for i in range(2):
            v4 = top8[:, i, 3:4]
            tg_ = ts(gt[:, i, :], lgt[:, i, :], v4, None, ALU.is_gt, None, tm)
            te = ts(eq[:, i, :], lgt[:, i, :], v4, None, ALU.is_equal, None, tm)
            tn = red(ngt[:, i:i + 1], gt[:, i, :], ALU.add, tg_)
            tn = ts(ngt[:, i:i + 1], ngt[:, i:i + 1], -1.0, 4.0, ALU.mult, ALU.add, tn)
            tc = V.op(lambda e, i=i: e.tensor_tensor_scan(ce[:, i, :], CT(C_ONE, 32), eq[:, i, :], 0.0,
                                                          ALU.mult, ALU.add), te)
            tc = stt(eq[:, i, :], ce[:, i, :], ngt[:, i:i + 1], eq[:, i, :], ALU.is_le, ALU.mult, tc, tn)
            tc = tt_(gt[:, i, :], gt[:, i, :], eq[:, i, :], ALU.add, tc)
            tx = ts(nmx[:, i:i + 1], top8[:, i, 0:1], -1.0, None, ALU.mult, None, tm)
            tx = act(ce[:, i, :], lgt[:, i, :], ACT.Exp, tx, tc, bias=nmx[:, i:i + 1])
            tx = tt_(ce[:, i, :], ce[:, i, :], gt[:, i, :], ALU.mult, tx)
            tx = red(nmx[:, 2 + i:3 + i], ce[:, i, :], ALU.add, tx)
            tx = recip(nmx[:, 2 + i:3 + i], nmx[:, 2 + i:3 + i], tx)
            t_gate = ts(gate[:, i, :], ce[:, i, :], nmx[:, 2 + i:3 + i], None, ALU.mult, None, tx)
        t_selm = tc
        mm(PS[:, 1, 0:32], CT(C_T1), gt[:, 0, :], True, True, t_selm, t_x1)
        mm(PS[:, 1, 32:64], ones, gt[:, 0, :], True, False)
        t = mm(PS[:, 1, 32:64], CT(C_T1), gt[:, 1, :], False, True, sig=True)
        t_pos = tt_(posm, PS[:, 1, 0:64].rearrange("p (t n) -> p t n", t=2), gt, ALU.mult, t)
        mm(PS[0:1, 2, 0:32], CT(C_ONE, 1), gt[:, 0, :], True, False, t_x1)
        t = mm(PS[0:1, 2, 0:32], CT(C_ONE, 1), gt[:, 1, :], False, True, sig=True)
        cnt = A[0:1, o_cnt:o_cnt + 32].bitcast(I32)
        t_cnt = vcopy(cnt, PS[0:1, 2, 0:32], t)
        for i in range(2):
            t = tr(PS[0:32, 3, i * 128:(i + 1) * 128], gate[:, i, :], ident, t_gate, t_x1, sig=(i == 1))
        gT = v1(rt, 256, 0, 32)
        t_gT = vcopy(gT, PS[0:32, 3, 0:256], t, t_pos, t_gate)

        G2B = v1(o_P + 4096, 1024)
        o_acc = o_P
        ACCv = v1(o_acc, 2048).rearrange("p (t n) -> p t n", t=2)
        B1 = v1(o_P + 2048, 2048, 0, 32)
        B2 = v1(o_P + 5120, 1024, 0, 32)
        t_b1 = load(B1, I["b_mlp1"][0], t_h2)
        t_b2 = load(B2, I["b_mlp2"][0], t_h2)
        tg2 = []
        for hf in range(2):
            t = mod_row(4 + hf, 5, hf, *t_h2T)
            tg2.append(act(G2B[:, hf * 512:(hf + 1) * 512], PS[:, 4 + hf, :], ACT.Copy, t, t_h2))
        for i in range(2):
            for ns in range(2):
                b = 4 + 2 * i + ns
                t = mm(PS[:, b, :], gT[:, i * 128:(i + 1) * 128], B2[:, ns * 512:(ns + 1) * 512], True, True,
                       t_gT, t_b2, *tg2, *t_h2T, sig=True)
                t_acc = vcopy(ACCv[:, i, ns * 512:(ns + 1) * 512], PS[:, b, :], t, t_h2)
        t_moe0 = [t_acc, t_gT, t_pos, t_gate, t_cnt]

        w_ = [o_ws, o_ws + 4608]

        def take(n):
            o = w_[0]
            w_[0] += n
            assert w_[0] <= w_[1]
            return v1(o, n)

        XG = take(512)
        GLU = take(512)
        LIN = take(512)
        LINO = take(512)
        SIG = take(512)
        OB = take(512)
        OBO = take(512)
        AT = take(512)
        SG = take(256)
        ST = take(128)
        w_ = [o_qk, o_qk + 2560]
        XGT = [take(512) for _ in range(3)]
        SGT = [take(256) for _ in range(4)]
        w_ = [o_mr, o_mr + 1536]
        pc = take(128)

        fb = {b: list(t_moe0) for b in range(8)}
        B = {"xg": list(t_moe0), "glu": list(t_moe0), "at": [], "ob": [], "obo": [], "sg": list(t_moe0), "st": []}
        xr = [list(t_moe0), list(t_moe0), list(t_moe0)]
        sr = [list(t_moe0) for _ in range(4)]

        def picks(e, c):
            if c:
                t0 = ts(pc[:, 0:2], posm[:, :, e], -float(CAP * c), None, ALU.add, None, *B["st"], *B["sg"], tg2[1])
                at = lambda i: pc[:, i:i + 1]
            else:
                t0 = t_pos
                at = lambda i: posm[:, i, e:e + 1]
            for i in range(2):
                t1 = ts(ST[:, i * 64:(i + 1) * 64], CT(C_IOTA, 64), at(i), None, ALU.is_equal, None, t0, *B["st"])
            for i in range(2):
                t2 = ts(SG[:, i * 128:(i + 1) * 128], CT(C_IOTA), at(i), gate[:, i, e:e + 1], ALU.is_equal, ALU.mult,
                        t0, *B["sg"])
            return t1, t2

        def gather_rows(t1):
            for i in range(2):
                for g in range(2):
                    t = mm(PS[64 * g:64 * g + 64, 3, :], ST[:, i * 64:(i + 1) * 64], H2[:, i, g * 512:(g + 1) * 512],
                           i == 0, i == 1, t1, *fb[3], sig=(i == 1 and g == 1))
            B["st"] = [t]
            t = act(XG, PS[:, 3, :], ACT.Copy, t, *B["xg"])
            fb[3] = [t]
            return t

        def gather_turn(k, t):
            for q in range(4):
                tq = tr(PS[:, 2, q * 128:(q + 1) * 128], XG[:, q * 128:(q + 1) * 128], ident, t, *fb[2], sig=(q == 3))
            B["xg"] = [tq]
            t = vcopy(XGT[k], PS[:, 2, :], tq, *xr[k])
            fb[2] = [t]
            return t

        def back_turn(k, t2):
            for i in range(2):
                tq = tr(PS[:, 2, i * 128:(i + 1) * 128], SG[:, i * 128:(i + 1) * 128], ident, t2, *fb[2], sig=(i == 1))
            B["sg"] = [tq]
            t = vcopy(SGT[k], PS[:, 2, 0:256], tq, *sr[k])
            fb[2] = [t]
            return t

        def mlp1_bias(e):
            for g in range(2):
                for ns in range(2):
                    f = (2 * g + ns) * 512
                    mm(PS[64 * g:64 * g + 64, ns, :], sel(0, 32, e, 64), B1[:, f:f + 512], True, False,
                       t_b1, *fb[0])

        def mlp1(u1, k, t_x, k8s):
            x4 = XGT[k].rearrange("p (c z) -> p c z", c=4)
            for k8 in k8s:
                u, tk, n = u1[k8]
                kg, kc = k8 // 4, k8 % 4
                for ns in range(2):
                    for g in range(2):
                        f = (2 * g + ns) * 512
                        t = mm(PS[64 * g:64 * g + 64, ns, :], x4[:, kc, 64 * kg:64 * kg + 64], u[:, 0, f:f + 512],
                               False, k8 == 7, tk, t_x, sig=(k8 == 7 and ns == 1 and g == 1))
            if k8 == 7:
                xr[k] = [t]
            return t

        def glu(t, lin, key):
            U = PS[:, 0:2, :].rearrange("p b (n two) -> p b n two", two=2)
            g3 = GLU.rearrange("p (b n) -> p b n", b=2)
            l3 = lin.rearrange("p (b n) -> p b n", b=2)
            tg = ts(g3, U[:, :, :, 0], 7.0, None, ALU.min, None, t, *B["glu"])
            tl = ts(l3, U[:, :, :, 1], 7.0, -7.0, ALU.min, ALU.max, t, *B[key])
            fb[0] = [tl]
            t_s = act(SIG, GLU, ACT.Sigmoid, tg, *B["glu"], scale=1.702)
            tl = stt(lin, lin, 1.0, GLU, ALU.add, ALU.mult, tl)
            t = tt_(lin, lin, SIG, ALU.mult, t_s, tl)
            B["glu"] = [t]
            return t

        def mlp2(u2, t_a, lin, lkey, ob, key):
            for q in range(4):
                t = tr(PS[:, 2, q * 128:(q + 1) * 128], lin[:, q * 128:(q + 1) * 128], ident, t_a, *fb[2], sig=(q == 3))
            B[lkey] = [t]
            t_at = act(AT, PS[:, 2, :], ACT.Copy, t, *B["at"])
            fb[2] = [t_at]
            a4 = AT.rearrange("p (c z) -> p c z", c=4)
            for k8 in range(8):
                u, tk, n = u2[k8 // 2]
                kg, kc = k8 // 4, k8 % 4
                for g in range(2):
                    t = mm(PS[64 * g:64 * g + 64, 3, :], a4[:, kc, 64 * kg:64 * kg + 64],
                           u[:, k8 % 2, g * 512:(g + 1) * 512], k8 == 0, k8 == 7, tk, t_at, *fb[3],
                           sig=(k8 == 7 and g == 1))
            B["at"] = [t]
            t = act(ob, PS[:, 3, :], ACT.Copy, t, *B[key])
            fb[3] = [t]
            return t

        def back(k, ob, key, t_o, t_s):
            for i in range(2):
                for g in range(2):
                    t = mm(PS[:, 4 + 2 * i + g, :], SGT[k][64 * g:64 * g + 64, i * 128:(i + 1) * 128],
                           ob[64 * g:64 * g + 64, :], True, True, t_o, t_s, *fb[4 + 2 * i], sig=(g == 1))
                ta = tt_(ACCv[:, i, :].rearrange("p (g n) -> p g n", g=2), PS[:, 4 + 2 * i:6 + 2 * i, :],
                         ACCv[:, i, :].rearrange("p (g n) -> p g n", g=2), ALU.add, t, t_acc, *acc_last[i])
                acc_last[i] = [ta]
                fb[4 + 2 * i] = [ta]
            B[key] = [t]
            sr[k] = [t]

        acc_last = [[], []]
        B["lin"], B["lino"] = list(t_moe0), list(t_moe0)
        engines = (P, V, S)

        def lot_in(e, c, u1):
            t1, t2 = picks(e, c)
            t_x = gather_turn(2, gather_rows(t1))
            t_s = back_turn(3, t2)
            mlp1_bias(e)
            return glu(mlp1(u1, 2, t_x, range(8)), LINO, "lino"), t_s

        def lot_out(u2, t_a, t_s):
            t_o = mlp2(u2, t_a, LINO, "lino", OBO, "obo")
            back(3, OBO, "obo", t_o, t_s)

        p0 = picks(0, 0)
        t_x = gather_turn(0, gather_rows(p0[0]))
        t_s = back_turn(0, p0[1])
        pending = None
        for e in range(NEXP):
            u1 = [rows_item(I["w_mlp1"][0, e], k * 128, 1, 0, 2048) for k in range(8)]
            u2 = [rows_item(I["w_mlp2"][0, e], k * 256, 2, 0, 1024) for k in range(4)]
            more = e + 1 < NEXP
            if more:
                p1 = picks(e + 1, 0)
            mlp1_bias(e)
            mlp1(u1, e % 2, t_x, range(0, 3))
            if more:
                t_g = gather_rows(p1[0])
            mlp1(u1, e % 2, t_x, range(3, 5))
            if more:
                t_x1 = gather_turn((e + 1) % 2, t_g)
            mlp1(u1, e % 2, t_x, range(5, 7))
            if more:
                t_s1 = back_turn((e + 1) % 3, p1[1])
            t = mlp1(u1, e % 2, t_x, range(7, 8))
            t_a = glu(t, LIN, "lin")
            if pending:
                back(*pending)
            ce_ = cnt[0:1, e:e + 1]
            for q in engines:
                q.begin(ce_, CAP, t_cnt)
                q.begin(ce_, 2 * CAP, t_cnt)
            for c in (2, 3):
                lot_out(u2, *lot_in(e, c, u1))
            for q in engines:
                q.end()
            lot1 = lot_in(e, 1, u1)
            for q in engines:
                q.end()
            release(u1[7][2] + 1)
            t_o = mlp2(u2, t_a, LIN, "lin", OB, "ob")
            for q in engines:
                q.begin(ce_, CAP, t_cnt)
            lot_out(u2, *lot1)
            for q in engines:
                q.end()
            release(u2[3][2] + 1)
            pending = (e % 3, OB, "ob", t_o, t_s)
            if more:
                t_x, t_s = t_x1, t_s1
        back(*pending)
        t_back = acc_last[0] + acc_last[1]

        for i in range(2):
            t = tt_(ACCv[:, i, :], ACCv[:, i, :], G2B, ALU.mult, *t_back, *tg2)
            t_x2 = tt_(X[:, i, :], X[:, i, :], ACCv[:, i, :], ALU.add, t)
        free = {b: [*t_back, t_x2, P.last(), V.last(), S.last()] for b in range(8)}

        top[0] = base
        o_n = al(2048)
        XN = v1(o_n, 2048).rearrange("p (t n) -> p t n", t=2)
        o_n2 = al(2048)
        XS = v1(o_n2, 2048).rearrange("p (t n) -> p t n", t=2)
        o_h = al(2048)
        HT = v1(o_h, 2048).rearrange("p (k t) -> p k t", k=8)
        o_f = al(4224)
        av = v1(o_f, 1024).rearrange("p (t n) -> p t n", t=2)
        UP = 15 + 256 + 15
        uT = v1(o_f + 1024, 4 * UP).rearrange("p (c n) -> p c n", c=4)
        SGm = v1(o_f + 2176, 1024).rearrange("p (c n) -> p c n", c=4)
        CV = v1(o_f + 3200, 1024).rearrange("p (c n) -> p c n", c=4)
        o_y = al(2048)
        YT = v1(o_y, 2048).rearrange("p (k t) -> p k t", k=8)
        o_cw2 = al(124 + 16)
        cw2 = v1(o_cw2, 124).rearrange("p (c w) -> p c w", c=4)
        cb2 = v1(o_cw2 + 124, 4)
        lg2 = v1(o_cw2 + 128, 4)
        lb2 = v1(o_cw2 + 132, 4)
        turn["slots"], turn["at"] = list(range(7)), 0
        at_s = at_ring + 7 * UNIT * 4
        FTH = rounded("fth", at_s, NFF * 256).rearrange("p (k t) -> p k t", k=NFF)
        FTL = rounded("ftl", at_s + NFF * 1024, NFF * 256).rearrange("p (k t) -> p k t", k=NFF)
        HTH = rounded("hth", at_s + 2 * NFF * 1024, 2048).rearrange("p (k t) -> p k t", k=8)
        assert 2 * NFF * 1024 + 8192 <= 7 * UNIT * 4
        o_r = -(-(top[0]) // 8) * 8
        assert o_r + 2048 + 4096 <= AW and o_r <= o_cwr
        HTL = rounded("htl", at_arena + 4 * o_r, 2048).rearrange("p (k t) -> p k t", k=8)
        CS = v1(o_r, 512)
        FH = v1(o_r + 512, 256)
        o_r += 2048
        WH, WL = [], []
        for q in range(4):
            at = at_arena + 4 * (o_f + 2048 * q if q < 2 else o_r + 2048 * (q - 2))
            WH.append(rounded(f"wh{q}", at, 1024))
            WL.append(rounded(f"wl{q}", at + 4096, 1024))

        for c in range(4):
            t = tr(PS[:, 7, c * 31:(c + 1) * 31], cwrow[:, c * 128:(c + 1) * 128], CT(C_IE + 128, 31, 0, 31),
                   t_cwr, *free[7], sig=True)
        t_cwa = vcopy(v1(o_cw2, 124), PS[:, 7, 0:124], t, *free[7])
        t = tr(PS[:, 6, 0:12], vrow, CT(C_IE + 160, 12, 32, 44), *t_vr, sig=True)
        t_cw2 = vcopy(v1(o_cw2 + 124, 12), PS[:, 6, 0:12], t, t_cwa)
        free[7] = free[6] = [t_cw2]
        t_up = V.op(lambda e: e.memset(v1(o_f + 1024, 4 * UP), 0.0), *free[0])

        def gk(name):
            return lambda k: gcol[:, k, RID[name]:RID[name] + 1]

        def norm_T(name, t_x, banks=(0, 1, 2, 3)):
            t = rms_rows(XN, XS, t_x, *free[0])
            tt = to_T(lambda i, k: XN[:, i, k * 128:(k + 1) * 128], HT, list(banks), t,
                      [x for b in banks for x in free[b]], scale=gk(name))
            for b in banks:
                free[b] = list(tt)
            return tt

        t_h = norm_T("mix0", t_x2)
        ups = [rows_item(I["w_in_ab_2"][0], kk * 256, 2, 0, 1024) for kk in range(4)]
        for k in range(8):
            u, tk, n = ups[k // 2]
            for i in range(2):
                t = mm(PS[:, 4 + i, :], HT[:, k, i * 128:(i + 1) * 128], u[:, k % 2, 0:512], k == 0, k == 7,
                       tk, *t_h, *free[4 + i], sig=(k == 7))
        ta = [vcopy(av[:, 0, :], PS[:, 4, :], t, *free[4]), act(av[:, 1, :], PS[:, 5, :], ACT.Copy, t, *free[5])]
        for c in range(4):
            for k in range(8):
                u, tk, n = ups[k // 2]
                t = mm(PS[:, c // 2, (c % 2) * 256:(c % 2) * 256 + 256], u[:, k % 2, 512 + c * 128:640 + c * 128],
                       HT[:, k, :], k == 0, k == 7, tk, *free[c // 2], sig=(k == 7))
        t_vT = t
        release(ups[3][2] + 1)
        gps = [rows_item(I["w_in_ab_2"][0], kk * 512, 4, 1024, 512) for kk in range(2)]
        for c in range(4):
            for k in range(8):
                u, tk, n = gps[k // 4]
                t = mm(PS[:, 2 + c // 2, (c % 2) * 256:(c % 2) * 256 + 256], u[:, k % 4, c * 128:(c + 1) * 128],
                       HT[:, k, :], k == 0, k == 7, tk, *free[2 + c // 2], sig=(k == 7))
        release(gps[1][2] + 1)
        t = act(SGm, PS[:, 2:4, :].rearrange("p b (c n) -> p (b c) n", c=2), ACT.Sigmoid, t, *free[0])
        t_u = tt_(uT[:, :, 15:271], PS[:, 0:2, :].rearrange("p b (c n) -> p (b c) n", c=2), SGm, ALU.mult,
                  t, t_vT, t_up)
        for b in range(4):
            free[b] = [t_u]

        dft, t_dft, n_dft = item(I["dft"], lambda u: u[:, 0:1280])
        fm, t_fm, n_fm = item(I["fnet_map_2"][0].rearrange("h d e -> d h e"),
                              lambda u: u[:, 0:512].rearrange("p (h e) -> p h e", h=4))
        t_yf = []
        prevs = list(free[0])
        for h in range(4):
            for i in range(2):
                t = mm(PS[:, 6, :], av[:, i, h * 128:(h + 1) * 128], dft[:, i * 512:(i + 1) * 512], i == 0, i == 1,
                       t_dft, *ta, *free[6], sig=(i == 1))
            t = act(CS, PS[:, 6, :], ACT.Copy, t, *prevs)
            free[6] = [t]
            mm(PS[:, 7, 0:256], dft[:, 1024:1152], CS[:, 0:256], True, False, t, *free[7])
            t = mm(PS[:, 7, 0:256], dft[:, 1152:1280], CS[:, 256:512], False, True, sig=True)
            prevs = [t]
            t = act(FH, PS[:, 7, 0:256], ACT.Copy, t)
            free[7] = [t]
            t = mm(PS[:, 5, 0:256], fm[:, h, :], FH, True, True, t, t_fm, *ta, *free[5], sig=True)
            prevs.append(t)
            t = act(YT[:, h, :], PS[:, 5, 0:256], ACT.Copy, t)
            free[5] = [t]
            t_yf.append(t)
        release(n_fm + 1)

        for c in range(4):
            t = ts(CV[:, c, :], uT[:, c, 0:256], cw2[:, c, 0:1], cb2[:, c:c + 1], ALU.mult, ALU.add, t_u, t_cw2)
        tk4 = [t] * 4
        for w in range(1, 31):
            for c in range(4):
                tk4[c] = stt(CV[:, c, :], uT[:, c, w:w + 256], cw2[:, c, w:w + 1], CV[:, c, :], ALU.mult, ALU.add,
                             tk4[c])
        c2 = CV.rearrange("p (b c) n -> p b (c n)", b=2)
        s2 = SGm.rearrange("p (b c) n -> p b (c n)", b=2)
        t = tk4[3]
        for b in range(2):
            t1 = mm(PS[:, b, :], ones, c2[:, b, :], True, True, t, *free[b], sig=True)
        t = stt(c2, PS[:, 0:2, :], -1.0 / 128, c2, ALU.mult, ALU.add, t1)
        t = act(s2, c2, ACT.Square, t)
        for b in range(2):
            t1 = mm(PS[:, 2 + b, :], ones, s2[:, b, :], True, True, t, *free[2 + b], sig=True)
        t = ts(s2, PS[:, 2:4, :], 1.0 / 128, 1e-5, ALU.mult, ALU.add, t1)
        t = act(s2, s2, ACT.Sqrt, t)
        t = recip(s2, s2, t)
        t = tt_(c2, c2, s2, ALU.mult, t)
        for c in range(4):
            t = ts(CV[:, c, :], CV[:, c, :], lg2[:, c:c + 1], lb2[:, c:c + 1], ALU.mult, ALU.add, t)
        t = act(SGm, CV, ACT.Sigmoid, t)
        t_yc = tt_(YT[:, 4:8, :], CV, SGm, ALU.mult, t, *free[0])
        for b in range(4):
            free[b] = [t_yc]
        t_x3 = out_proj(I["w_out_ab_2"][0], YT, [t_yc, *t_yf], None, [t_yc])
        for b in range(4):
            free[b] = [t_x3]
        t_ffree = [t_x3, t_yc, *t_yf]

        lots = {"n": 0, "used": [None] * 4}

        def split(src, shape, tk, t_free):
            q = lots["n"] % 4
            lots["n"] += 1
            hi, lo = WH[q].rearrange(*shape[0], **shape[1]), WL[q].rearrange(*shape[0], **shape[1])
            w = [lots["used"][q]] if lots["used"][q] else t_free
            t = act(hi, src, ACT.Copy, tk, *w)
            t = tt_(lo, src, hi.bitcast(F32), ALU.subtract, t, tk, *w)
            return hi, lo, t, q

        def used(q):
            lots["used"][q] = P.mark()

        def pieces(plan, ahead=3):
            ready = []
            for n in range(len(plan)):
                while len(ready) < len(plan) and len(ready) <= n + ahead:
                    src, shape, tk, t_free, done = plan[len(ready)]
                    ready.append(split(src(), shape, tk(), t_free))
                    if done is not None:
                        release(done() + 1, ready[-1][2])
                yield ready[n]

        def mm3(o, lh, ll, rh, rl, first, last, *after, sig=False):
            mm(o, lh, rh, first, False, *after)
            mm(o, lh, rl, False, False)
            return mm(o, ll, rh, False, last, sig=sig)

        def ffn(l, t_x, name, t_free):
            t = rms_rows(XN, XS, t_x)
            t_h = []
            for m in range(4):
                b = 4 + m
                for k in (2 * m, 2 * m + 1):
                    for i in range(2):
                        o = (k % 2) * 256 + i * 128
                        t1 = tr(PS[:, b, o:o + 128], XN[:, i, k * 128:(k + 1) * 128], ident, t, *free[b],
                                sig=(k % 2 == 1 and i == 1))
                for k in (2 * m, 2 * m + 1):
                    o = (k % 2) * 256
                    t2 = act(HTH[:, k, :], PS[:, b, o:o + 256], ACT.Copy, t1, *t_free, scale=gk(name)(k))
                for k in (2 * m, 2 * m + 1):
                    o = (k % 2) * 256
                    t3 = stt(HTL[:, k, :], PS[:, b, o:o + 256], gk(name)(k), HTH[:, k, :].bitcast(F32),
                             ALU.mult, ALU.subtract, t2, *t_free)
                free[b] = [t3]
                t_h.append(t3)
            SGF = XS.rearrange("p t n -> p (t n)")
            TA = XN.rearrange("p t n -> p (t n)")
            wg, wu, wd = I["ffn_w_gate_2"][l], I["ffn_w_up_2"][l], I["ffn_w_down_2"][l]
            tf, ta = [], []
            cols = (("p (k n) -> p k n",), {"k": 8})
            flat = (("p n -> p n",), {})
            plan = []

            def add(make, cut, shape):
                box = []

                def unit():
                    if not box:
                        box.append(make())
                    return box[0]
                for m in range(2):
                    plan.append((lambda m=m: cut(unit()[0], m), shape, lambda: unit()[1], t_free,
                                 (lambda: unit()[2]) if m else None))

            for j in range(NFF // 2):
                for w in (wg, wu):
                    add(lambda w=w, j=j: rows_item(w, 0, 8, j * 256, 256),
                        lambda u, m: u[:, :, m * 128:(m + 1) * 128], cols)
            for kk in range(NFF // 2):
                add(lambda kk=kk: rows_item(wd, kk * 256, 2, 0, 1024), lambda u, m: u[:, m, :], flat)
            stream_of = pieces(plan)

            for j in range(NFF // 2):
                bg, bu = [(0, 1), (2, 3)][j % 2]
                for bank in (bg, bu):
                    for m in range(2):
                        hi, lo, t, q = next(stream_of)
                        for k in range(8):
                            t = mm3(PS[:, bank, m * 256:(m + 1) * 256], hi[:, k, :], lo[:, k, :], HTH[:, k, :],
                                    HTL[:, k, :], k == 0, k == 7, t, *t_h, *free[bank], sig=(k == 7))
                        used(q)
                o = (j % 2) * 512
                sg, tmp = SGF[:, o:o + 512], TA[:, o:o + 512]
                w = ta[-2:-1]
                t1 = act(sg, PS[:, bg, :], ACT.Sigmoid, t, *w)
                t1 = tt_(sg, sg, PS[:, bg, :], ALU.mult, t1)
                t1 = tt_(tmp, sg, PS[:, bu, :], ALU.mult, t1, *w)
                free[bg] = free[bu] = [t1]
                hi = FTH[:, 2 * j:2 * j + 2, :].rearrange("p c n -> p (c n)")
                lo = FTL[:, 2 * j:2 * j + 2, :].rearrange("p c n -> p (c n)")
                t2 = act(hi, tmp, ACT.Copy, t1, *t_free)
                t2 = tt_(lo, tmp, hi.bitcast(F32), ALU.subtract, t2, *t_free)
                ta.append(t2)
                tf.append(t2)
            for k in range(NFF):
                hi, lo, t, q = next(stream_of)
                for i in range(2):
                    for ns in range(2):
                        b = 4 + 2 * i + ns
                        t = mm3(PS[:, b, :], FTH[:, k, i * 128:(i + 1) * 128], FTL[:, k, i * 128:(i + 1) * 128],
                                hi[:, ns * 512:(ns + 1) * 512], lo[:, ns * 512:(ns + 1) * 512],
                                k == 0, k == NFF - 1, t, tf[k // 2], *free[b], sig=(k == NFF - 1))
                used(q)
            for i in range(2):
                for ns in range(2):
                    xs = X[:, i, ns * 512:(ns + 1) * 512]
                    t2 = tt_(xs, xs, PS[:, 4 + 2 * i + ns, :], ALU.add, t)
            for b in range(8):
                free[b] = [t2]
            return t2

        t_x4 = ffn(0, t_x3, "ffn0", t_ffree)

        t = rms_rows(XN, XS, t_x4)
        pt, t_pt, n_pt = item(I["pool"], lambda u: u)
        pm, t_pm, n_pm = item(I["pool_map_2"][0].rearrange("g (c p) e -> p (g c) e", p=128),
                              lambda u: u.rearrange("p (g e) -> p g e", g=8))
        tp = []
        for k in range(8):
            g = k // 2
            b = k % 4
            for i in range(2):
                t1 = mm(PS[:, b, 0:256], XN[:, i, k * 128:(k + 1) * 128], pt[:, (g * 2 + i) * 256:(g * 2 + i + 1) * 256],
                        i == 0, i == 1, t, t_pt, *free[b], sig=(i == 1))
            sc_ = gk("mix1")(k)
            if k % 2:
                tk = act(HT[:, k, :], PS[:, b, 0:256], ACT.Copy, t1, scale=sc_)
            else:
                tk = ts(HT[:, k, :], PS[:, b, 0:256], sc_, None, ALU.mult, None, t1)
            free[b] = [tk]
            tp.append(tk)
        SC = XS.rearrange("p t n -> p (t n)")
        tsb = []
        for hf in range(2):
            t = spread(4 + hf, NROW, 0, RID["pool_scale"], A[0:NROW, o_rows + hf * 512:o_rows + hf * 512 + 512], *free[4])
            tsb.append(act(SC[:, hf * 512:(hf + 1) * 512], PS[:, 4 + hf, :], ACT.Copy, t))
        for b in (4, 5):
            free[b] = list(tsb)
        for i in range(2):
            for g in range(4):
                b = 4 + 2 * i + g // 2
                for c in range(2):
                    t = mm(PS[:, b, (g % 2) * 256:(g % 2) * 256 + 256], HT[:, 2 * g + c, i * 128:(i + 1) * 128],
                           pm[:, 2 * g + c, :], c == 0, c == 1, t_pm, *tp, *free[b], *tsb, sig=(c == 1))
        release(n_pm + 1)
        for i in range(2):
            for ns in range(2):
                tmp = SC[:, 1024:1536]
                t1 = tt_(tmp, PS[:, 4 + 2 * i + ns, :], SC[:, ns * 512:(ns + 1) * 512], ALU.mult, t, *tsb, V.last())
                xs = X[:, i, ns * 512:(ns + 1) * 512]
                t_x5 = tt_(xs, xs, tmp, ALU.add, t1)
        for b in range(8):
            free[b] = [t_x5, *tp]
        t_x6 = ffn(1, t_x5, "ffn1", [t_x5])

        t = rms_rows(XN, XS, t_x6)
        for hf in range(2):
            t1 = spread(hf, NROW, 0, RID["final"], A[0:NROW, o_rows + hf * 512:o_rows + hf * 512 + 512], *free[0])
            for i in range(2):
                xs = XN[:, i, hf * 512:(hf + 1) * 512]
                t_out = tt_(xs, xs, PS[:, hf, :], ALU.mult, t1, t)

        s_out = sem("s_out")
        block = ctx.enter_context(nc.Block())

        @block.sync
        def _(e):
            early = [x for x in small if not x[3] or x[3] == (t_z0,)]
            for n, (dst, src, s, before) in enumerate(stream):
                for _ in range(2 if n in (0, 1) else 3):
                    if early:
                        d_, s_, q_, a_ = early.pop(0)
                        for q, v in a_:
                            e.wait_ge(q, v)
                        e.dma_start(d_, s_).then_inc(q_, 16)
                if before is not None:
                    e.wait_ge(*freed[before])
                e.dma_start(dst, src).then_inc(s_slot[s], 16)
            e.wait_ge(*t_out)
            e.dma_start(out.rearrange("a (t p) d -> p (a t) d", p=128), XN).then_inc(s_out, 16)
            e.wait_ge(s_out, 16)

        @block.gpsimd
        def _(e):
            for dst, src, s, after in small:
                if not after or after == (t_z0,):
                    continue
                for q, v in after:
                    e.wait_ge(q, v)
                e.dma_start(dst, src).then_inc(s, 16)

        @block.scalar
        def _(e):
            S.play(e)

        @block.vector
        def _(e):
            V.play(e)

        @block.tensor
        def _(e):
            P.play(e)


_INS = ["x", "c", "norm1_g", "w_ada", "b_ada", "w_in", "conv_w", "sb_q_g", "sb_k_g", "fox_q_g", "fox_k_g", "fox_f_b",
        "out_norm_g", "w_out", "norm2_g", "router_w", "router_b", "w_mlp1", "b_mlp1", "w_mlp2", "b_mlp2",
        "norm_mix_g_2", "norm_ffn_g_2", "w_in_ab_2", "fnet_map_2", "conv_w_2", "conv_b_2", "conv_ln_g_2",
        "conv_ln_b_2", "w_out_ab_2", "pool_map_2", "pool_scale_2", "ffn_w_gate_2", "ffn_w_up_2", "ffn_w_down_2",
        "final_g_2"]


def kernel(**inputs):
    import concourse.bacc as _bacc
    from concourse.bass_utils import run_bass_kernel_spmd as _run

    nc = _bacc.Bacc("TRN2", target_bir_lowering=False, num_devices=1)
    arrays, aps = {}, {}
    for name in _INS:
        a = np.ascontiguousarray(inputs[name])
        arrays[f"in_{name}"] = a
        aps[name] = nc.dram_tensor(f"in_{name}", a.shape, mybir.dt.from_np(a.dtype), kind="ExternalInput").ap()
    for name, a in (("const", constants()), ("dft", dft_tables()), ("pool", pool_tables())):
        arrays[f"in_{name}"] = a
        aps[name] = nc.dram_tensor(f"in_{name}", a.shape, mybir.dt.from_np(a.dtype), kind="ExternalInput").ap()
    out = nc.dram_tensor("out_0", (1, 256, 1024), F32, kind="ExternalOutput").ap()
    build(nc, aps, out)
    r = _run(nc, [arrays], core_ids=[0])
    return r.results[0]["out_0"]
```

```python
from contextlib import ExitStack

import numpy as np

import concourse.bass as bass
from concourse import mybir

F32 = mybir.dt.float32
F32R = mybir.dt.float32r
I32 = mybir.dt.int32
ALU = mybir.AluOpType
ACT = mybir.ActivationFunctionType
AX = mybir.AxisListType.X

NRING = 14
UNIT = 2048
NEXP = 32
CAP = 64
NFF = 22
BIG = 1.0e30

C_IE, C_T1, C_T2, C_MS, C_CM, C_ONE, C_IOTA, C_END = 0, 384, 512, 640, 768, 1152, 1280, 1408

ROWS = ["norm1_g", "norm2_g", "out_norm_g", "mix0", "mix1", "ffn0", "ffn1", "pool_scale", "final"]
RID = {n: i for i, n in enumerate(ROWS)}

CB, CC, CU, SQ, SK, SV, FQ, FK, FV, FL = 0, 256, 512, 768, 1152, 1536, 1920, 2304, 2688, 3072


def constants():
    p = np.arange(128)[:, None]
    c = np.arange(128)[None, :]
    t = np.zeros((128, C_END), np.float32)
    t[:, C_IE:C_IE + 384] = (np.arange(384)[None, :] == p + 128)
    t[:, C_T1:C_T1 + 128] = (p <= c)
    t[:, C_T2:C_T2 + 128] = (p > c)
    t[:, C_MS:C_MS + 128] = (p < c)
    causal = np.where(c <= p, 0.0, -BIG)
    t[:, C_CM:C_CM + 128] = causal
    t[:, C_CM + 256:C_CM + 384] = causal
    t[:, C_ONE:C_ONE + 128] = 1.0
    t[:, C_IOTA:C_IOTA + 128] = c % CAP + 1
    return t


def dft_tables():
    def cs(n, scale):
        k = (np.arange(n)[:, None] * np.arange(n)[None, :]) % n
        a = 2.0 * np.pi * k / n
        return np.cos(a) * scale, np.sin(a) * scale
    c2, s2 = cs(256, 1.0 / 16.0)
    c1, s1 = cs(128, 128.0 ** -0.5)
    out = np.zeros((128, 1280), np.float32)
    for b in range(2):
        out[:, b * 512:b * 512 + 256] = c2[b * 128:(b + 1) * 128]
        out[:, b * 512 + 256:b * 512 + 512] = s2[b * 128:(b + 1) * 128]
    out[:, 1024:1152] = c1
    out[:, 1152:1280] = -s1
    return out


def pool_tables():
    out = np.zeros((128, 2048), np.float32)
    pos = np.arange(256)
    for g, w in enumerate((2, 4, 8, 16)):
        lo = np.clip(pos - w // 2, 0, 256)
        hi = np.clip(pos - w // 2 + w, 0, 256)
        m = np.zeros((256, 256))
        for t in range(256):
            m[lo[t]:hi[t], t] = 1.0 / (hi[t] - lo[t])
        m -= np.eye(256)
        for b in range(2):
            out[:, (g * 2 + b) * 256:(g * 2 + b + 1) * 256] = m[b * 128:(b + 1) * 128]
    return out


class Queue:

    def __init__(self, sem):
        self.sem, self.n, self.items, self.seen, self.open = sem, 0, [], {}, []
        self.loaded, self.depth = [], 0

    def op(self, fn, *after, sig=True):
        waits = []
        for sem, val in after:
            if self.seen.get(id(sem), 0) < val:
                waits.append((sem, val))
                self.seen[id(sem)] = val
        self.items.append(("op", waits, fn, sig))
        if sig:
            self.n += 1
        return (self.sem, self.n)

    def mark(self):
        if self.items[-1][0] == "op" and self.items[-1][2] is not None and not self.items[-1][3]:
            self.items[-1] = self.items[-1][:3] + (True,)
            self.n += 1
        return (self.sem, self.n)

    def last(self):
        return (self.sem, self.n)

    def begin(self, count_ap, limit, ready):
        self.op(None, ready, sig=False)
        self.open.append((self.items, self.n, dict(self.seen), count_ap, limit))
        self.items = []

    def end(self):
        body = self.items
        self.items, n0, self.seen, ap, limit = self.open.pop()
        self.items.append(("if", ap, limit, body, n0, self.n - n0))

    def loads(self, items):
        out = {}
        for it in items:
            if it[0] == "dma":
                out[id(it[3])] = (it[3], out.get(id(it[3]), (None, 0))[1] + 16)
            elif it[0] == "if":
                for key, (s, k) in self.loads(it[3]).items():
                    out[key] = (s, out.get(key, (None, 0))[1] + k)
        return out

    def play(self, eng, items=None):
        for it in self.items if items is None else items:
            if it[0] == "dma":
                eng.dma_start(it[1], it[2]).then_inc(it[3], 16)
            elif it[0] == "op":
                for sem, val in it[1]:
                    eng.wait_ge(sem, val)
                if it[2] is not None:
                    ins = it[2](eng)
                    if it[3]:
                        ins.then_inc(self.sem, 1)
            else:
                _, ap, limit, body, n0, n = it
                v = next((r for key, r in self.loaded if key is ap), None)
                if v is None:
                    v = eng.value_load(ap, min_val=0, max_val=256)
                    self.loaded = [(ap, v)] + (self.loaded[:1] if self.depth == 0 else self.loaded)
                self.depth += 1
                was = self.loaded
                with eng.If(v > limit):
                    self.play(eng, body)
                self.loaded = was
                self.depth -= 1
                with eng.Else():
                    if n:
                        eng.wait_ge(self.sem, n0)
                        eng.sem_inc(self.sem, n)
                    for s, k in self.loads(body).values():
                        eng.sem_inc(s, k)


def build(nc, I, out):
    with ExitStack() as ctx:
        def sem(name):
            return ctx.enter_context(nc.semaphore(name))

        AW = 24536
        at_ring = -(-nc.sbuf_base // 32) * 32
        ring = ctx.enter_context(nc.sbuf_tensor("ring", [128, NRING * UNIT], F32))
        A = ctx.enter_context(nc.sbuf_tensor("arena", [128, AW], F32))
        at_arena = at_ring + NRING * UNIT * 4

        def rounded(name, at, n):
            return nc.alloc_sbuf_tensor_at(name, [128, n], F32R, offset=at)[:, :]
        PS = ctx.enter_context(nc.psum_tensor("ps", [128, 8, 512], F32))

        P = Queue(sem("s_pe"))
        V = Queue(sem("s_dve"))
        S = Queue(sem("s_act"))

        top = [0]

        def al(n):
            o = top[0]
            top[0] += n
            assert top[0] <= AW, top[0]
            return o

        def v1(o, n, p0=0, p1=128):
            return A[p0:p1, o:o + n]

        def mm(o, l, r, start, stop, *after, sig=False, skip=False):
            return P.op(lambda e: e.matmul(o, l, r, start=start, stop=stop, skip_group_check=skip), *after, sig=sig)

        def tr(o, i, n, *after, sig=False):
            return P.op(lambda e: e.transpose(o, i, n), *after, sig=sig)

        def ts(o, i, s1, s2, op0, op1, *after):
            if op1 is None:
                return V.op(lambda e: e.tensor_scalar(o, i, s1, None, op0), *after)
            return V.op(lambda e: e.tensor_scalar(o, i, s1, s2, op0, op1), *after)

        def tt_(o, a, b, op, *after):
            return V.op(lambda e: e.tensor_tensor(o, a, b, op), *after)

        def stt(o, a, s, b, op0, op1, *after):
            return V.op(lambda e: e.scalar_tensor_tensor(out=o, in0=a, scalar=s, in1=b, op0=op0, op1=op1), *after)

        def vcopy(o, i, *after):
            return V.op(lambda e: e.tensor_copy(o, i), *after)

        def red(o, i, op, *after):
            return V.op(lambda e: e.tensor_reduce(o, i, AX, op), *after)

        def recip(o, i, *after):
            return V.op(lambda e: e.reciprocal(o, i), *after)

        def act(o, i, f, *after, **kw):
            return S.op(lambda e: e.activation(o, i, f, **kw), *after)

        s_slot = [sem(f"s_slot{i}") for i in range(NRING)]
        stream = []
        freed = {}
        held = {}
        turn = {"slots": list(range(7)), "at": 0}
        guard = {}

        def item(src, view):
            n = len(stream)
            s = turn["slots"][turn["at"] % len(turn["slots"])]
            turn["at"] += 1
            before = held.setdefault(s, [])
            stream.append((view(ring[:, s * UNIT:(s + 1) * UNIT]), src, s, before[-1] if before else None,
                           guard.pop(s, None)))
            before.append(n)
            return view(ring[:, s * UNIT:(s + 1) * UNIT]), (s_slot[s], 16 * len(before)), n

        def release(n, t=None):
            t = t or P.mark()
            for k in range(n):
                freed.setdefault(k, t)

        def release_these(units, t):
            for u in units:
                freed[u[2]] = t

        def rows_item(w, r0, nk, c0, ncol):
            src = w[r0:r0 + 128 * nk, c0:c0 + ncol].rearrange("(c p) n -> p c n", p=128)
            return item(src, lambda u: u[:, 0:nk * ncol].rearrange("p (c n) -> p c n", c=nk))

        lots = {"n": 0, "used": [None] * 4, "bufs": []}

        def split(src, shape, tk, t_free):
            q = lots["n"] % len(lots["bufs"])
            lots["n"] += 1
            hi, lo = (w.rearrange(*shape[0], **shape[1]) for w in lots["bufs"][q])
            w = [*([lots["used"][q]] if lots["used"][q] else []), *t_free]
            t = act(hi, src, ACT.Copy, tk, *w)
            t = tt_(lo, src, hi.bitcast(F32), ALU.subtract, t, tk, *w)
            return hi, lo, t, q

        def used(q):
            lots["used"][q] = P.mark()

        def mm3(o, lh, ll, rh, rl, first, last, *after, sig=False):
            mm(o, lh, rh, first, False, *after)
            mm(o, lh, rl, False, False)
            return mm(o, ll, rh, False, last, sig=sig)

        def pieces(plan, ahead=3, first=2):
            ready = []

            def upto(n):
                while len(ready) < min(n, len(plan)):
                    src, shape, tk, t_free, done = plan[len(ready)]
                    ready.append(split(src(), shape, tk(), t_free))
                    if done is not None:
                        release(done() + 1, ready[-1][2])

            def rest():
                for n in range(len(plan)):
                    upto(n + ahead + 1)
                    yield ready[n]
            upto(first)
            return rest()

        def add_units(plan, make, cut, shape, t_free):
            box = []

            def unit():
                if not box:
                    box.append(make())
                return box[0]
            for m in range(2):
                plan.append((lambda m=m: cut(unit()[0], m), shape, lambda: unit()[1], t_free,
                             (lambda: unit()[2]) if m else None))

        COLS = (("p (k n) -> p k n",), {"k": 8})
        FLAT = (("p n -> p n",), {})

        small = []

        def load(dst, src, *after):
            s = sem(f"s_l{len(small)}")
            small.append((dst, src, s, after))
            return (s, 16)

        o_c = al(C_END)
        CT = lambda a, n=128, p0=0, p1=128: v1(o_c + a, n, p0, p1)
        ident = CT(C_IE + 128)
        ones = CT(C_ONE)

        def sel(p0, k, r, m):
            return A[p0:p0 + k, o_c + C_IE + 128 + p0 + r:o_c + C_IE + 129 + p0 + r].to_broadcast([k, m])

        def shifted(s, prev):
            a = C_IE + (256 if prev else 128) - s
            return CT(a)

        o_x = al(2048)
        X = v1(o_x, 2048).rearrange("p (t d) -> p t d", t=2)
        o_rows = al(1024)
        NROW = len(ROWS)
        rows = v1(o_rows, 1024, 0, NROW)
        o_gc = al(8 * NROW)
        gcol = v1(o_gc, 8 * NROW).rearrange("p (k r) -> p k r", k=8)
        o_sm = al(400)
        sm_top = [o_sm]

        def sm(n, p0=0, p1=128):
            o = sm_top[0]
            sm_top[0] += n
            assert sm_top[0] <= o_sm + 400
            return v1(o, n, p0, p1)

        o_c8 = al(128)
        base = top[0]

        c8 = v1(o_c8, 128, 0, 8)
        t_c = load(c8, I["c"].rearrange("a (k p) -> (a k) p", p=128))
        t_const = load(v1(o_c, C_END), I["const"])
        t_x = load(X, I["x"].rearrange("a (t p) d -> p (a t) d", p=128))
        t_rows = [load(v1(o_rows, 1024, i, i + 1), a) for i, a in enumerate([
            I["norm1_g"][0:1, :], I["norm2_g"][0:1, :], I["out_norm_g"][0:1, :],
            I["norm_mix_g_2"][0:1, :], I["norm_mix_g_2"][1:2, :],
            I["norm_ffn_g_2"][0:1, :], I["norm_ffn_g_2"][1:2, :],
            I["pool_scale_2"][0:1, :], I["final_g_2"].rearrange("(a n) -> a n", a=1)])]

        o_P = al(6144)
        PJ = v1(o_P, 6144).rearrange("p (t n) -> p t n", t=2)
        o_hT = al(2304)
        hT = v1(o_hT, 2048).rearrange("p (k t) -> p k t", k=8)
        o_qk = al(3072)
        QKT = v1(o_qk, 3072).rearrange("p (c t) -> p c t", c=12)
        o_mr = al(1536)
        modr = v1(o_mr, 1536).rearrange("p (b n) -> p b n", b=3)
        o_ws = al(4608)
        WS = [v1(o_ws + 1152 * i, 1152).rearrange("p (h n) -> p h n", h=3) for i in range(4)]
        Y = v1(o_ws, 2048).rearrange("p (t n) -> p t n", t=2)
        T2k = v1(o_ws + 2048, 2048).rearrange("p (t n) -> p t n", t=2)
        o_cT = al(256)
        cTp = v1(o_cT, 256).rearrange("p (k m) -> p k m", k=8)
        o_wf = al(48)
        wf = v1(o_wf, 48).rearrange("p (k n) -> p k n", k=8)
        o_small1 = al(256)
        fbrow = v1(o_small1, 6, 0, 1)
        rbrow = sm(32, 0, 1)
        o_cw = al(256)
        cwr = v1(o_cw, 256, 0, 3)
        gq = [v1(o_small1 + 8 + i, 1) for i in range(4)]

        t_ab = []
        for q in range(4):
            t_ab.append(load(modr[32 * q:32 * q + 1, :, :],
                             I["b_ada"].rearrange("a (b q n) -> a q b n", b=3, q=4)[:, q, :, :],
                             None))
        t_wf = load(wf, I["w_in"][0, :, FL:FL + 6].rearrange("(k p) n -> p k n", p=128))
        t_fb = load(fbrow, I["fox_f_b"])
        t_rb = load(rbrow, I["router_b"])
        t_cw = load(cwr, I["conv_w"][0, :, :])
        t_gq = []
        o_cwr = al(512)
        cwrow = v1(o_cwr, 512, 0, 31)
        vrow = v1(o_c8, 128, 32, 44)
        t_cwr = load(cwrow, I["conv_w_2"][0])
        t_vr = [load(v1(o_c8, 128, 32 + 4 * j, 36 + 4 * j), I[n][0].rearrange("(c p) -> c p", p=128))
                for j, n in enumerate(["conv_b_2", "conv_ln_g_2", "conv_ln_b_2"])]
        for i, n in enumerate(["sb_q_g", "sb_k_g", "fox_q_g", "fox_k_g"]):
            for hf in range(2):
                t_gq.append(load(A[64 * hf:64 * hf + 64, o_small1 + 8 + i:o_small1 + 9 + i],
                                 I[n].rearrange("a d -> d a")))

        t_z0 = V.op(lambda e: e.memset(v1(o_mr, 1536), 0.0))
        t_z1 = V.op(lambda e: e.memset(v1(o_cT, 256), 0.0))
        for i, (d, s, q, a) in enumerate(small):
            if a == (None,):
                small[i] = (d, s, q, (t_z0,))

        sc = sm(128, 0, 8)
        t = act(sc, c8, ACT.Sigmoid, t_c)
        t = tt_(sc, sc, c8, ALU.mult, t)
        t = tr(PS[:, 0, 0:8], sc, CT(C_IE + 128, 8, 0, 8), t, t_const, sig=True)
        t_cT = vcopy(cTp[:, :, 0], PS[:, 0, 0:8], t, t_z1)
        rs = sm(8)

        def rms_rows(dst, sq, *after, by=None):
            ss, rr = [rs[:, i:i + 1] for i in range(2)], [rs[:, 2 + i:3 + i] for i in range(2)]
            t = [act(sq[:, i, :], X[:, i, :], ACT.Square, *(by[i] if by else ()), *after, accum_out=ss[i])
                 for i in range(2)]
            for i in range(2):
                t[i] = ts(rr[i], ss[i], 1.0 / 1024, 1e-6, ALU.mult, ALU.add, t[i])
                t[i] = act(rr[i], rr[i], ACT.Sqrt, t[i])
            for i in range(2):
                t[i] = recip(rr[i], rr[i], t[i])
                if dst is not None:
                    t[i] = ts(dst[:, i, :], X[:, i, :], rr[i], None, ALU.mult, None, t[i])
            return t

        def to_T(src, dst, banks, t_src, t_bank, scale=None, bias=None, t_sb=()):
            toks = []
            for m in range(4):
                b = banks[m % len(banks)]
                for k in (2 * m, 2 * m + 1):
                    for i in range(2):
                        w = [t_src] + t_bank
                        if m >= len(banks):
                            w.append(toks[m - len(banks)])
                        o = (k % 2) * 256 + i * 128
                        t = tr(PS[:, b, o:o + 128], src(i, k), ident, *w, sig=(k % 2 == 1 and i == 1))
                for k in ((2 * m,) if scale is None else (2 * m, 2 * m + 1)):
                    o = (k % 2) * 256
                    if scale is None:
                        po = dst[:, k:k + 2, :]
                        pin = PS[:, b, :].rearrange("p (c n) -> p c n", c=2)
                        tk = act(po, pin, ACT.Copy, t) if m % 2 else vcopy(po, pin, t)
                        continue
                    pin, po = PS[:, b, o:o + 256], dst[:, k, :]
                    if bias is None:
                        s = scale(k)
                        if m % 2:
                            tk = act(po, pin, ACT.Copy, t, *t_sb, scale=s)
                        else:
                            tk = ts(po, pin, s, None, ALU.mult, None, t, *t_sb)
                    else:
                        s, b_ = scale(k), bias(k)
                        if m % 2:
                            tk = act(po, pin, ACT.Identity, t, *t_sb, scale=s, bias=b_)
                        else:
                            tk = ts(po, pin, s, b_, ALU.mult, ALU.add, t, *t_sb)
                toks.append(tk)
            return toks

        xn = Y
        t_xn = rms_rows(xn, T2k, t_x)[1]

        def ada_block(b, bank, t_bank):
            us = [rows_item(I["w_ada"][0], k * 128, 1, b * 2048, 2048) for k in range(8)]

            def step(k):
                u, tk, n = us[k]
                for q in range(4):
                    t = mm(PS[32 * q:32 * q + 32, bank, :], cTp[:, k, :], u[:, 0, q * 512:(q + 1) * 512],
                           k == 0, k == 7, tk, t_cT, *t_bank, sig=(q == 3))
                release(n + 1)
                return t

            def fin(t):
                return tt_(modr[:, b, :], PS[:, bank, :], modr[:, b, :], ALU.add, t, *t_ab)
            return step, fin

        step, fin = ada_block(0, 2, [])
        for k in range(8):
            t_ada = step(k)
        for k in range(8):
            t = tr(PS[:, 1, k * NROW:(k + 1) * NROW], A[0:NROW, o_rows + k * 128:o_rows + (k + 1) * 128],
                   CT(C_IE + 128, NROW, 0, NROW), *t_rows, sig=(k == 7))
        t_gcol = vcopy(gcol.rearrange("p k r -> p (k r)"), PS[:, 1, 0:8 * NROW], t)

        t_m0 = fin(t_ada)
        for cc in range(4):
            t = tr(PS[:, 3, cc * 128:(cc + 1) * 128], modr[:, 0, cc * 128:(cc + 1) * 128], ident, t_m0, sig=(cc == 3))
        mview = PS[:, 3, :].rearrange("p (c q z) -> p q c z", c=4, q=4)
        a1 = sm(8)
        s1 = sm(8)
        t_a1 = stt(a1.rearrange("p (q c) -> p q c", q=2), mview[:, 2:4, :, 0], 1.0,
                   gcol[:, :, RID["norm1_g"]].rearrange("p (q c) -> p q c", q=2), ALU.add, ALU.mult, t, t_gcol)
        t_s1 = vcopy(s1.rearrange("p (q c) -> p q c", q=2), mview[:, 0:2, :, 0], t)
        at_tail = at_ring + 7 * UNIT * 4
        hTH, hTL = (rounded(f"ht{n}", at_tail + 8192 * n, 2048).rearrange("p (k t) -> p k t", k=8) for n in range(2))
        lots["bufs"] = [tuple(rounded(f"wp{q}{n}", at_tail + 8192 * (2 + q) + 4096 * n, 1024) for n in range(2))
                        for q in range(4)]
        plan = []
        for j in range(3):
            for kk in range(4):
                add_units(plan, lambda j=j, kk=kk: rows_item(I["w_in"][0], kk * 256, 2, j * 1024, 1024),
                          lambda u, m: u[:, m, :], FLAT, [])
        in_stream = pieces(plan)
        t_hT = to_T(lambda i, k: xn[:, i, k * 128:(k + 1) * 128], hT, [4, 5, 6, 7], t_xn, [],
                    scale=lambda k: a1[:, k:k + 1], bias=lambda k: s1[:, k:k + 1], t_sb=[t_a1, t_s1])

        free = {b: [t_a1, t_s1, t_cT, t_gcol, *(t_hT if b > 3 else [])] for b in range(8)}

        t_hh = []
        for m in range(4):
            hc = hT[:, 2 * m:2 * m + 2, :]
            t = act(hTH[:, 2 * m:2 * m + 2, :], hc, ACT.Copy, t_hT[m])
            t_hh.append(tt_(hTL[:, 2 * m:2 * m + 2, :], hc, hTH[:, 2 * m:2 * m + 2, :].bitcast(F32), ALU.subtract, t,
                            t_hT[m]))
        ev = {}

        def project(j, bk):
            for k in range(8):
                hi, lo, tk, q = next(in_stream)
                for i in range(2):
                    for ns in range(2):
                        b = bk + 2 * i + ns
                        t = mm3(PS[:, b, :], hTH[:, k, i * 128:(i + 1) * 128], hTL[:, k, i * 128:(i + 1) * 128],
                                hi[:, ns * 512:(ns + 1) * 512], lo[:, ns * 512:(ns + 1) * 512], k == 0, k == 7,
                                tk, t_hh[k // 2], *free[b], sig=(k == 7))
                used(q)
            return t

        def land(j, bk, t):
            ev[j] = []
            for i in range(2):
                for ns in range(2):
                    b = bk + 2 * i + ns
                    d = PJ[:, i, j * 1024 + ns * 512:j * 1024 + (ns + 1) * 512]
                    ev[j].append(act(d, PS[:, b, :], ACT.Copy, t) if ns else vcopy(d, PS[:, b, :], t))
                    free[b] = ev[j][-1:]

        t_g8 = [ts(gq[i], gq[i], 0.125, None, ALU.mult, None, *t_gq) for i in (0, 2)]

        def head_norm(kind, c0, o_sq, *after):
            sqs = v1(o_sq, 1536).rearrange("p (t n) -> p t n", t=2)
            seg = PJ[:, :, c0:c0 + 768]
            t = act(sqs, seg, ACT.Square, *after)
            o_r = o_small1 + 16 + kind * 24
            r = v1(o_r, 24)
            t = red(r, v1(o_sq, 1536).rearrange("p (h d) -> p h d", d=64), ALU.add, t)
            t = ts(r, r, 1.0 / 64, 1e-6, ALU.mult, ALU.add, t)
            t = act(r, r, ACT.Sqrt, t)
            t = recip(r, r, t)
            for i in range(2):
                sg = seg[:, i, :].rearrange("p (h d) -> p h d", d=64)
                ri = v1(o_r + 12 * i, 12).rearrange("p (h o) -> p h o", o=1).to_broadcast([128, 12, 64])
                t2 = tt_(sg, sg, ri, ALU.mult, t)
            return t2

        t_qk = {}

        def head_turn(kind, c0, b0, t_n):
            for m in range(3):
                b = b0 + m
                for c in (2 * m, 2 * m + 1):
                    for i in range(2):
                        o = (c % 2) * 256 + i * 128
                        t = tr(PS[:, b, o:o + 128], PJ[:, i, c0 + c * 128:c0 + (c + 1) * 128], ident, t_n, *free[b],
                               sig=(c % 2 == 1 and i == 1))
                for c in (2 * m, 2 * m + 1):
                    g = gq[2 * kind + (c >= 3)]
                    d, o = QKT[:, kind * 6 + c, :], (c % 2) * 256
                    if m % 2:
                        tk = act(d, PS[:, b, o:o + 256], ACT.Copy, t, *t_g8, *t_gq, t_v, t_vw, scale=g)
                    else:
                        tk = ts(d, PS[:, b, o:o + 256], g, None, ALU.mult, None, t, *t_g8, *t_gq, t_v, t_vw)
                t_qk.setdefault(kind, []).append(tk)
                free[b] = [tk]

        t_p0 = project(0, 0)
        cwb = v1(o_qk, 768)
        for w in range(3):
            t = mm(PS[:, 4 + w // 2, (w % 2) * 256:(w % 2) * 256 + 256], sel(0, 3, w, 128), cwr, True, True, t_cw,
                   *free[4], sig=True)
            if w:
                t_cwb = vcopy(cwb[:, 512 * (w - 1):512 * (w - 1) + 512 // w], PS[:, 3 + w, 0:512 // w], t)
                free[3 + w] = [t_cwb]
        land(0, 0, t_p0)
        vcv = v1(o_ws, 512).rearrange("p (t n) -> p t n", t=2)
        vw = [v1(o_ws + 512 + 512 * i, 512).rearrange("p (t n) -> p t n", t=2) for i in range(3)]
        t_v = tt_(vcv, PJ[:, :, CC:CC + 256], PJ[:, :, CU:CU + 256], ALU.mult, *ev[0], *t_hT)
        for w in range(3):
            cb_ = cwb[:, w * 256:(w + 1) * 256].rearrange("p (o n) -> p o n", o=1).to_broadcast([128, 2, 256])
            t_vw = tt_(vw[w], vcv, cb_, ALU.mult, t_v, t_cwb)
        t = project(1, 4)
        land(1, 4, t)
        t_n0 = head_norm(0, SQ, o_ws + 2304, *ev[0], *ev[1], *t_hT)
        t = project(2, 0)
        turn["slots"], turn["at"] = [(turn["at"] + i) % 7 for i in range(7)] + list(range(7, NRING)), 0
        for n in range(7, NRING):
            guard[n] = P.last()
        for i in range(2):
            for k in range(8):
                mm(PS[:, 4, i * 8:i * 8 + 6], hT[:, k, i * 128:(i + 1) * 128], wf[:, k, :], k == 0, False, t_wf, *free[4])
            t_fl = mm(PS[:, 4, i * 8:i * 8 + 6], CT(C_ONE, 128, 0, 1), fbrow, False, True, t_fb, sig=True)
        land(2, 0, t)
        head_turn(0, SQ, 5, t_n0)
        t_n1 = head_norm(1, FQ, o_ws + 2304, *ev[1], *ev[2], t_n0)

        for i in range(2):
            o = PS[:, 0, i * 256:(i + 1) * 256]
            for w in range(3):
                last = w == 2
                t = mm(o, shifted(2 - w, False), vw[w][:, i, :], w == 0, last and i == 0, t_vw, *free[0])
            if i == 1:
                mm(o, shifted(2, True), vw[0][:, 0, :], False, False)
                t_cv = mm(o, shifted(1, True), vw[1][:, 0, :], False, True, sig=True)

        fz = PS[:, 4, 0:16].rearrange("p (t h) -> p t h", t=2)[:, :, 0:6]
        lf = sm(12).rearrange("p (t h) -> p t h", t=2)
        lg = sm(12).rearrange("p (t h) -> p t h", t=2)
        t = act(lg, fz, ACT.Abs, t_fl)
        t = act(lg, lg, ACT.Exp, t, scale=-1.0)
        t = act(lg, lg, ACT.Ln, t, bias=CT(C_ONE, 1))
        t_lf = stt(lf, fz, 0.0, lg, ALU.min, ALU.subtract, t)
        free[4] = [t_lf]

        ada = [ada_block(1, 4, [t_lf]), ada_block(2, 4, [t_lf])]
        ada_at = {"n": 0}
        t_mod = []

        def ada_more(n):
            for _ in range(n):
                k = ada_at["n"]
                if k == 16:
                    return
                ada_at["n"] += 1
                if k == 8:
                    P.op(None, t_mod[0], sig=False)
                t = ada[k // 8][0](k % 8)
                if k % 8 == 7:
                    t_mod.append(ada[k // 8][1](t))

        cum = sm(12).rearrange("p (t h) -> p t h", t=2)
        o_cumT = al(256)
        cumT = v1(o_cumT, 256, 0, 6)

        def running():
            mm(PS[:, 4, 16:22], CT(C_T1), lf[:, 0, :], True, True, t_lf)
            mm(PS[:, 4, 24:30], ones, lf[:, 0, :], True, False)
            t = mm(PS[:, 4, 24:30], CT(C_T1), lf[:, 1, :], False, True, sig=True)
            t_cum = vcopy(cum, PS[:, 4, 16:32].rearrange("p (t h) -> p t h", t=2)[:, :, 0:6], t)
            for i in range(2):
                t = tr(PS[0:6, 4, i * 128:(i + 1) * 128], cum[:, i, :], ident, t_cum, sig=(i == 1))
            t = ts(cumT, PS[0:6, 4, 0:256], -1.0, None, ALU.mult, None, t)
            P.op(None, t, sig=False)
            return t

        WC = [v1(o_hT + 1152 * i, 1152).rearrange("p (h n) -> p h n", h=3) for i in range(2)]
        MS2 = CT(C_MS).rearrange("p (a b n) -> p a b n", a=1, b=1).to_broadcast([128, 3, 2, 128])
        st = {}

        def diag(x):
            return x.rearrange("p h (b n) -> p h b n", b=3)[:, :, 0:3:2, :]

        def sb_z(g):
            for hh in range(3):
                h = 3 * g + hh
                c, o = h // 2, (h % 2) * 64
                kT, qT = QKT[o:o + 64, 3 + c, :], QKT[o:o + 64, c, :]
                mm(PS[:, 5 + hh, 0:256], kT[:, 0:128], qT, True, True, *free[5 + hh], *t_qk[0])
                t = mm(PS[:, 5 + hh, 256:384], kT[:, 128:256], qT[:, 128:256], True, True, sig=True)
            st["sz", g] = t

        def sb_a(g, L, LB, *after):
            Z = PS[:, 5:8, 0:384]
            t = act(L, Z, ACT.Abs, st["sz", g], *after)
            t = act(L, L, ACT.Exp, t, scale=-1.0)
            t = act(L, L, ACT.Ln, t, bias=CT(C_ONE, 1))
            t = stt(LB, Z, 0.0, L, ALU.min, ALU.subtract, t, *after)
            t = tt_(L, LB, Z, ALU.subtract, t)
            for b in (5, 6, 7):
                free[b] = [t]
            st["sa", g] = tt_(diag(L), diag(L), MS2, ALU.mult, t)

        def sb_r(g, L):
            for hh in range(3):
                b = 5 + hh
                mm(PS[:, b, 0:256], CT(C_T2), L[:, hh, 0:256], True, False, st["sa", g], *free[b])
                mm(PS[:, b, 128:256], ones, L[:, hh, 256:384], False, False)
                t = mm(PS[:, b, 256:384], CT(C_T2), L[:, hh, 256:384], False, True, sig=True)
            st["sr", g] = t

        def sb_b(g, L, LB):
            t = tt_(LB, LB, PS[:, 5:8, 0:384], ALU.add, st["sr", g])
            for b in (5, 6, 7):
                free[b] = [t]
            t = act(L, LB, ACT.Exp, t, st["sr", g])
            st["sb", g] = tt_(diag(L), diag(L), MS2, ALU.mult, t)

        def weigh(g, W, t_w, c_v):
            for hh in range(3):
                h = 3 * g + hh
                vv = [PJ[:, i, c_v + h * 64:c_v + (h + 1) * 64] for i in range(2)]
                oo = [PS[:, 0, i * 256 + hh * 64:i * 256 + (hh + 1) * 64] for i in range(2)]
                mm(oo[0], W[:, hh, 0:128], vv[0], True, True, t_w, *free[0])
                mm(oo[1], W[:, hh, 128:256], vv[0], True, False)
                t = mm(oo[1], W[:, hh, 256:384], vv[1], False, True, sig=True)
            return t

        def sb_o(g, L):
            t = weigh(g, L, st["sb", g], SV)
            t2 = vcopy(PJ[:, :, SQ + 192 * g:SQ + 192 * g + 192],
                       PS[:, 0, :].rearrange("p (t n) -> p t n", t=2)[:, :, 0:192], t)
            free[0] = [t2]
            st["so", g] = t2

        mxs = [v1(o_small1 + 64 + 16 * g, 6) for g in range(2)]
        sms = [v1(o_small1 + 72 + 16 * g, 6) for g in range(2)]

        def fx_z(g):
            for hh in range(3):
                h = 3 * g + hh
                b = 1 + hh
                c, o = h // 2, (h % 2) * 64
                kT, qT = QKT[o:o + 64, 9 + c, :], QKT[o:o + 64, 6 + c, :]
                mm(PS[:, b, 0:128], qT[:, 0:128], kT[:, 0:128], True, False, *free[b], *t_qk[1])
                mm(PS[:, b, 0:128], sel(0, 6, h, 128), cumT[:, 0:128], False, True, t_cumT)
                mm(PS[:, b, 128:384], qT[:, 128:256], kT, True, False)
                t = mm(PS[:, b, 128:384], sel(0, 6, h, 128), cumT[:, 0:256], False, True, sig=True)
            st["fz", g] = t

        def fx_a(g, E, *after):
            mx, sums, t = mxs[g], sms[g], st["fz", g]
            for hh in range(3):
                h = 3 * g + hh
                stt(E[:, hh, 0:128], PS[:, 1 + hh, 0:128], cum[:, 0, h:h + 1], CT(C_CM), ALU.add, ALU.add, t, *after)
                tl = stt(E[:, hh, 128:384], PS[:, 1 + hh, 128:384], cum[:, 1, h:h + 1], CT(C_CM + 128, 256),
                         ALU.add, ALU.add, t)
                free[1 + hh] = [tl]
            red(mx[:, 0:3], E[:, :, 0:128], ALU.max, tl)
            t = red(mx[:, 3:6], E[:, :, 128:384], ALU.max, tl)
            t = ts(mx, mx, -1.0, None, ALU.mult, None, t)
            for hh in range(3):
                act(E[:, hh, 0:128], E[:, hh, 0:128], ACT.Exp, t, bias=mx[:, hh:hh + 1],
                    accum_out=sums[:, hh:hh + 1])
                t2 = act(E[:, hh, 128:384], E[:, hh, 128:384], ACT.Exp, bias=mx[:, 3 + hh:4 + hh],
                         accum_out=sums[:, 3 + hh:4 + hh])
            st["fe", g] = t2
            st["fr", g] = recip(sums, sums, t2)

        def fx_t(g, E):
            for hh in range(3):
                for q in range(3):
                    t = tr(PS[:, 1 + hh, q * 128:(q + 1) * 128], E[:, hh, q * 128:(q + 1) * 128], ident,
                           st["fe", g], *free[1 + hh], sig=(q == 2))
            st["ft", g] = t

        def fx_b(g, ET, *after):
            t = act(ET, PS[:, 1:4, 0:384], ACT.Copy, st["ft", g], *after)
            for b in (1, 2, 3):
                free[b] = [t]
            st["fb", g] = t

        def fx_o(g, ET):
            t = weigh(g, ET, st["fb", g], FV)
            for i in range(2):
                rb = sms[g][:, 3 * i:3 * i + 3].rearrange("p (h o) -> p h o", o=1).to_broadcast([128, 3, 64])
                t2 = tt_(PJ[:, i, FQ + 192 * g:FQ + 192 * g + 192].rearrange("p (h d) -> p h d", d=64),
                         PS[:, 0, i * 256:i * 256 + 192].rearrange("p (h d) -> p h d", d=64), rb, ALU.mult, t,
                         st["fr", g])
            free[0] = [t2]
            st["fo", g] = t2

        sb_z(0)
        head_turn(1, FQ, 1, t_n1)
        t_cumT = running()
        t_yc0 = tt_(PJ[:, :, CB:CB + 256], PS[:, 0, :].rearrange("p (t n) -> p t n", t=2), PJ[:, :, CB:CB + 256],
                    ALU.mult, t_cv)
        free[0] = [t_yc0]
        sb_a(0, WS[0], WS[1], t_cv, t_qk[0][-1])
        fx_z(0)
        fx_a(0, WS[2], t_n1)
        sb_r(0, WS[0])
        sb_b(0, WS[0], WS[1])
        ada_more(3)
        fx_t(0, WS[2])
        fx_b(0, WS[3])
        sb_z(1)
        sb_a(1, WC[0], WC[1], t_fl)
        sb_o(0, WS[0])
        ada_more(2)
        fx_z(1)
        fx_a(1, WS[0], st["so", 0])
        fx_o(0, WS[3])
        sb_r(1, WC[0])
        sb_b(1, WC[0], WC[1])
        ada_more(3)
        fx_t(1, WS[0])
        fx_b(1, WS[1], st["sb", 0])
        ada_more(3)
        sb_o(1, WC[0])
        fx_o(1, WS[1])
        t_y = V.last()
        t_ws = [t_y, st["fb", 1], P.last()]
        t2 = t_y
        for b in range(8):
            free[b] = [*free[b], t_y]
        ada_more(16)

        gr = v1(o_small1 + 80, 32).rearrange("p (t g) -> p t g", t=2)
        segs = [(CB, 4, 0), (SQ, 6, 4), (FQ, 6, 10)]
        for c0, n, g0 in segs:
            t = act(Y[:, :, g0 * 64:(g0 + n) * 64], PJ[:, :, c0:c0 + n * 64], ACT.Square, t_y, *t_ws)
        t = red(gr.rearrange("p t g -> p (t g)"), v1(o_ws, 2048).rearrange("p (g d) -> p g d", d=64), ALU.add, t)
        t = ts(gr, gr, 1.0 / 64, 1e-6, ALU.mult, ALU.add, t)
        t = act(gr, gr, ACT.Sqrt, t)
        t = recip(gr, gr, t)
        for i in range(2):
            for c0, n, g0 in segs:
                rb = gr[:, i, g0:g0 + n].rearrange("p (g o) -> p g o", o=1).to_broadcast([128, n, 64])
                t2 = tt_(Y[:, i, g0 * 64:(g0 + n) * 64].rearrange("p (g d) -> p g d", d=64),
                         PJ[:, i, c0:c0 + n * 64].rearrange("p (g d) -> p g d", d=64), rb, ALU.mult, t)
        def spread(bank, k, p0, r, rhs, *after):
            return mm(PS[:, bank, :], sel(p0, k, r, 128), rhs, True, True, *after, sig=True)

        def mod_row(bank, v, half, *after):
            f = v * 1024 + half * 512
            b, q = f // 2048, (f % 2048) // 512
            return mm(PS[:, bank, :], sel_w(q), modr[:, b, :], True, True, *after, sig=True)

        def sel_w(q):
            return A[:, o_c + C_IE + 128 + 32 * q:o_c + C_IE + 129 + 32 * q].to_broadcast([128, 128])

        t_Y = t2
        G1B = v1(o_P, 1024)
        A2B = v1(o_P + 1024, 1024)
        S2B = v1(o_P + 2048, 1024)
        TMP = v1(o_P + 3072, 1024)
        tg = []
        for hf in range(2):
            t = mod_row(4 + hf, 2, hf, *t_mod, *free[4])
            tg.append(act(G1B[:, hf * 512:(hf + 1) * 512], PS[:, 4 + hf, :], ACT.Copy, t, t2))
        for hf in range(2):
            t = mod_row(6 + hf, 3, hf, *t_mod, *free[6])
            tg.append(act(S2B[:, hf * 512:(hf + 1) * 512], PS[:, 6 + hf, :], ACT.Copy, t))
        yH = rounded("yh", at_arena + 4 * o_hT, 2048).rearrange("p (k t) -> p k t", k=8)
        yL = rounded("yl", at_arena + 4 * (o_ws + 2048), 2048).rearrange("p (k t) -> p k t", k=8)
        lots["n"], lots["used"] = 0, [None] * 2
        lots["bufs"] = [tuple(rounded(f"wo{q}{n}", at_arena + 4 * (at + 1024 * n), 1024) for n in range(2))
                        for q, at in enumerate((o_P + 4096, o_qk))]
        plan = []
        for kk in range(4):
            add_units(plan, lambda kk=kk: rows_item(I["w_out"][0], kk * 256, 2, 0, 1024), lambda u, m: u[:, m, :],
                      FLAT, [t_y, t_Y])
        out_stream = pieces(plan, 1, 1)
        t_yT = []
        for m in range(4):
            for k in (2 * m, 2 * m + 1):
                for i in range(2):
                    o = (k % 2) * 256 + i * 128
                    t = tr(PS[:, m, o:o + 128], Y[:, i, k * 128:(k + 1) * 128], ident, t_y, t_Y, *free[m],
                           sig=(k % 2 == 1 and i == 1))
            for k in (2 * m, 2 * m + 1):
                o, g = (k % 2) * 256, gcol[:, k, RID["out_norm_g"]:RID["out_norm_g"] + 1]
                t1 = act(yH[:, k, :], PS[:, m, o:o + 256], ACT.Copy, t, t_Y, scale=g)
            for k in (2 * m, 2 * m + 1):
                o, g = (k % 2) * 256, gcol[:, k, RID["out_norm_g"]:RID["out_norm_g"] + 1]
                t1 = stt(yL[:, k, :], PS[:, m, o:o + 256], g, yH[:, k, :].bitcast(F32), ALU.mult, ALU.subtract, t1)
            free[m] = [t1]
            t_yT.append(t1)
        def out_proj():
            done = []
            for k in range(8):
                hi, lo, tk, q = next(out_stream)
                for i in range(2):
                    for ns in range(2):
                        t = mm3(PS[:, 2 * i + ns, :], yH[:, k, i * 128:(i + 1) * 128], yL[:, k, i * 128:(i + 1) * 128],
                                hi[:, ns * 512:(ns + 1) * 512], lo[:, ns * 512:(ns + 1) * 512], k == 0, k == 7,
                                tk, t_yT[k // 2], *free[2 * i + ns], sig=(k == 7))
                        if k == 7:
                            done.append(t)
                used(q)
            for i in range(2):
                for ns in range(2):
                    xs = X[:, i, ns * 512:(ns + 1) * 512]
                    pb, t = PS[:, 2 * i + ns, :], done[2 * i + ns]
                    tmp = v1(o_P + 4096 + 1024 * i + 512 * ns, 512)
                    t = tt_(tmp, pb, G1B[:, ns * 512:(ns + 1) * 512], ALU.mult, t, *tg, lots["used"][0])
                    t = tt_(xs, xs, tmp, ALU.add, t)
                by_x1.append([t])
            return t

        by_x1 = []
        tw = t_vw
        t_x1 = out_proj()
        for hf in range(2):
            t = mod_row(4 + hf, 4, hf, *tg)
            tg.append(act(TMP[:, hf * 512:(hf + 1) * 512], PS[:, 4 + hf, :], ACT.Copy, t))
        t_a2 = []
        for hf in range(2):
            t = spread(6 + hf, NROW, 0, RID["norm2_g"], A[0:NROW, o_rows + hf * 512:o_rows + hf * 512 + 512], *tg)
            t_a2.append(stt(A2B[:, hf * 512:(hf + 1) * 512], TMP[:, hf * 512:(hf + 1) * 512], 1.0, PS[:, 6 + hf, :],
                            ALU.add, ALU.mult, t, *tg))

        o_h2 = o_hT
        H2 = v1(o_h2, 2048).rearrange("p (t n) -> p t n", t=2)
        t = rms_rows(None, T2k, t_x1, by=by_x1)
        for i in range(2):
            t1 = stt(H2[:, i, :], X[:, i, :], rs[:, 2 + i:3 + i], A2B, ALU.mult, ALU.mult, t[i], *t_a2)
            t[i] = tt_(H2[:, i, :], H2[:, i, :], S2B, ALU.add, t1)
        t_h2 = t[1]
        H2T = T2k.rearrange("p t n -> p (t n)").rearrange("p (k t) -> p k t", k=8)
        t_h2T = to_T(lambda i, k: H2[:, i, k * 128:(k + 1) * 128], H2T, [4, 5, 6, 7], t_h2, [t_h2, *t_a2])
        o_rw = o_qk + 2048
        rw = v1(o_rw, 256).rearrange("p (k n) -> p k n", k=8)
        t_rw = load(rw, I["router_w"][0].rearrange("(k p) n -> p k n", p=128), t_v, tw, t_x1)
        rt = o_rw + 256
        lgt = v1(rt, 64).rearrange("p (t n) -> p t n", t=2)
        top8 = v1(rt + 64, 16).rearrange("p (t n) -> p t n", t=2)
        gt = v1(rt + 80, 64).rearrange("p (t n) -> p t n", t=2)
        eq = v1(rt + 144, 64).rearrange("p (t n) -> p t n", t=2)
        ce = v1(rt + 208, 64).rearrange("p (t n) -> p t n", t=2)
        ex = v1(rt + 288, 64).rearrange("p (t n) -> p t n", t=2)
        ngt = v1(rt + 272, 4)
        nmx = v1(rt + 276, 4)
        for i in range(2):
            o = PS[:, 0, i * 32:(i + 1) * 32]
            for k in range(8):
                mm(o, H2T[:, k, i * 128:(i + 1) * 128], rw[:, k, :], k == 0, False, t_rw, *t_h2T, t_x1)
            t = mm(o, CT(C_ONE, 128, 0, 1), rbrow, False, True, t_rb, sig=True)
        t = vcopy(lgt, PS[:, 0, 0:64].rearrange("p (t n) -> p t n", t=2), t)
        o_gate = al(64)
        gate = v1(o_gate, 64).rearrange("p (t n) -> p t n", t=2)
        o_pos = al(64)
        posm = v1(o_pos, 64).rearrange("p (t n) -> p t n", t=2)
        o_cnt = al(40)
        for i in range(2):
            tm = V.op(lambda e, i=i: e.max(top8[:, i, :], lgt[:, i, :]), t)
        def chosen(i):
            v4 = top8[:, i, 3:4]
            tx = ts(nmx[:, i:i + 1], top8[:, i, 0:1], -1.0, None, ALU.mult, None, tm)
            tx = act(ex[:, i, :], lgt[:, i, :], ACT.Exp, tx, bias=nmx[:, i:i + 1])
            tg_ = ts(gt[:, i, :], lgt[:, i, :], v4, None, ALU.is_gt, None, tm)
            te = ts(eq[:, i, :], lgt[:, i, :], v4, None, ALU.is_equal, None, tm)
            yield
            tn = red(ngt[:, i:i + 1], gt[:, i, :], ALU.add, tg_)
            tc = V.op(lambda e: e.tensor_tensor_scan(ce[:, i, :], CT(C_ONE, 32), eq[:, i, :], 0.0,
                                                     ALU.mult, ALU.add), te)
            yield
            tn = ts(ngt[:, i:i + 1], ngt[:, i:i + 1], -1.0, 4.0, ALU.mult, ALU.add, tn)
            yield
            tc = stt(eq[:, i, :], ce[:, i, :], ngt[:, i:i + 1], eq[:, i, :], ALU.is_le, ALU.mult, tc, tn)
            yield
            tc = tt_(gt[:, i, :], gt[:, i, :], eq[:, i, :], ALU.add, tc)
            t_sel.append(tc)
            yield
            tx = tt_(ex[:, i, :], ex[:, i, :], gt[:, i, :], ALU.mult, tx, tc)
            yield
            tx = red(nmx[:, 2 + i:3 + i], ex[:, i, :], ALU.add, tx)
            yield
            tx = recip(nmx[:, 2 + i:3 + i], nmx[:, 2 + i:3 + i], tx)
            yield
            t_gates.append(ts(gate[:, i, :], ex[:, i, :], nmx[:, 2 + i:3 + i], None, ALU.mult, None, tx))
            yield

        t_sel, t_gates = [], []
        both = [chosen(0), chosen(1)]
        for _ in range(9):
            for g in both:
                next(g)
        tc, t_gate = t_sel[1], t_gates[1]
        t_selm = tc
        G2B = v1(o_P + 4096, 1024)
        tg2 = []
        for hf in range(2):
            t = mod_row(4 + hf, 5, hf, *t_h2T)
            tg2.append(act(G2B[:, hf * 512:(hf + 1) * 512], PS[:, 4 + hf, :], ACT.Copy, t, t_h2))
        mm(PS[:, 1, 0:32], CT(C_T1), gt[:, 0, :], True, True, t_selm, t_x1)
        mm(PS[:, 1, 32:64], ones, gt[:, 0, :], True, False)
        t = mm(PS[:, 1, 32:64], CT(C_T1), gt[:, 1, :], False, True, sig=True)
        t_pos = tt_(posm, PS[:, 1, 0:64].rearrange("p (t n) -> p t n", t=2), gt, ALU.mult, t)
        mm(PS[0:1, 2, 0:32], CT(C_ONE, 1), gt[:, 0, :], True, False, t_x1)
        t = mm(PS[0:1, 2, 0:32], CT(C_ONE, 1), gt[:, 1, :], False, True, sig=True)
        cnt = A[0:1, o_cnt:o_cnt + 32].bitcast(I32)
        cmax = A[0:1, o_cnt + 32:o_cnt + 33]
        t_cm = red(cmax, PS[0:1, 2, 0:32], ALU.max, t)
        vcopy(cnt, PS[0:1, 2, 0:32], t)
        most = A[0:1, o_cnt + 34:o_cnt + 35].bitcast(I32)
        t_cnt = vcopy(most, cmax, t_cm)
        for i in range(2):
            t = tr(PS[0:32, 3, i * 128:(i + 1) * 128], gate[:, i, :], ident, t_gate, t_x1, sig=(i == 1))
        gT = v1(rt, 256, 0, 32)
        t_gT = vcopy(gT, PS[0:32, 3, 0:256], t, t_pos, t_gate)

        o_acc = o_P
        ACCv = v1(o_acc, 2048).rearrange("p (t n) -> p t n", t=2)
        B1 = v1(o_P + 2048, 2048, 0, 32)
        B2 = v1(o_P + 5120, 1024, 0, 32)
        t_b1 = load(B1, I["b_mlp1"][0], t_h2)
        t_b2 = load(B2, I["b_mlp2"][0], t_h2)
        t_moe0 = [t_gT, t_pos, t_gate, t_cnt, *tg2]

        w_ = [o_ws, o_ws + 4608]

        def take(n):
            o = w_[0]
            w_[0] += n
            assert w_[0] <= w_[1]
            return v1(o, n)

        XG = take(512)
        GLU = take(512)
        SIG = take(512)
        LIN = [take(512), take(512)]
        OB = [take(512), take(512)]
        AT = [take(512), None]
        SG = take(256)
        ST = take(128)
        w_ = [o_qk, o_qk + 4608]
        XGT = [take(512) for _ in range(4)]
        SGT = [take(256) for _ in range(5)]
        pc = take(128)
        AT[1] = take(512)

        fb = {b: list(t_moe0) for b in range(8)}
        B = {k: list(t_moe0) for k in ("xg", "glu", "at0", "at1", "lin0", "lin1", "ob0", "ob1", "sg", "st")}
        xr = [list(t_moe0) for _ in range(4)]
        sr = [list(t_moe0) for _ in range(5)]
        HB = [(0, 1), (4, 5), (6, 7)]
        OBK = [3, 3]

        def hid(e, s):
            return 1 if s else 2 * (e % 2)

        acc_last = [[], []]

        def picks(e, c):
            if c:
                t0 = ts(pc[:, 0:2], posm[:, :, e], -float(CAP * c), None, ALU.add, None, *B["st"], *B["sg"], V.last())
                at = lambda i: pc[:, i:i + 1]
            else:
                t0 = t_pos
                at = lambda i: posm[:, i, e:e + 1]
            for i in range(2):
                t1 = ts(ST[:, i * 64:(i + 1) * 64], CT(C_IOTA, 64), at(i), None, ALU.is_equal, None, t0, *B["st"])
            for i in range(2):
                t2 = ts(SG[:, i * 128:(i + 1) * 128], CT(C_IOTA), at(i), gate[:, i, e:e + 1], ALU.is_equal, ALU.mult,
                        t0, *B["sg"])
            return t1, t2

        def gather_rows(t1):
            for i in range(2):
                for g in range(2):
                    t = mm(PS[64 * g:64 * g + 64, 3, :], ST[:, i * 64:(i + 1) * 64], H2[:, i, g * 512:(g + 1) * 512],
                           i == 0, i == 1, t1, *fb[3], sig=(i == 1 and g == 1))
            B["st"] = [t]
            t = act(XG, PS[:, 3, :], ACT.Copy, t, *B["xg"])
            fb[3] = [t]
            return t

        def gather_turn(k, t):
            for q in range(4):
                tq = tr(PS[:, 2, q * 128:(q + 1) * 128], XG[:, q * 128:(q + 1) * 128], ident, t, *fb[2], sig=(q == 3))
            B["xg"] = [tq]
            t = vcopy(XGT[k], PS[:, 2, :], tq, *xr[k])
            fb[2] = [t]
            return t

        def back_turn(k, t2):
            for i in range(2):
                tq = tr(PS[:, 2, i * 128:(i + 1) * 128], SG[:, i * 128:(i + 1) * 128], ident, t2, *fb[2], sig=(i == 1))
            B["sg"] = [tq]
            t = vcopy(SGT[k], PS[:, 2, 0:256], tq, *sr[k])
            fb[2] = [t]
            return t

        def mlp1_bias(e, s):
            for g in range(2):
                for ns in range(2):
                    f = (2 * g + ns) * 512
                    b = HB[hid(e, s)]
                    mm(PS[64 * g:64 * g + 64, b[ns], :], sel(0, 32, e, 64), B1[:, f:f + 512], True, False,
                       t_b1, *fb[b[0]])

        def mlp1(u1, k, hb, t_x, k8s):
            x4 = XGT[k].rearrange("p (c z) -> p c z", c=4)
            for k8 in k8s:
                u, tk = u1[k8][:2]
                kg, kc = k8 // 4, k8 % 4
                for ns in range(2):
                    for g in range(2):
                        f = (2 * g + ns) * 512
                        t = mm(PS[64 * g:64 * g + 64, HB[hb][ns], :], x4[:, kc, 64 * kg:64 * kg + 64],
                               u[:, 0, f:f + 512], False, k8 == 7, tk, t_x, sig=(k8 == 7 and ns == 1 and g == 1))
            if k8 == 7:
                xr[k] = [t]
            return t

        def glu(t, s, hb):
            lin, key = LIN[s], f"lin{s}"
            b = HB[hb][0]
            U = PS[:, b:b + 2, :].rearrange("p b (n two) -> p b n two", two=2)
            g3 = GLU.rearrange("p (b n) -> p b n", b=2)
            l3 = lin.rearrange("p (b n) -> p b n", b=2)
            tg = ts(g3, U[:, :, :, 0], 7.0, None, ALU.min, None, t, *B["glu"])
            tl = ts(l3, U[:, :, :, 1], 7.0, -7.0, ALU.min, ALU.max, t, *B[key])
            fb[b] = [tl]
            t_s = act(SIG, GLU, ACT.Sigmoid, tg, *B["glu"], scale=1.702)
            tl = stt(lin, lin, 1.0, GLU, ALU.add, ALU.mult, tl)
            t = tt_(lin, lin, SIG, ALU.mult, t_s, tl)
            B["glu"] = [t]
            return t

        def mlp2_turn(s, t_a):
            for q in range(4):
                t = tr(PS[:, 2, q * 128:(q + 1) * 128], LIN[s][:, q * 128:(q + 1) * 128], ident, t_a, *fb[2],
                       sig=(q == 3))
            B[f"lin{s}"] = [t]
            t = act(AT[s], PS[:, 2, :], ACT.Copy, t, *B[f"at{s}"])
            fb[2] = [t]
            return t

        def mlp2(u2, s, t_at, units):
            a4 = AT[s].rearrange("p (c z) -> p c z", c=4)
            for k8 in [2 * n + c for n in units for c in range(2)]:
                u, tk = u2[k8 // 2][:2]
                kg, kc = k8 // 4, k8 % 4
                for g in range(2):
                    t = mm(PS[64 * g:64 * g + 64, OBK[s], :], a4[:, kc, 64 * kg:64 * kg + 64],
                           u[:, k8 % 2, g * 512:(g + 1) * 512], k8 == 0, k8 == 7, tk, t_at, *fb[OBK[s]],
                           sig=(k8 == 7 and g == 1))
            if k8 == 7:
                B[f"at{s}"] = [t]
                t = act(OB[s], PS[:, OBK[s], :], ACT.Copy, t, *B[f"ob{s}"])
                fb[OBK[s]] = [t]
            return t

        def back(i, k, s, t_o, t_s, b):
            for g in range(2):
                t = mm(PS[:, b + g, :], SGT[k][64 * g:64 * g + 64, i * 128:(i + 1) * 128],
                       OB[s][64 * g:64 * g + 64, :], True, True, t_o, t_s, *fb[b], sig=(g == 1))
            av = ACCv[:, i, :].rearrange("p (g n) -> p g n", g=2)
            ta = tt_(av, PS[:, b:b + 2, :], av, ALU.add, t, t_acc, *acc_last[i])
            acc_last[i] = [ta]
            fb[b] = [ta]
            B[f"ob{s}"] = [t]
            sr[k] = [t]

        engines = (P, V, S)

        def begin(ap, limit, who=engines):
            for q in who:
                q.begin(ap, limit, t_cnt)

        def end(who=engines):
            for q in who:
                q.end()

        def cnt_of(e, made={}):
            return made.setdefault(e, cnt[0:1, e:e + 1])

        p0 = picks(0, 0)
        t_x = gather_turn(0, gather_rows(p0[0]))
        t_s = back_turn(0, p0[1])
        begin(cnt_of(0), CAP)
        p0 = picks(0, 1)
        t_xb = gather_turn(2, gather_rows(p0[0]))
        t_sb = back_turn(3, p0[1])
        end()
        for i in range(2):
            for ns in range(2):
                b = 4 + 2 * i + ns
                t = mm(PS[:, b, :], gT[:, i * 128:(i + 1) * 128], B2[:, ns * 512:(ns + 1) * 512], True, True,
                       t_gT, t_b2, *tg2, *t_h2T, sig=True)
                fb[b] = [vcopy(ACCv[:, i, ns * 512:(ns + 1) * 512], PS[:, b, :], t, t_h2)]
        t_acc = fb[7][0]
        fb[4] = fb[6] = [t_acc]

        def w1_pieces(e, ks):
            return [rows_item(I["w_mlp1"][0, e], k * 128, 1, 0, 2048) for k in ks]

        pending = None
        u1 = w1_pieces(0, (0, 1))
        mlp1_bias(0, 0)
        mlp1(u1, 0, hid(0, 0), t_x, (0, 1))

        def second_start(e, u, k, t):
            P.mark()
            begin(cnt_of(e), CAP, (P,))
            mlp1_bias(e, 1)
            mlp1(u, k, 1, t, (0, 1))
            P.mark()
            end((P,))
            release_these(u, P.last())

        second_start(0, u1, 2, t_xb)
        for e in range(NEXP):
            more = e + 1 < NEXP
            here, then = cnt_of(e), cnt_of(e + 1) if more else None
            k0, k1 = e % 2, (e + 1) % 2
            h0, h1 = hid(e, 0), hid(e + 1, 0)
            u1 = u1 + w1_pieces(e, range(2, 8))
            if more:
                v1_ = w1_pieces(e + 1, (0, 1))
                p1 = picks(e + 1, 0)
            u2 = [rows_item(I["w_mlp2"][0, e], k * 256, 2, 0, 1024) for k in range(4)]
            for m in range(2, 8):
                t = mlp1(u1, k0, h0, t_x, (m,))
                if m == 7:
                    t_a = glu(t, 0, h0)
                if more and m == 2:
                    t_g = gather_rows(p1[0])
                if m in (3, 7):
                    mine = (2, 3) if m == 3 else range(4, 8)
                    P.mark()
                    begin(here, CAP, (P,))
                    tb = mlp1(u1, 2 + k0, 1, t_xb, mine)
                    P.mark()
                    end((P,))
                    release_these([u1[n] for n in mine], P.last())
                if more and m == 3:
                    t_x1 = gather_turn(k1, t_g)
                if pending and m in (4, 6):
                    back(m // 2 - 2, *pending, HB[h1][0])
                if more and m == 5:
                    t_s1 = back_turn((e + 1) % 3, p1[1])
                    begin(then, CAP)
                    p1b = picks(e + 1, 1)
                    t_g = gather_rows(p1b[0])
                    t_xb1 = gather_turn(2 + k1, t_g)
                    t_sb1 = back_turn(3 + k1, p1b[1])
                    end()
            begin(here, CAP, (V, S))
            t_ab = glu(tb, 1, 1)
            end((V, S))
            if more:
                mlp1_bias(e + 1, 0)
                mlp1(v1_, k1, h1, t_x1, (0,))
            t_at = mlp2_turn(0, t_a)
            if more:
                mlp1(v1_, k1, h1, t_x1, (1,))
                second_start(e + 1, v1_, 2 + k1, t_xb1)
            t_o = mlp2(u2, 0, t_at, range(4))
            P.mark()
            begin(here, CAP)
            t_ob = mlp2(u2, 1, mlp2_turn(1, t_ab), range(4))
            P.mark()
            for i in range(2):
                back(i, 3 + k0, 1, t_ob, t_sb, HB[h0][0])
            end()
            release_these(u2, P.last())
            pending = (e % 3, 0, t_o, t_s)
            if more:
                u1 = v1_
                t_x, t_s, t_xb, t_sb = t_x1, t_s1, t_xb1, t_sb1
        for i in range(2):
            back(i, *pending, 0)

        Q = Queue(sem("s_sp"))
        s_again = sem("s_again")
        t_main = (P.last(), V.last(), S.last())
        begin(most, 2 * CAP, (*engines, Q))
        Q.op(None, *t_main, sig=False)
        for e in range(NEXP):
            begin(cnt_of(e), 2 * CAP, (*engines, Q))
            again = []
            for k in range(12):
                dst = ring[:, k * UNIT:(k + 1) * UNIT]
                if k < 8:
                    dst = dst.rearrange("p (c n) -> p c n", c=1)
                    src = I["w_mlp1"][0, e][k * 128:(k + 1) * 128, :].rearrange("(c p) n -> p c n", p=128)
                else:
                    dst = dst.rearrange("p (c n) -> p c n", c=2)
                    src = I["w_mlp2"][0, e][(k - 8) * 256:(k - 7) * 256, :].rearrange("(c p) n -> p c n", p=128)
                Q.items.append(("dma", dst, src, s_again))
                again.append((dst, (s_again, 192 * (e + 1))))
            for c in (2, 3):
                p0 = picks(e, c)
                t_x = gather_turn(0, gather_rows(p0[0]))
                t_s = back_turn(0, p0[1])
                mlp1_bias(e, 0)
                t_a = glu(mlp1(again[:8], 0, hid(e, 0), t_x, range(8)), 0, hid(e, 0))
                t_o = mlp2(again[8:], 0, mlp2_turn(0, t_a), range(4))
                for i in range(2):
                    back(i, 0, 0, t_o, t_s, 4)
            Q.op(None, P.last(), sig=False)
            end((*engines, Q))
        end((*engines, Q))
        t_back = acc_last[0] + acc_last[1]

        by_x2 = []
        for i in range(2):
            t = tt_(ACCv[:, i, :], ACCv[:, i, :], G2B, ALU.mult, *acc_last[i], *tg2)
            t_x2 = tt_(X[:, i, :], X[:, i, :], ACCv[:, i, :], ALU.add, t)
            by_x2.append([t_x2])
        free = {b: [*t_back, t_x2, P.last(), V.last(), S.last()] for b in range(8)}

        top[0] = base
        o_n = al(2048)
        XN = v1(o_n, 2048).rearrange("p (t n) -> p t n", t=2)
        o_n2 = al(2048)
        XS = v1(o_n2, 2048).rearrange("p (t n) -> p t n", t=2)
        o_h = al(2048)
        HT = v1(o_h, 2048).rearrange("p (k t) -> p k t", k=8)
        o_f = al(4224)
        av = v1(o_f, 1024).rearrange("p (t n) -> p t n", t=2)
        UP = 15 + 256 + 15
        uT = v1(o_f + 1024, 4 * UP).rearrange("p (c n) -> p c n", c=4)
        SGm = v1(o_f + 2176, 1024).rearrange("p (c n) -> p c n", c=4)
        CV = v1(o_f + 3200, 1024).rearrange("p (c n) -> p c n", c=4)
        o_y = al(2048)
        YT = v1(o_y, 2048).rearrange("p (k t) -> p k t", k=8)
        o_cw2 = al(124 + 16)
        cw2 = v1(o_cw2, 124).rearrange("p (c w) -> p c w", c=4)
        cb2 = v1(o_cw2 + 124, 4)
        lg2 = v1(o_cw2 + 128, 4)
        lb2 = v1(o_cw2 + 132, 4)
        turn["slots"], turn["at"] = list(range(7)), 0
        n_post = len(stream)
        at_s = at_ring + 7 * UNIT * 4
        FTH = rounded("fth", at_s, NFF * 256).rearrange("p (k t) -> p k t", k=NFF)
        FTL = rounded("ftl", at_s + NFF * 1024, NFF * 256).rearrange("p (k t) -> p k t", k=NFF)
        HTH = rounded("hth", at_s + 2 * NFF * 1024, 2048).rearrange("p (k t) -> p k t", k=8)
        assert 2 * NFF * 1024 + 8192 <= 7 * UNIT * 4
        o_r = -(-(top[0]) // 8) * 8
        assert o_r + 2048 + 4096 <= AW and o_r <= o_cwr
        HTL = rounded("htl", at_arena + 4 * o_r, 2048).rearrange("p (k t) -> p k t", k=8)
        o_r += 2048
        WH, WL = [], []
        for q in range(4):
            at = at_arena + 4 * (o_f + 2048 * q if q < 2 else o_r + 2048 * (q - 2))
            WH.append(rounded(f"wh{q}", at, 1024))
            WL.append(rounded(f"wl{q}", at + 4096, 1024))

        for c in range(4):
            t = tr(PS[:, 7, c * 31:(c + 1) * 31], cwrow[:, c * 128:(c + 1) * 128], CT(C_IE + 128, 31, 0, 31),
                   t_cwr, *free[7], sig=True)
        t_cwa = vcopy(v1(o_cw2, 124), PS[:, 7, 0:124], t, *free[7])
        t = tr(PS[:, 6, 0:12], vrow, CT(C_IE + 160, 12, 32, 44), *t_vr, sig=True)
        t_cw2 = vcopy(v1(o_cw2 + 124, 12), PS[:, 6, 0:12], t, t_cwa)
        free[7] = free[6] = [t_cw2]
        t_up = V.op(lambda e: e.memset(v1(o_f + 1024, 4 * UP), 0.0), *free[0])

        def gk(name):
            return lambda k: gcol[:, k, RID[name]:RID[name] + 1]

        def turned_norm(t, name, t_free):
            t_h = []
            turned = []
            for i in range(2):
                for k in range(8):
                    b, o = 4 + k // 2, (k % 2) * 256 + i * 128
                    t1 = tr(PS[:, b, o:o + 128], XN[:, i, k * 128:(k + 1) * 128], ident, t[i], *free[b],
                            sig=(i == 1 and k % 2 == 1))
                    if i == 1 and k % 2:
                        turned.append(t1)
            for m in range(4):
                b, t1 = 4 + m, turned[m]
                for k in (2 * m, 2 * m + 1):
                    o = (k % 2) * 256
                    t2 = act(HTH[:, k, :], PS[:, b, o:o + 256], ACT.Copy, t1, *t_free, scale=gk(name)(k))
                for k in (2 * m, 2 * m + 1):
                    o = (k % 2) * 256
                    t3 = stt(HTL[:, k, :], PS[:, b, o:o + 256], gk(name)(k), HTH[:, k, :].bitcast(F32),
                             ALU.mult, ALU.subtract, t2, *t_free)
                free[b] = [t3]
                t_h.append(t3)
            return t_h

        NPT = 9
        DG = ring[:, 7 * UNIT:7 * UNIT + NPT * 512].rearrange("p (c w n) -> p c w n", c=4, w=NPT)
        at = at_s + 4 * NPT * 512
        assert NPT * 512 + 6144 <= 2 * NFF * 256
        lots["n"], lots["used"] = 0, [None] * 3
        lots["bufs"] = [tuple(rounded(f"wm{q}{n}", at + 8192 * q + 4096 * n, 1024) for n in range(2))
                        for q in range(3)]
        t = rms_rows(XN, XS, *free[0], by=by_x2)
        plan = []
        for c0 in (512, 768, 1024, 1280):
            add_units(plan, lambda c0=c0: rows_item(I["w_in_ab_2"][0], 0, 8, c0, 256),
                      lambda u, m: u[:, :, m * 128:(m + 1) * 128], COLS, free[0])
        for kk in range(2):
            add_units(plan, lambda kk=kk: rows_item(I["w_in_ab_2"][0], kk * 512, 4, 0, 512),
                      lambda u, m: u[:, 2 * m:2 * m + 2, :], (("p (k n) -> p k n",), {"k": 2}), free[0])
        ab_stream = pieces(plan, 2)
        t_h = turned_norm(t, "mix0", free[0])

        def diagonals():
            for c in range(4):
                for w in range(NPT):
                    yield act(DG[:, c, w, :], ident, ACT.Copy, t_cw2, t_x2, *free[0],
                              scale=cw2[:, c, 31 - NPT + w:32 - NPT + w])

        diag_ = diagonals()
        for c in range(8):
            hi, lo, t, q = next(ab_stream)
            for k in range(8):
                t = mm3(PS[:, c // 2, (c % 2) * 256:(c % 2) * 256 + 256], hi[:, k, :], lo[:, k, :], HTH[:, k, :],
                        HTL[:, k, :], k == 0, k == 7, t, t_h[k // 2], *free[c // 2], sig=(k == 7))
            used(q)
            if c == 3:
                t_vT = t
            for _ in range(5):
                t_dg = next(diag_, t_dg if c else None)
        t = act(SGm, PS[:, 2:4, :].rearrange("p b (c n) -> p (b c) n", c=2), ACT.Sigmoid, t, *free[0])
        t_u = tt_(uT[:, :, 15:271], PS[:, 0:2, :].rearrange("p b (c n) -> p (b c) n", c=2), SGm, ALU.mult,
                  t, t_vT, t_up)
        for b in range(4):
            free[b] = [t_u]
        for u in range(4):
            hi, lo, t, q = next(ab_stream)
            for m in range(2):
                k = 2 * u + m
                for i in range(2):
                    t = mm3(PS[:, 4 + i, :], HTH[:, k, i * 128:(i + 1) * 128], HTL[:, k, i * 128:(i + 1) * 128],
                            hi[:, m, :], lo[:, m, :], k == 0, k == 7, t, t_h[k // 2], *free[4 + i], sig=(k == 7))
            used(q)
        ta = [act(av[:, i, :], PS[:, 4 + i, :], ACT.Copy, t, *free[4 + i]) for i in range(2)]

        dft, t_dft, n_dft = item(I["dft"], lambda u: u[:, 0:1280])
        fm, t_fm, n_fm = item(I["fnet_map_2"][0].rearrange("h d e -> d h e"),
                              lambda u: u[:, 0:512].rearrange("p (h e) -> p h e", h=4))
        def pe_taps(c):
            for w in range(NPT):
                at = 31 - NPT + w
                t = mm(PS[:, c // 2, (c % 2) * 256:(c % 2) * 256 + 256], DG[:, c, w, :], uT[:, c, at:at + 256],
                       w == 0, w == NPT - 1, t_dg, t_u, *free[c // 2], sig=(w == NPT - 1))
            return t

        def taps(h):
            pair = [None, None]
            for w in range(31 - NPT):
                for m in range(2):
                    c = 2 * h + m
                    if w == 0:
                        pair[m] = ts(CV[:, c, :], uT[:, c, 0:256], cw2[:, c, 0:1], cb2[:, c:c + 1],
                                     ALU.mult, ALU.add, t_u, t_cw2)
                    else:
                        pair[m] = stt(CV[:, c, :], uT[:, c, w:w + 256], cw2[:, c, w:w + 1], CV[:, c, :],
                                      ALU.mult, ALU.add, pair[m])
            c2 = CV[:, 2 * h:2 * h + 2, :].rearrange("p c n -> p (c n)")
            t = tt_(c2, c2, PS[:, h, :], ALU.add, pair[1], t_pt[2 * h + 1])
            free[h] = [t]
            t_cv.append(t)

        def layer_norm(h):
            c2 = CV[:, 2 * h:2 * h + 2, :].rearrange("p c n -> p (c n)")
            s2 = SGm[:, 2 * h:2 * h + 2, :].rearrange("p c n -> p (c n)")
            t = mm(PS[:, 2 + h, :], ones, c2, True, True, t_cv[h], *free[2 + h], sig=True)
            t = stt(c2, PS[:, 2 + h, :], -1.0 / 128, c2, ALU.mult, ALU.add, t)
            t = act(s2, c2, ACT.Square, t)
            yield
            t = mm(PS[:, h, :], ones, s2, True, True, t, *free[h], sig=True)
            t = ts(s2, PS[:, h, :], 1.0 / 128, 1e-5, ALU.mult, ALU.add, t)
            t = act(s2, s2, ACT.Sqrt, t)
            yield
            t = recip(s2, s2, t)
            t = tt_(c2, c2, s2, ALU.mult, t)
            for m in range(2):
                c = 2 * h + m
                t = ts(CV[:, c, :], CV[:, c, :], lg2[:, c:c + 1], lb2[:, c:c + 1], ALU.mult, ALU.add, t)
            t = act(s2, c2, ACT.Sigmoid, t)
            yield
            t_yc.append(tt_(YT[:, 4 + 2 * h:6 + 2 * h, :].rearrange("p c n -> p (c n)"), c2, s2, ALU.mult, t, *free[0]))
            free[h] = [t_yc[-1]]
            yield

        def some(gen, n=1):
            for _ in range(n):
                next(gen, None)

        t_cv, t_yc = [], []
        t_pt = [pe_taps(c) for c in (0, 1)]
        taps(0)
        ln0, ln1 = layer_norm(0), layer_norm(1)
        t_yf, tA, tB, used_cs, used_fh = [], {}, {}, {}, {}
        CSs = [v1(o_r - 2048 + 768 * n, 512) for n in range(2)]
        FHs = [v1(o_r - 2048 + 768 * n + 512, 256) for n in range(2)]

        def over_tokens(h):
            b = 6 + h % 2
            for i in range(2):
                t = mm(PS[:, b, :], av[:, i, h * 128:(h + 1) * 128], dft[:, i * 512:(i + 1) * 512], i == 0, i == 1,
                       t_dft, *ta, *free[b], sig=(i == 1))
            tA[h] = act(CSs[h % 2], PS[:, b, :], ACT.Copy, t, *used_cs.get(h - 2, t_h))
            free[b] = [tA[h]]

        def over_width(h):
            cs = CSs[h % 2]
            mm(PS[:, 4, 0:256], dft[:, 1024:1152], cs[:, 0:256], True, False, tA[h], *ta, *free[4])
            t = mm(PS[:, 4, 0:256], dft[:, 1152:1280], cs[:, 256:512], False, True, sig=True)
            used_cs[h] = [t]
            tB[h] = act(FHs[h % 2], PS[:, 4, 0:256], ACT.Copy, t, *used_fh.get(h - 2, t_h))
            free[4] = [tB[h]]

        def mapped(h):
            t = mm(PS[:, 5, 0:256], fm[:, h, :], FHs[h % 2], True, True, tB[h], t_fm, *ta, *free[5], sig=True)
            used_fh[h] = [t]
            t = act(YT[:, h, :], PS[:, 5, 0:256], ACT.Copy, t)
            free[5] = [t]
            t_yf.append(t)

        over_tokens(0)
        over_tokens(1)
        t_pt.append(pe_taps(2))
        over_width(0)
        t_pt.append(pe_taps(3))
        taps(1)
        over_width(1)
        mapped(0)
        over_tokens(2)
        mapped(1)
        over_tokens(3)
        over_width(2)
        over_width(3)
        mapped(2)
        mapped(3)
        release(n_fm + 1)

        done = []

        def out_ab(kk, *after):
            for c in range(2):
                if c == 0:
                    u, tk, n = rows_item(I["w_out_ab_2"][0], kk * 256, 2, 0, 1024)
                k = 2 * kk + c
                for i in range(2):
                    for ns in range(2):
                        b = 4 + 2 * i + ns
                        t = mm(PS[:, b, :], YT[:, k, i * 128:(i + 1) * 128], u[:, c, ns * 512:(ns + 1) * 512],
                               k == 0, k == 7, tk, *after, *free[b], sig=(k == 7))
                        if k == 7:
                            done.append(t)
                if c:
                    release(n + 1)
                yield

        part = out_ab(0, *t_yf)
        some(part)
        some(ln0)
        some(ln1)
        some(part, 2)
        some(ln0)
        some(ln1)
        some(ln0, 2)
        some(ln1, 2)
        some(out_ab(1, *t_yf), 3)
        for kk in (2, 3):
            some(out_ab(kk, t_yc[kk - 2]), 3)
        by_x3 = []
        for i in range(2):
            for ns in range(2):
                xs = X[:, i, ns * 512:(ns + 1) * 512]
                t_x3 = tt_(xs, xs, PS[:, 4 + 2 * i + ns, :], ALU.add, done[2 * i + ns])
            by_x3.append([t_x3])
        for b in range(4, 8):
            free[b] = [t_x3]
        for b in range(4):
            free[b] = [t_x3]
        t_ffree = [t_x3, *t_yc, *t_yf]

        lots["n"], lots["used"], lots["bufs"] = 0, [None] * 4, list(zip(WH, WL))

        def ffn(l, by, name, t_free):
            t = rms_rows(XN, XS, by=by)
            wg, wu, wd = I["ffn_w_gate_2"][l], I["ffn_w_up_2"][l], I["ffn_w_down_2"][l]
            plan = []
            for j in range(NFF // 2):
                for w in (wg, wu):
                    add_units(plan, lambda w=w, j=j: rows_item(w, 0, 8, j * 256, 256),
                              lambda u, m: u[:, :, m * 128:(m + 1) * 128], COLS, t_free)
            for kk in range(NFF // 2):
                add_units(plan, lambda kk=kk: rows_item(wd, kk * 256, 2, 0, 1024), lambda u, m: u[:, m, :], FLAT,
                          t_free)
            stream_of = pieces(plan)
            t_h = turned_norm(t, name, t_free)
            SGF = XS.rearrange("p t n -> p (t n)")
            TA = XN.rearrange("p t n -> p (t n)")
            tf, ta = [], []
            for j in range(NFF // 2):
                bg, bu = [(0, 1), (2, 3)][j % 2]
                for bank in (bg, bu):
                    for m in range(2):
                        hi, lo, t, q = next(stream_of)
                        for k in range(8):
                            t = mm3(PS[:, bank, m * 256:(m + 1) * 256], hi[:, k, :], lo[:, k, :], HTH[:, k, :],
                                    HTL[:, k, :], k == 0, k == 7, t, t_h[k // 2], *free[bank], sig=(k == 7))
                        used(q)
                o = (j % 2) * 512
                sg, tmp = SGF[:, o:o + 512], TA[:, o:o + 512]
                w = ta[-2:-1]
                t1 = act(sg, PS[:, bg, :], ACT.Sigmoid, t, *w)
                t1 = tt_(sg, sg, PS[:, bg, :], ALU.mult, t1)
                t1 = tt_(tmp, sg, PS[:, bu, :], ALU.mult, t1, *w)
                free[bg] = free[bu] = [t1]
                hi = FTH[:, 2 * j:2 * j + 2, :].rearrange("p c n -> p (c n)")
                lo = FTL[:, 2 * j:2 * j + 2, :].rearrange("p c n -> p (c n)")
                t2 = act(hi, tmp, ACT.Copy, t1, *t_free)
                t2 = tt_(lo, tmp, hi.bitcast(F32), ALU.subtract, t2, *t_free)
                ta.append(t2)
                tf.append(t2)
            done = []
            for k in range(NFF):
                hi, lo, t, q = next(stream_of)
                for i in range(2):
                    for ns in range(2):
                        b = 4 + 2 * i + ns
                        t = mm3(PS[:, b, :], FTH[:, k, i * 128:(i + 1) * 128], FTL[:, k, i * 128:(i + 1) * 128],
                                hi[:, ns * 512:(ns + 1) * 512], lo[:, ns * 512:(ns + 1) * 512],
                                k == 0, k == NFF - 1, t, tf[k // 2], *free[b], sig=(k == NFF - 1))
                        if k == NFF - 1:
                            done.append(t)
                used(q)
            by = []
            for i in range(2):
                for ns in range(2):
                    xs = X[:, i, ns * 512:(ns + 1) * 512]
                    t2 = tt_(xs, xs, PS[:, 4 + 2 * i + ns, :], ALU.add, done[2 * i + ns])
                by.append([t2])
            for b in range(8):
                free[b] = [t2]
            return by

        t_x4 = ffn(0, by_x3, "ffn0", t_ffree)

        t = rms_rows(XN, XS, by=t_x4)[1]
        pt, t_pt, n_pt = item(I["pool"], lambda u: u)
        pm, t_pm, n_pm = item(I["pool_map_2"][0].rearrange("g (c p) e -> p (g c) e", p=128),
                              lambda u: u.rearrange("p (g e) -> p g e", g=8))
        tp = []
        for k in range(8):
            g = k // 2
            b = k % 4
            for i in range(2):
                t1 = mm(PS[:, b, 0:256], XN[:, i, k * 128:(k + 1) * 128], pt[:, (g * 2 + i) * 256:(g * 2 + i + 1) * 256],
                        i == 0, i == 1, t, t_pt, *free[b], sig=(i == 1))
            sc_ = gk("mix1")(k)
            if k % 2:
                tk = act(HT[:, k, :], PS[:, b, 0:256], ACT.Copy, t1, scale=sc_)
            else:
                tk = ts(HT[:, k, :], PS[:, b, 0:256], sc_, None, ALU.mult, None, t1)
            free[b] = [tk]
            tp.append(tk)
        SC = v1(o_f, 2048)
        tsb = []
        for hf in range(2):
            t = spread(4 + hf, NROW, 0, RID["pool_scale"], A[0:NROW, o_rows + hf * 512:o_rows + hf * 512 + 512], *free[4])
            tsb.append(act(SC[:, hf * 512:(hf + 1) * 512], PS[:, 4 + hf, :], ACT.Copy, t, *t_x4[1]))
        for b in (4, 5):
            free[b] = list(tsb)
        mixed = {}
        for i in range(2):
            for g in range(4):
                b = 4 + 2 * i + g // 2
                for c in range(2):
                    t = mm(PS[:, b, (g % 2) * 256:(g % 2) * 256 + 256], HT[:, 2 * g + c, i * 128:(i + 1) * 128],
                           pm[:, 2 * g + c, :], c == 0, c == 1, t_pm, *tp[:2 * g + 2], *free[b], *tsb, sig=(c == 1))
                mixed[b] = t
        release(n_pm + 1)
        by_x5 = []
        for i in range(2):
            for ns in range(2):
                b, tmp = 4 + 2 * i + ns, SC[:, 1024 + 512 * (ns % 2):1536 + 512 * (ns % 2)]
                t1 = tt_(tmp, PS[:, b, :], SC[:, ns * 512:(ns + 1) * 512], ALU.mult, mixed[b], *tsb, V.last())
                xs = X[:, i, ns * 512:(ns + 1) * 512]
                t_x5 = tt_(xs, xs, tmp, ALU.add, t1)
            by_x5.append([t_x5])
        for b in range(8):
            free[b] = [t_x5, *tp]
        t_x6 = ffn(1, by_x5, "ffn1", [t_x5])

        t_g = [spread(hf, NROW, 0, RID["final"], A[0:NROW, o_rows + hf * 512:o_rows + hf * 512 + 512], *free[0])
               for hf in range(2)]
        t = rms_rows(None, XS, by=t_x6)
        t_out = []
        for i in range(2):
            for hf in range(2):
                to = stt(XN[:, i, hf * 512:(hf + 1) * 512], X[:, i, hf * 512:(hf + 1) * 512], rs[:, 2 + i:3 + i],
                         PS[:, hf, :], ALU.mult, ALU.mult, t[i], t_g[hf])
            t_out.append(to)

        s_out = sem("s_out")
        block = ctx.enter_context(nc.Block())

        @block.sync
        def _(e):
            early = [x for x in small if not x[3] or x[3] == (t_z0,)]
            for n, (dst, src, s, before, other) in enumerate(stream):
                if n == n_post:
                    Q.play(e)
                for _ in range(2 if n in (0, 1) else 3):
                    if early:
                        d_, s_, q_, a_ = early.pop(0)
                        for q, v in a_:
                            e.wait_ge(q, v)
                        e.dma_start(d_, s_).then_inc(q_, 16)
                if before is not None:
                    e.wait_ge(*freed[before])
                if other is not None:
                    e.wait_ge(*other)
                e.dma_start(dst, src).then_inc(s_slot[s], 16)
            for i in range(2):
                e.wait_ge(*t_out[i])
                e.dma_start(out[0, 128 * i:128 * i + 128, :], XN[:, i, :]).then_inc(s_out, 16)
            e.wait_ge(s_out, 32)

        @block.gpsimd
        def _(e):
            for dst, src, s, after in small:
                if not after or after == (t_z0,):
                    continue
                for q, v in after:
                    e.wait_ge(q, v)
                e.dma_start(dst, src).then_inc(s, 16)

        @block.scalar
        def _(e):
            S.play(e)

        @block.vector
        def _(e):
            V.play(e)

        @block.tensor
        def _(e):
            P.play(e)


_INS = ["x", "c", "norm1_g", "w_ada", "b_ada", "w_in", "conv_w", "sb_q_g", "sb_k_g", "fox_q_g", "fox_k_g", "fox_f_b",
        "out_norm_g", "w_out", "norm2_g", "router_w", "router_b", "w_mlp1", "b_mlp1", "w_mlp2", "b_mlp2",
        "norm_mix_g_2", "norm_ffn_g_2", "w_in_ab_2", "fnet_map_2", "conv_w_2", "conv_b_2", "conv_ln_g_2",
        "conv_ln_b_2", "w_out_ab_2", "pool_map_2", "pool_scale_2", "ffn_w_gate_2", "ffn_w_up_2", "ffn_w_down_2",
        "final_g_2"]


def kernel(**inputs):
    import concourse.bacc as _bacc
    from concourse.bass_utils import run_bass_kernel_spmd as _run

    nc = _bacc.Bacc("TRN2", target_bir_lowering=False, num_devices=1)
    arrays, aps = {}, {}
    for name in _INS:
        a = np.ascontiguousarray(inputs[name])
        arrays[f"in_{name}"] = a
        aps[name] = nc.dram_tensor(f"in_{name}", a.shape, mybir.dt.from_np(a.dtype), kind="ExternalInput").ap()
    for name, a in (("const", constants()), ("dft", dft_tables()), ("pool", pool_tables())):
        arrays[f"in_{name}"] = a
        aps[name] = nc.dram_tensor(f"in_{name}", a.shape, mybir.dt.from_np(a.dtype), kind="ExternalInput").ap()
    out = nc.dram_tensor("out_0", (1, 256, 1024), F32, kind="ExternalOutput").ap()
    build(nc, aps, out)
    r = _run(nc, [arrays], core_ids=[0])
    return r.results[0]["out_0"]
```
